# Optimizing a Trainium2 kernel written in Bass

```python
import math
import jax, jax.numpy as jnp
from jax import lax
import numpy as np

D_MODEL = 1024
BATCH = 1
SEQ = 256
DEPTH = 2

N_MIXERS = 2
HEAD_DIM = 128
GDN_HEADS = D_MODEL // HEAD_DIM
GDN_CONV = 4
GDN_CHUNK = 64
NSA_Q_HEADS = D_MODEL // HEAD_DIM
NSA_KV_HEADS = NSA_Q_HEADS // 4
CMP_LEN = 32
CMP_STRIDE = 16
SLC_BLOCK = 64
SLC_TOPK = 16
WINDOW = 512
NSA_Q_BLOCK = 64
MEM_TOKENS = 256
MEM_HEADS = 4
NUM_BUCKETS = 32
MAX_DISTANCE = 128
D_FF = ((8 * D_MODEL // 3 + 255) // 256) * 256
FFN_CONV = 3
MEM_WIDTH = MEM_HEADS * HEAD_DIM
MIX_WIDTH = D_MODEL + MEM_WIDTH
GDN_COLS = 4 * GDN_HEADS * HEAD_DIM + 2 * GDN_HEADS
NSA_KV_WIDTH = NSA_KV_HEADS * HEAD_DIM
NSA_COLS = NSA_Q_HEADS * HEAD_DIM + 6 * NSA_KV_WIDTH + 3 * NSA_Q_HEADS
N_GDN = (DEPTH + 1) // 2
N_NSA = DEPTH // 2
EPS = 1e-6


def rms_norm(x, w):
    xf = x.astype(jnp.float32)
    y = xf * lax.rsqrt(jnp.mean(xf * xf, axis=-1, keepdims=True) + EPS)
    return (y * w.astype(jnp.float32)).astype(x.dtype)

def l2norm(x):
    xf = x.astype(jnp.float32)
    return xf * lax.rsqrt(jnp.sum(xf * xf, axis=-1, keepdims=True) + EPS)

def causal_dwconv(x, w):
    K = w.shape[0]
    S = x.shape[1]
    xp = jnp.pad(x, ((0, 0), (K - 1, 0), (0, 0)))
    y = xp[:, 0:S] * w[0]
    for j in range(1, K):
        y = y + xp[:, j:j + S] * w[j]
    return y

def t5_bucket(dist):
    n = jnp.maximum(dist, 0)
    max_exact = NUM_BUCKETS // 2
    logv = jnp.log(jnp.maximum(n, 1).astype(jnp.float32) / max_exact) / math.log(MAX_DISTANCE / max_exact)
    large = max_exact + (logv * (NUM_BUCKETS - max_exact)).astype(jnp.int32)
    large = jnp.minimum(large, NUM_BUCKETS - 1)
    return jnp.where(n < max_exact, n, large)

def masked_softmax(s, mask):
    s = jnp.where(mask, s.astype(jnp.float32), -jnp.inf)
    m = jnp.max(s, axis=-1, keepdims=True)
    m = jnp.where(jnp.isfinite(m), m, 0.0)
    p = jnp.where(mask, jnp.exp(s - m), 0.0)
    return p / jnp.maximum(jnp.sum(p, axis=-1, keepdims=True), 1e-30)

def gated_delta_rule_chunked(q, k, v, g, beta):
    f32 = jnp.float32
    B, H, S, dk = q.shape
    dv = v.shape[-1]
    C = GDN_CHUNK
    N = S // C
    q = (q.astype(f32) * dk ** -0.5).reshape(B, H, N, C, dk)
    k = k.astype(f32).reshape(B, H, N, C, dk)
    v = v.astype(f32).reshape(B, H, N, C, dv)
    beta = beta.astype(f32).reshape(B, H, N, C)
    gc = jnp.cumsum(g.astype(f32).reshape(B, H, N, C), axis=-1)
    incl = jnp.tril(jnp.ones((C, C), bool))
    strict = jnp.tril(jnp.ones((C, C), bool), -1)
    diff = gc[..., :, None] - gc[..., None, :]
    decay = jnp.where(incl, jnp.exp(jnp.where(incl, diff, 0.0)), 0.0)
    kb = k * beta[..., None]
    L = jnp.where(strict, jnp.einsum('bhnid,bhnjd->bhnij', kb, k) * decay, 0.0)
    eye = jnp.eye(C, dtype=f32)
    T = lax.linalg.triangular_solve(eye + L, jnp.broadcast_to(eye, L.shape),
                                    left_side=True, lower=True, unit_diagonal=True)
    u = jnp.einsum('bhnij,bhnjd->bhnid', T, v * beta[..., None])
    w = jnp.einsum('bhnij,bhnjd->bhnid', T, kb * jnp.exp(gc)[..., None])
    a_intra = jnp.where(incl, jnp.einsum('bhnid,bhnjd->bhnij', q, k) * decay, 0.0)
    q_dec = q * jnp.exp(gc)[..., None]
    k_dec = k * jnp.exp(gc[..., -1:] - gc)[..., None]
    g_last = jnp.exp(gc[..., -1])

    def chunk_step(state, xs):
        u_n, w_n, a_n, qd_n, kd_n, gl_n = xs
        v_new = u_n - jnp.einsum('bhcd,bhde->bhce', w_n, state)
        o_n = jnp.einsum('bhcd,bhde->bhce', qd_n, state) + jnp.einsum('bhij,bhje->bhie', a_n, v_new)
        state = state * gl_n[..., None, None] + jnp.einsum('bhcd,bhce->bhde', kd_n, v_new)
        return state, o_n

    to_n = lambda t: jnp.moveaxis(t, 2, 0)
    state0 = jnp.zeros((B, H, dk, dv), f32)
    _, o = lax.scan(chunk_step, state0,
                    (to_n(u), to_n(w), to_n(a_intra), to_n(q_dec), to_n(k_dec), to_n(g_last)))
    return jnp.moveaxis(o, 0, 2).reshape(B, H, S, dv)

def gdn_mixer(cols, conv_w, a_log, dt_bias, norm_w):
    B, S, _ = cols.shape
    H, dh = GDN_HEADS, HEAD_DIM
    wd = H * dh
    qkv = jax.nn.silu(causal_dwconv(cols[..., :3 * wd], conv_w)).reshape(B, S, 3, H, dh)
    q, k, v = qkv[:, :, 0], qkv[:, :, 1], qkv[:, :, 2]
    z = cols[..., 3 * wd:4 * wd].reshape(B, S, H, dh)
    b = cols[..., 4 * wd:4 * wd + H]
    a = cols[..., 4 * wd + H:4 * wd + 2 * H]
    beta = jax.nn.sigmoid(b.astype(jnp.float32))
    g = -jnp.exp(a_log.astype(jnp.float32)) * jax.nn.softplus(a.astype(jnp.float32) + dt_bias.astype(jnp.float32))
    heads = lambda t: jnp.swapaxes(t, 1, 2)
    o = gated_delta_rule_chunked(heads(l2norm(q)), heads(l2norm(k)), heads(v.astype(jnp.float32)),
                                 heads(g), heads(beta))
    o = jnp.swapaxes(o, 1, 2)
    o = rms_norm(o, norm_w) * jax.nn.silu(z.astype(jnp.float32))
    return o.reshape(B, S, wd).astype(cols.dtype)

def compress_blocks(t, pos_emb, w1, w2):
    B, S, G, dh = t.shape
    n_cmp = (S - CMP_LEN) // CMP_STRIDE + 1
    idx = (np.arange(n_cmp, dtype=np.int32)[:, None] * CMP_STRIDE
           + np.arange(CMP_LEN, dtype=np.int32)[None, :])
    blk = t[:, idx] + pos_emb[:, None, :]
    flat = jnp.transpose(blk, (0, 3, 1, 2, 4)).reshape(B, G, n_cmp, CMP_LEN * dh)
    return jax.nn.silu(flat @ w1) @ w2

def nsa_mixer(cols, rel_bias, pos_k, w1_k, w2_k, pos_v, w1_v, w2_v):
    B, S, _ = cols.shape
    HQ, G, dh = NSA_Q_HEADS, NSA_KV_HEADS, HEAD_DIM
    R = HQ // G
    Q = NSA_Q_BLOCK
    scale = dh ** -0.5
    qw = HQ * dh
    q = cols[..., :qw]
    kvs = [cols[..., qw + j * NSA_KV_WIDTH:qw + (j + 1) * NSA_KV_WIDTH].reshape(B, S, G, dh) for j in range(6)]
    k_cmp, v_cmp, k_slc, v_slc, k_win, v_win = kvs
    gates = jax.nn.sigmoid(cols[..., qw + 6 * NSA_KV_WIDTH:].astype(jnp.float32)).reshape(B, S, HQ, 3)

    n_q = S // Q
    n_cmp = (S - CMP_LEN) // CMP_STRIDE + 1
    n_slc = S // SLC_BLOCK
    n_sel = min(SLC_TOPK, n_slc)

    kc = compress_blocks(k_cmp, pos_k, w1_k, w2_k)
    vc = compress_blocks(v_cmp, pos_v, w1_v, w2_v)
    c_start = np.arange(n_cmp, dtype=np.int32) * CMP_STRIDE
    c_end = c_start + CMP_LEN - 1
    s_start = np.arange(n_slc, dtype=np.int32) * SLC_BLOCK
    sel_map = ((c_start[:, None] < s_start[None, :] + SLC_BLOCK)
               & (s_start[None, :] <= c_end[:, None])).astype(np.float32)
    to_blocks = lambda t: jnp.swapaxes(t, 1, 2).reshape(B, G, n_slc, SLC_BLOCK, dh)
    ks, vs = to_blocks(k_slc), to_blocks(v_slc)
    pad = lambda t: jnp.pad(jnp.swapaxes(t, 1, 2), ((0, 0), (0, 0), (WINDOW, 0), (0, 0)))
    kw, vw = pad(k_win), pad(v_win)
    tab = rel_bias.reshape(NUM_BUCKETS, G, R)
    c_end_j = jnp.asarray(c_end)
    bi = jnp.arange(B)[:, None, None, None]
    gi = jnp.arange(G)[None, :, None, None]

    def head_bias(dist):
        return jnp.moveaxis(tab[t5_bucket(dist)], (-2, -1), (0, 1))

    qh = jnp.moveaxis(q.reshape(B, S, G, R, dh).transpose(0, 2, 3, 1, 4).reshape(B, G, R, n_q, Q, dh), 3, 0)
    gh = jnp.moveaxis(gates.reshape(B, S, G, R, 3).transpose(0, 2, 3, 1, 4).reshape(B, G, R, n_q, Q, 3), 3, 0)

    def step(args):
        qi, qb, gb = args
        s0 = qi * Q
        t = s0 + jnp.arange(Q, dtype=jnp.int32)
        dist_c = t[:, None] - c_end_j[None, :]
        sc = jnp.einsum('bgrqd,bgcd->bgrqc', qb, kc).astype(jnp.float32) * scale + head_bias(dist_c)
        p_c = masked_softmax(sc, dist_c >= 0)
        o_c = jnp.einsum('bgrqc,bgcd->bgrqd', p_c, vc.astype(jnp.float32))
        imp = jnp.einsum('bgqc,cs->bgqs', jnp.sum(p_c, axis=2), sel_map)
        jb = jnp.arange(n_slc, dtype=jnp.int32)[None, :]
        tb = (t // SLC_BLOCK)[:, None]
        forced = (jb == 0) | (jb == tb) | (jb == tb - 1)
        score = jnp.where(jb <= tb, jnp.where(forced, jnp.inf, imp), -jnp.inf)
        vals, idx = lax.top_k(score, n_sel)
        ok = vals > -jnp.inf
        kg = ks[bi, gi, idx].reshape(B, G, Q, n_sel * SLC_BLOCK, dh)
        vg = vs[bi, gi, idx].reshape(B, G, Q, n_sel * SLC_BLOCK, dh)
        pos = idx[..., None] * SLC_BLOCK + jnp.arange(SLC_BLOCK, dtype=jnp.int32)
        dist_s = t[:, None, None] - pos
        mask_s = (ok[..., None] & (dist_s >= 0)).reshape(B, G, Q, n_sel * SLC_BLOCK)
        bias_s = jnp.moveaxis(tab[t5_bucket(dist_s).reshape(B, G, Q, n_sel * SLC_BLOCK), gi], -1, 2)
        ss = jnp.einsum('bgrqd,bgqkd->bgrqk', qb, kg).astype(jnp.float32) * scale + bias_s
        p_s = masked_softmax(ss, mask_s[:, :, None])
        o_s = jnp.einsum('bgrqk,bgqkd->bgrqd', p_s, vg.astype(jnp.float32))
        kwb = lax.dynamic_slice_in_dim(kw, s0, Q + WINDOW, axis=2)
        vwb = lax.dynamic_slice_in_dim(vw, s0, Q + WINDOW, axis=2)
        kpos = s0 - WINDOW + jnp.arange(Q + WINDOW, dtype=jnp.int32)
        dist_w = t[:, None] - kpos[None, :]
        mask_w = (dist_w >= 0) & (dist_w < WINDOW) & (kpos[None, :] >= 0)
        sw = jnp.einsum('bgrqd,bgkd->bgrqk', qb, kwb).astype(jnp.float32) * scale + head_bias(dist_w)
        p_w = masked_softmax(sw, mask_w)
        o_w = jnp.einsum('bgrqk,bgkd->bgrqd', p_w, vwb.astype(jnp.float32))
        o = gb[..., 0:1] * o_c + gb[..., 1:2] * o_s + gb[..., 2:3] * o_w
        return o.astype(cols.dtype)

    out = lax.map(step, (jnp.arange(n_q, dtype=jnp.int32), qh, gh))
    return jnp.transpose(out, (1, 0, 4, 2, 3, 5)).reshape(B, S, HQ * dh)

def memory_attention(qm, mem_n, w_kv):
    B, S = qm.shape[:2]
    kv = (mem_n @ w_kv).reshape(B, -1, 2, MEM_HEADS, HEAD_DIM)
    k, v = kv[:, :, 0], kv[:, :, 1]
    s = jnp.einsum('bshd,bmhd->bhsm', qm, k).astype(jnp.float32) * HEAD_DIM ** -0.5
    p = jax.nn.softmax(s, axis=-1)
    o = jnp.einsum('bhsm,bmhd->bshd', p, v.astype(jnp.float32))
    return o.reshape(B, S, MEM_WIDTH).astype(qm.dtype)

def conv_glu(h, w_up, conv_w, conv_b, w_down):
    gate, val = jnp.split(h @ w_up, 2, axis=-1)
    gate = causal_dwconv(gate, conv_w) + conv_b
    return (jax.nn.silu(gate) * val) @ w_down

def first_inputs(seed: int = 0) -> dict:
    key = jax.random.key(seed)
    ks = iter(jax.random.split(key, 32))
    f32 = jnp.float32
    nrm = lambda shape, scale: scale * jax.random.normal(next(ks), shape, f32)
    gain = lambda shape: 1.0 + nrm(shape, 0.02)
    x = nrm((BATCH, SEQ, D_MODEL), 1.0)
    mem = nrm((BATCH, MEM_TOKENS, D_MODEL), 1.0)
    rel_bias = nrm((NUM_BUCKETS, NSA_Q_HEADS), 0.2)
    norm_mix_w = gain((DEPTH, D_MODEL))
    norm_ffn_w = gain((DEPTH, D_MODEL))
    final_norm_w = gain((D_MODEL,))
    mem_norm_w = gain((DEPTH, D_MODEL))
    mem_w_kv = nrm((DEPTH, D_MODEL, 2 * MEM_WIDTH), D_MODEL ** -0.5)
    w_out = nrm((DEPTH, MIX_WIDTH, D_MODEL), MIX_WIDTH ** -0.5)
    gdn_w_in = nrm((N_GDN, D_MODEL, GDN_COLS + MEM_WIDTH), D_MODEL ** -0.5)
    gdn_conv_w = nrm((N_GDN, GDN_CONV, 3 * GDN_HEADS * HEAD_DIM), GDN_CONV ** -0.5)
    gdn_a_log = jnp.log(jax.random.uniform(next(ks), (N_GDN, GDN_HEADS), f32, 1.0, 16.0))
    dt = jnp.exp(jax.random.uniform(next(ks), (N_GDN, GDN_HEADS), f32, math.log(1e-3), math.log(1e-1)))
    gdn_dt_bias = dt + jnp.log(-jnp.expm1(-dt))
    gdn_norm_w = gain((N_GDN, HEAD_DIM))
    nsa_w_in = nrm((N_NSA, D_MODEL, NSA_COLS + MEM_WIDTH), D_MODEL ** -0.5)
    nsa_cmp_pos_k = nrm((N_NSA, CMP_LEN, HEAD_DIM), 0.1)
    nsa_cmp_w1_k = nrm((N_NSA, CMP_LEN * HEAD_DIM, HEAD_DIM), (CMP_LEN * HEAD_DIM) ** -0.5)
    nsa_cmp_w2_k = nrm((N_NSA, HEAD_DIM, HEAD_DIM), HEAD_DIM ** -0.5)
    nsa_cmp_pos_v = nrm((N_NSA, CMP_LEN, HEAD_DIM), 0.1)
    nsa_cmp_w1_v = nrm((N_NSA, CMP_LEN * HEAD_DIM, HEAD_DIM), (CMP_LEN * HEAD_DIM) ** -0.5)
    nsa_cmp_w2_v = nrm((N_NSA, HEAD_DIM, HEAD_DIM), HEAD_DIM ** -0.5)
    ffn_w_up = nrm((DEPTH, D_MODEL, 2 * D_FF), D_MODEL ** -0.5)
    ffn_conv_w = nrm((DEPTH, FFN_CONV, D_FF), FFN_CONV ** -0.5)
    ffn_conv_b = nrm((DEPTH, D_FF), 0.02)
    ffn_w_down = nrm((DEPTH, D_FF, D_MODEL), D_FF ** -0.5)
    return {'x': x, 'mem': mem, 'rel_bias': rel_bias, 'norm_mix_w': norm_mix_w,
            'norm_ffn_w': norm_ffn_w, 'final_norm_w': final_norm_w, 'mem_norm_w': mem_norm_w,
            'mem_w_kv': mem_w_kv, 'w_out': w_out, 'gdn_w_in': gdn_w_in, 'gdn_conv_w': gdn_conv_w,
            'gdn_a_log': gdn_a_log, 'gdn_dt_bias': gdn_dt_bias, 'gdn_norm_w': gdn_norm_w,
            'nsa_w_in': nsa_w_in, 'nsa_cmp_pos_k': nsa_cmp_pos_k, 'nsa_cmp_w1_k': nsa_cmp_w1_k,
            'nsa_cmp_w2_k': nsa_cmp_w2_k, 'nsa_cmp_pos_v': nsa_cmp_pos_v, 'nsa_cmp_w1_v': nsa_cmp_w1_v,
            'nsa_cmp_w2_v': nsa_cmp_w2_v, 'ffn_w_up': ffn_w_up, 'ffn_conv_w': ffn_conv_w,
            'ffn_conv_b': ffn_conv_b, 'ffn_w_down': ffn_w_down}

def first_block(x, mem, rel_bias, norm_mix_w, norm_ffn_w, final_norm_w, mem_norm_w, mem_w_kv, w_out,
              gdn_w_in, gdn_conv_w, gdn_a_log, gdn_dt_bias, gdn_norm_w, nsa_w_in, nsa_cmp_pos_k,
              nsa_cmp_w1_k, nsa_cmp_w2_k, nsa_cmp_pos_v, nsa_cmp_w1_v, nsa_cmp_w2_v, ffn_w_up,
              ffn_conv_w, ffn_conv_b, ffn_w_down):
    B, S, _ = x.shape
    for i in range(DEPTH):
        h = rms_norm(x, norm_mix_w[i])
        mem_n = rms_norm(mem, mem_norm_w[i])
        j = i // N_MIXERS
        if i % N_MIXERS == 0:
            proj = h @ gdn_w_in[j]
            mix = gdn_mixer(proj[..., :GDN_COLS], gdn_conv_w[j], gdn_a_log[j], gdn_dt_bias[j], gdn_norm_w[j])
            qm = proj[..., GDN_COLS:]
        else:
            proj = h @ nsa_w_in[j]
            mix = nsa_mixer(proj[..., :NSA_COLS], rel_bias, nsa_cmp_pos_k[j], nsa_cmp_w1_k[j],
                            nsa_cmp_w2_k[j], nsa_cmp_pos_v[j], nsa_cmp_w1_v[j], nsa_cmp_w2_v[j])
            qm = proj[..., NSA_COLS:]
        mo = memory_attention(qm.reshape(B, S, MEM_HEADS, HEAD_DIM), mem_n, mem_w_kv[i])
        x = x + jnp.concatenate([mix, mo], axis=-1) @ w_out[i]
        x = x + conv_glu(rms_norm(x, norm_ffn_w[i]), ffn_w_up[i], ffn_conv_w[i], ffn_conv_b[i], ffn_w_down[i])
    return rms_norm(x, final_norm_w)


GRID_W = 64
MLSTM_HEADS = 4
MLSTM_HD = 128
MLSTM_W = MLSTM_HEADS * MLSTM_HD
MLSTM_CHUNK = 64
CONV_W = 5
ATTN_HEADS = 8
KV_HEADS = 2
ATTN_HD = 64
ATTN_W = ATTN_HEADS * ATTN_HD
KV_W = KV_HEADS * ATTN_HD
Q_BLOCK = 128
ROPE_BASE = 10000.0
N_GROUPS = 4
EXPERTS_PER_GROUP = 8
N_EXPERTS = N_GROUPS * EXPERTS_PER_GROUP
TOP_K = 2
EXPERT_HIDDEN = 512
NORM_EPS = 1e-6
SPLIT_SIZES = (MLSTM_W, MLSTM_W, MLSTM_W, MLSTM_W, 4 * MLSTM_HEADS, ATTN_W, KV_W, KV_W, D_MODEL, D_MODEL)
IN_W = sum(SPLIT_SIZES)


def rms_norm_2(x, g):
    xf = x.astype(jnp.float32)
    y = xf * lax.rsqrt(jnp.mean(xf * xf, axis=-1, keepdims=True) + NORM_EPS)
    return (y * g.astype(jnp.float32)).astype(x.dtype)

def rope_tables(seq):
    rows = seq // GRID_W
    row = jnp.repeat(jnp.arange(rows, dtype=jnp.float32), GRID_W)
    col = jnp.tile(jnp.arange(GRID_W, dtype=jnp.float32), rows)
    half = ATTN_HD // 2
    inv_freq = ROPE_BASE ** (-jnp.arange(0, half, 2, dtype=jnp.float32) / half)
    ang_r = row[:, None] * inv_freq
    ang_c = col[:, None] * inv_freq
    return (jnp.cos(ang_r), jnp.sin(ang_r), jnp.cos(ang_c), jnp.sin(ang_c))

def rotate(x, cos, sin):
    x1, x2 = jnp.split(x, 2, axis=-1)
    return jnp.concatenate([x1 * cos - x2 * sin, x2 * cos + x1 * sin], axis=-1)

def axial_rope(x, tables):
    cr, sr, cc, sc = [t[:, None, :] for t in tables]
    xr, xc = jnp.split(x, 2, axis=-1)
    return jnp.concatenate([rotate(xr, cr, sr), rotate(xc, cc, sc)], axis=-1)

def bidirectional_gqa(q, k, v, q_g, k_g, tables):
    B, S = q.shape[0], q.shape[1]
    G = ATTN_HEADS // KV_HEADS
    q = axial_rope(rms_norm_2(q, q_g).astype(jnp.float32), tables)
    k = axial_rope(rms_norm_2(k, k_g).astype(jnp.float32), tables)
    nb = S // Q_BLOCK
    qb = q.reshape(B, nb, Q_BLOCK, KV_HEADS, G, ATTN_HD).transpose(1, 0, 3, 4, 2, 5)
    kt = k.transpose(0, 2, 1, 3)
    vt = v.transpose(0, 2, 1, 3)
    scale = ATTN_HD ** -0.5

    def block(q_blk):
        s = jnp.einsum('bkgqd,bksd->bkgqs', q_blk, kt) * scale
        p = jax.nn.softmax(s.astype(jnp.float32), axis=-1)
        return jnp.einsum('bkgqs,bksd->bkgqd', p.astype(vt.dtype), vt)

    o = lax.map(block, qb)
    return o.transpose(1, 0, 4, 2, 3, 5).reshape(B, S, ATTN_W)

def mlstm_one_direction(q, k, v, log_i, log_f):
    B, H, S, dh = q.shape
    L = MLSTM_CHUNK
    nc = S // L
    q = q.reshape(B, H, nc, L, dh)
    k = k.reshape(B, H, nc, L, dh)
    v = v.reshape(B, H, nc, L, dh)
    li = log_i.reshape(B, H, nc, L)
    lf = log_f.reshape(B, H, nc, L)
    b = jnp.cumsum(lf, axis=-1)
    b_last = b[..., -1]
    a = b_last[..., None] - b + li
    a_max = jnp.max(a, axis=-1)
    w = jnp.exp(a - a_max[..., None])
    c_chunk = jnp.einsum('bhcl,bhcld,bhcle->bhcde', w, v, k)
    n_chunk = jnp.einsum('bhcl,bhcle->bhce', w, k)

    def step(carry, inp):
        c_st, n_st, m_st = carry
        c_in, n_in, bl, am = inp
        m_new = jnp.maximum(bl + m_st, am)
        decay = jnp.exp(bl + m_st - m_new)
        inject = jnp.exp(am - m_new)
        c_new = decay[..., None, None] * c_st + inject[..., None, None] * c_in
        n_new = decay[..., None] * n_st + inject[..., None] * n_in
        return (c_new, n_new, m_new), (c_st, n_st, m_st)

    init = (jnp.zeros((B, H, dh, dh), jnp.float32), jnp.zeros((B, H, dh), jnp.float32), jnp.zeros((B, H), jnp.float32))
    xs = (jnp.moveaxis(c_chunk, 2, 0), jnp.moveaxis(n_chunk, 2, 0), jnp.moveaxis(b_last, 2, 0), jnp.moveaxis(a_max, 2, 0))
    _, (c_prev, n_prev, m_prev) = lax.scan(step, init, xs)
    c_prev = jnp.moveaxis(c_prev, 0, 2)
    n_prev = jnp.moveaxis(n_prev, 0, 2)
    m_prev = jnp.moveaxis(m_prev, 0, 2)

    lower = jnp.tril(jnp.ones((L, L), dtype=bool))
    d = jnp.where(lower, b[..., :, None] - b[..., None, :] + li[..., None, :], -jnp.inf)
    m_inter = b + m_prev[..., None]
    m_out = jnp.maximum(m_inter, jnp.max(d, axis=-1))
    dw = jnp.exp(d - m_out[..., None])
    inter_w = jnp.exp(m_inter - m_out)
    s = jnp.einsum('bhcjd,bhcld->bhcjl', q, k) * dw
    num = jnp.einsum('bhcjl,bhcld->bhcjd', s, v) + inter_w[..., None] * jnp.einsum('bhcde,bhcje->bhcjd', c_prev, q)
    den = jnp.sum(s, axis=-1) + inter_w * jnp.einsum('bhce,bhcje->bhcj', n_prev, q)
    h = num / jnp.maximum(jnp.abs(den), jnp.exp(-m_out))[..., None]
    return h.reshape(B, H, S, dh)

def mlstm_mixer(q_pre, k_pre, v, o_pre, gates, conv_w, conv_b, norm_g):
    B, S = q_pre.shape[0], q_pre.shape[1]
    H, dh = MLSTM_HEADS, MLSTM_HD
    qk = jnp.concatenate([q_pre, k_pre], axis=-1)
    qk = lax.conv_general_dilated(qk, conv_w, window_strides=(1,), padding=[(CONV_W // 2, CONV_W // 2)],
                                  dimension_numbers=('NWC', 'WIO', 'NWC'), feature_group_count=2 * MLSTM_W) + conv_b
    qk = jax.nn.silu(qk)
    q, k = jnp.split(qk, 2, axis=-1)

    def heads(t):
        return t.reshape(B, S, H, dh).transpose(0, 2, 1, 3).astype(jnp.float32)

    q = heads(q) * (MLSTM_HD ** -0.5)
    k = heads(k)
    v = heads(v)
    g = gates.astype(jnp.float32).reshape(B, S, 4, H).transpose(2, 0, 3, 1)
    h_fwd = mlstm_one_direction(q, k, v, g[0], jax.nn.log_sigmoid(g[1]))

    def flip(t):
        return jnp.flip(t, axis=2)

    h_bwd = flip(mlstm_one_direction(flip(q), flip(k), flip(v), flip(g[2]), flip(jax.nn.log_sigmoid(g[3]))))
    h = (h_fwd + h_bwd).transpose(0, 2, 1, 3)
    h = rms_norm_2(h, norm_g.reshape(H, dh))
    return h.reshape(B, S, MLSTM_W).astype(o_pre.dtype) * jax.nn.sigmoid(o_pre)

def hierarchical_moe(h, w_rg, b_rg, w_re, b_re, w_gate, w_up, w_down):
    B, S, D = h.shape
    t = h.reshape(B * S, D)
    tf = t.astype(jnp.float32)
    p_group = jax.nn.softmax(tf @ w_rg.astype(jnp.float32) + b_rg.astype(jnp.float32), axis=-1)
    p_top, g_idx = lax.top_k(p_group, 1)
    e_logits = (tf @ w_re.astype(jnp.float32) + b_re.astype(jnp.float32)).reshape(-1, N_GROUPS, EXPERTS_PER_GROUP)
    e_logits = jnp.take_along_axis(e_logits, g_idx[:, :, None], axis=1)[:, 0]
    p_exp = jax.nn.softmax(e_logits, axis=-1)
    w_top, e_idx = lax.top_k(p_exp, TOP_K)
    w_top = w_top / jnp.sum(w_top, axis=-1, keepdims=True) * p_top
    expert_id = g_idx * EXPERTS_PER_GROUP + e_idx
    combine = jnp.sum(jax.nn.one_hot(expert_id, N_EXPERTS, dtype=jnp.float32) * w_top[..., None], axis=1).astype(t.dtype)
    out = jnp.zeros_like(t)
    for g in range(N_GROUPS):
        sl = slice(g * EXPERTS_PER_GROUP, (g + 1) * EXPERTS_PER_GROUP)
        a = jnp.einsum('td,edf->tef', t, w_gate[sl])
        u = jnp.einsum('td,edf->tef', t, w_up[sl])
        act = jax.nn.silu(a) * u * combine[:, sl, None]
        out = out + jnp.einsum('tef,efd->td', act, w_down[sl])
    return out.reshape(B, S, D)

def second_inputs(seed: int = 0) -> dict:
    key = jax.random.key(seed)
    ks = iter(jax.random.split(key, 32))

    def normal(shape, scale):
        return scale * jax.random.normal(next(ks), shape, jnp.float32)

    D, H, F = D_MODEL, MLSTM_HEADS, EXPERT_HIDDEN
    x = normal((BATCH, SEQ, D), 1.0)
    c = normal((BATCH, D), 1.0)
    w_ada = normal((DEPTH, D, 6 * D), 0.5 * D ** -0.5)
    b_ada = normal((DEPTH, 6 * D), 0.02)
    norm1_g = 1.0 + normal((DEPTH, D), 0.02)
    w_in = normal((DEPTH, D, IN_W), D ** -0.5)
    b_in = normal((DEPTH, IN_W), 0.02)
    f_off = 4 * MLSTM_W
    f_bias = jnp.linspace(3.0, 6.0, H, dtype=jnp.float32)
    b_in = b_in.at[:, f_off + H:f_off + 2 * H].add(f_bias).at[:, f_off + 3 * H:f_off + 4 * H].add(f_bias)
    conv_w = normal((DEPTH, CONV_W, 1, 2 * MLSTM_W), CONV_W ** -0.5)
    conv_b = normal((DEPTH, 2 * MLSTM_W), 0.02)
    mlstm_norm_g = 1.0 + normal((DEPTH, MLSTM_W), 0.02)
    q_norm_g = 1.0 + normal((DEPTH, ATTN_HD), 0.02)
    k_norm_g = 1.0 + normal((DEPTH, ATTN_HD), 0.02)
    w_branch_m = normal((DEPTH, MLSTM_W, D), MLSTM_W ** -0.5)
    w_branch_a = normal((DEPTH, ATTN_W, D), ATTN_W ** -0.5)
    w_out = normal((DEPTH, D, D), D ** -0.5)
    norm2_g = 1.0 + normal((DEPTH, D), 0.02)
    w_router_group = normal((DEPTH, D, N_GROUPS), D ** -0.5)
    b_router_group = normal((DEPTH, N_GROUPS), 0.01)
    w_router_expert = normal((DEPTH, D, N_EXPERTS), D ** -0.5)
    b_router_expert = normal((DEPTH, N_EXPERTS), 0.01)
    w_gate = normal((DEPTH, N_EXPERTS, D, F), D ** -0.5)
    w_up = normal((DEPTH, N_EXPERTS, D, F), D ** -0.5)
    w_down = normal((DEPTH, N_EXPERTS, F, D), F ** -0.5)
    final_norm_g = 1.0 + normal((D,), 0.02)
    return {'x': x, 'c': c, 'w_ada': w_ada, 'b_ada': b_ada, 'norm1_g': norm1_g, 'w_in': w_in, 'b_in': b_in,
            'conv_w': conv_w, 'conv_b': conv_b, 'mlstm_norm_g': mlstm_norm_g, 'q_norm_g': q_norm_g,
            'k_norm_g': k_norm_g, 'w_branch_m': w_branch_m, 'w_branch_a': w_branch_a, 'w_out': w_out,
            'norm2_g': norm2_g, 'w_router_group': w_router_group, 'b_router_group': b_router_group,
            'w_router_expert': w_router_expert, 'b_router_expert': b_router_expert, 'w_gate': w_gate,
            'w_up': w_up, 'w_down': w_down, 'final_norm_g': final_norm_g}

def second_block(x, c, w_ada, b_ada, norm1_g, w_in, b_in, conv_w, conv_b, mlstm_norm_g, q_norm_g, k_norm_g,
              w_branch_m, w_branch_a, w_out, norm2_g, w_router_group, b_router_group, w_router_expert,
              b_router_expert, w_gate, w_up, w_down, final_norm_g):
    B, S, D = x.shape
    tables = rope_tables(S)
    offsets = np.cumsum(SPLIT_SIZES)[:-1].tolist()
    cond = jax.nn.silu(c)
    for l in range(DEPTH):
        mod = cond @ w_ada[l] + b_ada[l]
        shift1, scale1, gate1, shift2, scale2, gate2 = [m[:, None, :] for m in jnp.split(mod, 6, axis=-1)]
        h = rms_norm_2(x, norm1_g[l]) * (1 + scale1) + shift1
        proj = h @ w_in[l] + b_in[l]
        mq, mk, mv, mo, mgates, aq, ak, av, gm, ga = jnp.split(proj, offsets, axis=-1)
        y_m = mlstm_mixer(mq, mk, mv, mo, mgates, conv_w[l], conv_b[l], mlstm_norm_g[l])
        y_a = bidirectional_gqa(aq.reshape(B, S, ATTN_HEADS, ATTN_HD), ak.reshape(B, S, KV_HEADS, ATTN_HD),
                                av.reshape(B, S, KV_HEADS, ATTN_HD), q_norm_g[l], k_norm_g[l], tables)
        merged = jax.nn.sigmoid(gm) * (y_m @ w_branch_m[l]) + jax.nn.sigmoid(ga) * (y_a.astype(x.dtype) @ w_branch_a[l])
        x = x + gate1 * (merged @ w_out[l])
        h2 = rms_norm_2(x, norm2_g[l]) * (1 + scale2) + shift2
        x = x + gate2 * hierarchical_moe(h2, w_router_group[l], b_router_group[l], w_router_expert[l],
                                         b_router_expert[l], w_gate[l], w_up[l], w_down[l])
    return rms_norm_2(x, final_norm_g)


def setup_inputs(seed=0):
    out = dict(first_inputs(seed))
    for name, value in second_inputs(seed + 1).items():
        if name != "x":
            out[name + "_2"] = value
    return out


def reference(
    x, mem, rel_bias, norm_mix_w, norm_ffn_w, final_norm_w, mem_norm_w, mem_w_kv, w_out,
    gdn_w_in, gdn_conv_w, gdn_a_log, gdn_dt_bias, gdn_norm_w, nsa_w_in, nsa_cmp_pos_k,
    nsa_cmp_w1_k, nsa_cmp_w2_k, nsa_cmp_pos_v, nsa_cmp_w1_v, nsa_cmp_w2_v, ffn_w_up, ffn_conv_w,
    ffn_conv_b, ffn_w_down, c_2, w_ada_2, b_ada_2, norm1_g_2, w_in_2, b_in_2, conv_w_2,
    conv_b_2, mlstm_norm_g_2, q_norm_g_2, k_norm_g_2, w_branch_m_2, w_branch_a_2, w_out_2,
    norm2_g_2, w_router_group_2, b_router_group_2, w_router_expert_2, b_router_expert_2,
    w_gate_2, w_up_2, w_down_2, final_norm_g_2,
):
    x = first_block(
        x, mem, rel_bias, norm_mix_w, norm_ffn_w, final_norm_w, mem_norm_w, mem_w_kv, w_out,
        gdn_w_in, gdn_conv_w, gdn_a_log, gdn_dt_bias, gdn_norm_w, nsa_w_in, nsa_cmp_pos_k,
        nsa_cmp_w1_k, nsa_cmp_w2_k, nsa_cmp_pos_v, nsa_cmp_w1_v, nsa_cmp_w2_v, ffn_w_up,
        ffn_conv_w, ffn_conv_b, ffn_w_down,
    )
    return second_block(
        x, c_2, w_ada_2, b_ada_2, norm1_g_2, w_in_2, b_in_2, conv_w_2, conv_b_2, mlstm_norm_g_2,
        q_norm_g_2, k_norm_g_2, w_branch_m_2, w_branch_a_2, w_out_2, norm2_g_2,
        w_router_group_2, b_router_group_2, w_router_expert_2, b_router_expert_2, w_gate_2,
        w_up_2, w_down_2, final_norm_g_2,
    )


_drawn_inputs = setup_inputs


def setup_inputs(seed=0):
    import zlib

    import numpy as np

    out = dict(_drawn_inputs(seed))
    spreads = {}
    factors = {'mem_norm_w': 8.0,
     'gdn_norm_w': 2.996,
     'nsa_cmp_pos_k': 8.0,
     'ffn_conv_b': 3.19,
     'norm1_g_2': 6.929,
     'conv_b_2': 8.0,
     'mlstm_norm_g_2': 8.0,
     'q_norm_g_2': 8.0,
     'k_norm_g_2': 8.0,
     'norm2_g_2': 3.484,
     'b_router_group_2': 5.239,
     'b_router_expert_2': 6.3,
     'final_norm_g_2': 2.852}
    for name, (base, spread) in spreads.items():
        noise = np.random.default_rng([zlib.crc32(name.encode()), seed]).standard_normal(out[name].shape)
        drawn = base * np.exp(spread * noise) if base else spread * noise
        out[name] = __import__('jax').numpy.asarray(drawn.astype(out[name].dtype))
    for name, factor in factors.items():
        out[name] = (out[name] * factor).astype(out[name].dtype)
    return out
```

```python
from contextlib import ExitStack

import numpy as np

import concourse.bass as bass
from concourse import mybir

F32 = mybir.dt.float32
U32 = mybir.dt.uint32
ALU = mybir.AluOpType
ACT = mybir.ActivationFunctionType
AX = mybir.AxisListType
MUL, ADD, SUB, MAX, MIN = ALU.mult, ALU.add, ALU.subtract, ALU.max, ALU.min
NEG = -1e30
FLOOR = -1e28
NSLOT = 5
SLOT = 4096
ARENA = 16384


class Handle:

    def __init__(self, sem, step):
        self.sem, self.step, self.value, self.used = sem, step, None, False


class Queues:

    def __init__(self, nc, ctx):
        self.nc = nc
        self.sems = {k: ctx.enter_context(nc.semaphore(f"s_{k}")) for k in ("pe", "dve", "act", "pool")}
        self.q = {k: [] for k in ("pe", "dve", "act", "pool", "sp")}
        self.last = {}

    def add(self, k, fn, w=(), chain=False):
        w = [x for x in w if x is not None]
        if chain and k in self.last:
            w.append(self.last[k])
        for x in w:
            x.used = True
        h = Handle(self.sems[k], 1)
        self.q[k].append((fn, w, h))
        self.last[k] = h
        return h

    def dma(self, k, out, in_, sem, value, w=(), **kw):
        for x in w:
            x.used = True
        h = Handle(sem, 16)
        h.value, h.used = value, True
        self.q[k].append((lambda e: e.dma_start(out, in_, **kw), list(w), h))
        return h

    def count(self):
        for k in self.sems:
            n = 0
            for _, _, h in self.q[k]:
                if h.step == 1 and h.used:
                    n += 1
                    h.value = n

    def write(self, k, eng):
        seen = {}
        for fn, w, h in self.q[k]:
            need = {}
            for x in w:
                need[id(x.sem)] = max(need.get(id(x.sem), (0, None))[0], x.value), x.sem
            for i, (val, sem) in need.items():
                if seen.get(i, 0) < val:
                    eng.wait_ge(sem, val)
                    seen[i] = val
            ins = fn(eng)
            if h.used:
                ins.then_inc(h.sem, h.step)


class Ring:

    def __init__(self, places):
        self.places, self.busy, self.n = places, [[] for _ in places], 0

    def get(self):
        i = self.n % len(self.places)
        self.n += 1
        return i, self.places[i], self.busy[i]

    def put(self, i, readers):
        self.busy[i] = list(readers)


def vector_columns():
    at, n = {}, 0
    for name, cols in (("mix", 16), ("ffn", 16), ("mem", 16), ("gconv", 96), ("gnorm", 1), ("fconv", 132),
                       ("fconvb", 44), ("posk", 32), ("posv", 32), ("bqk", 16), ("bo", 8), ("bgm", 16), ("bga", 16),
                       ("mconv", 80), ("mconvb", 16), ("mnorm", 8), ("c", 8)):
        at[name] = n
        n += cols
    return at, n


def row_columns():
    at, n = {}, 0
    for name, cols in (("alog", 8), ("dt", 8), ("brg", 8), ("bre", 64), ("qg", 128), ("kg", 128), ("bgate", 32)):
        at[name] = n
        n += cols
    return at, n


def constants():
    p = np.arange(128)
    t = np.arange(256)
    parts = {}
    parts["ident"] = np.eye(128)
    parts["ones"] = np.ones((128, 128))
    parts["up"] = np.stack([(p[:, None] + 128 * k <= t[None]) for k in range(2)], 1).reshape(128, 512)
    parts["down"] = np.stack([(p[:, None] + 128 * k >= t[None]) for k in range(2)], 1).reshape(128, 512)
    parts["id2"] = np.stack([(p[:, None] + 128 * k == t[None]) for k in range(2)], 1).reshape(128, 512)
    parts["incl"] = p[:, None] >= p[None]
    levels = []
    for s in (1, 2, 4, 8, 16, 32, 64):
        m = (p[:, None] // (2 * s) == p[None] // (2 * s)) & (p[:, None] // s > p[None] // s)
        if s == 1:
            parts["lev1"] = m
        levels.append(m.T)
    parts["levT"] = np.stack(levels, 1).reshape(128, 7 * 128)
    parts["mfwd"] = np.stack([np.where(t[None] <= p[:, None] + 128 * k, 0.0, NEG) for k in range(2)], 1).reshape(128, 512)
    parts["mbwd"] = np.stack([np.where(t[None] >= p[:, None] + 128 * k, 0.0, NEG) for k in range(2)], 1).reshape(128, 512)
    half = 32
    inv = (10000.0 ** (-np.arange(0, half, 2, dtype=np.float32) / half)).astype(np.float32)
    row = np.repeat(np.arange(4, dtype=np.float32), 64)
    col = np.tile(np.arange(64, dtype=np.float32), 4)
    ar, ac = row[:, None] * inv, col[:, None] * inv
    c = np.concatenate([np.cos(ar), np.cos(ar), np.cos(ac), np.cos(ac)], 1)
    s = np.concatenate([-np.sin(ar), np.sin(ar), -np.sin(ac), np.sin(ac)], 1)
    parts["ropec"] = c.reshape(2, 128, 64).transpose(1, 0, 2).reshape(128, 128)
    parts["ropes"] = s.reshape(2, 128, 64).transpose(1, 0, 2).reshape(128, 128)
    parts["iota"] = np.broadcast_to(np.arange(8.0), (128, 8))
    at, n = {}, 0
    for k, v in parts.items():
        at[k] = n
        n += v.shape[1]
    table = np.concatenate([np.asarray(v, np.float32) for v in parts.values()], 1)
    d = 255 - np.arange(512)
    exact, f = 16, np.float32
    lg = np.log(np.maximum(d, 1).astype(f) / f(exact)) / f(np.log(128 / exact))
    big = np.minimum(exact + (lg * f(16)).astype(np.int32), 31)
    bucket = np.where(d < exact, np.maximum(d, 0), big)
    hot = np.zeros((33, 512), np.float32)
    hot[bucket[d >= 0], np.nonzero(d >= 0)[0]] = 1.0
    hot[32, d < 0] = 1.0
    return np.ascontiguousarray(table), at, n, hot


def build(nc, t, out, dbg=None):
    vat, nvec = vector_columns()
    rat, nrow = row_columns()
    _, cat_, ncst, _ = constants()
    with ExitStack() as ctx:
        def sb(name, shape, dt=F32):
            return ctx.enter_context(nc.sbuf_tensor(name, shape, dt))

        Q = Queues(nc, ctx)
        wring = sb("wring", [128, NSLOT * SLOT])
        X = sb("X", [128, 2, 1024])
        XN = sb("XN", [128, 2, 1024])
        HT = sb("HT", [128, 8, 256])
        MN = sb("MN", [128, 8, 256])
        PV = sb("PV", [128, nvec])
        RB = sb("RB", [128, nrow])
        CS = sb("CS", [128, ncst])
        SW = sb("SW", [128, 8, 144])
        AR = sb("AR", [128, ARENA])
        SM = sb("SM", [128, 1024])
        banks = [ctx.enter_context(nc.psum_tensor(f"ps{i}", [128, 512], F32)) for i in range(8)]
        scratch = nc.dram_tensor("bias_rows", [8, 128, 512], F32, kind="Internal").ap()

        wsem = [ctx.enter_context(nc.semaphore(f"w{i}")) for i in range(NSLOT)]
        dsems = {}

        def dsem(name):
            if name not in dsems:
                dsems[name] = [ctx.enter_context(nc.semaphore(f"d_{name}")), 0]
            return dsems[name]

        def load(group, dst, src, w=(), k="sp", **kw):
            s = dsem(group)
            s[1] += 16
            return Q.dma(k, dst, src, s[0], s[1], w, **kw)

        def loaded(group):
            s = dsem(group)
            h = Handle(s[0], 16)
            h.value, h.used = s[1], True
            return h

        def pe(fn, w=()):
            return Q.add("pe", fn, w)

        def v(fn, w=()):
            return Q.add("dve", fn, w, chain=True)

        def a(fn, w=()):
            return Q.add("act", fn, w, chain=True)

        def g(fn, w=()):
            return Q.add("pool", fn, w, chain=True)

        def mm(o, l, r, start, stop, w=()):
            return pe(lambda e: e.matmul(o, l, r, start=start, stop=stop), w)

        def tp(o, i, w=(), n=128):
            return pe(lambda e: e.transpose(o, i, IDENT[0:n, 0:n]), w)

        def act(o, i, f, w=(), **kw):
            return a(lambda e: e.activation(o, i, f, **kw), w)

        def ts(o, i, s1, s2, op0, op1=None, w=(), q=v):
            if op1 is None:
                return q(lambda e: e.tensor_scalar(o, i, s1, None, op0), w)
            return q(lambda e: e.tensor_scalar(o, i, s1, s2, op0, op1), w)

        def tt(o, i0, i1, op, w=(), q=v):
            return q(lambda e: e.tensor_tensor(o, i0, i1, op), w)

        def stt(o, i0, s, i1, op0, op1, w=()):
            return v(lambda e: e.scalar_tensor_tensor(o, i0, s, i1, op0, op1), w)

        def cp(o, i, w=(), q=v):
            return q(lambda e: e.tensor_copy(o, i), w)

        def red(o, i, op, w=()):
            return v(lambda e: e.tensor_reduce(o, i, AX.X, op), w)

        def barrier():
            last = list(Q.last.values())
            for k in ("pe", "dve", "act", "pool"):
                if k in Q.last:
                    Q.pending[k] = list(last)

        Q.pending = {}
        plain_add = Q.add

        def add(k, fn, w=(), chain=False):
            return plain_add(k, fn, list(w) + Q.pending.pop(k, []), chain)
        Q.add = add

        def edge():
            return list(Q.last.values())

        class Arena:
            n = 0

            def take(self, *shape):
                k = int(np.prod(shape))
                ap = AR[:, self.n:self.n + k]
                self.n += k
                assert self.n <= ARENA, self.n
                if len(shape) == 2:
                    return ap.rearrange("p (a b) -> p a b", a=shape[0])
                if len(shape) == 3:
                    return ap.rearrange("p (a b c) -> p a b c", a=shape[0], b=shape[1])
                return ap

        ar = Arena()
        small = [0]

        def sm(*shape):
            k = int(np.prod(shape))
            if small[0] + k > 1024:
                small[0] = 0
            ap = SM[:, small[0]:small[0] + k]
            small[0] += k
            if len(shape) == 2:
                return ap.rearrange("p (a b) -> p a b", a=shape[0])
            return ap

        def C(name, n, rows=128):
            return CS[0:rows, cat_[name]:cat_[name] + n]

        def bc(ap, n):
            return ap.broadcast_to([ap.shape[0], n])

        IDENT = C("ident", 128)
        ONES = C("ones", 128)

        def vec(name, i):
            return PV[:, vat[name] + i:vat[name] + i + 1]

        PA = Ring([banks[i] for i in range(4)])
        PB = Ring([banks[i] for i in range(4, 8)])
        W = Ring([wring[:, i * SLOT:(i + 1) * SLOT] for i in range(NSLOT)])

        turns = [0] * NSLOT

        def fill(parts):
            i, place, busy = W.get()
            for dst, src in parts(place):
                turns[i] += 16
                h = Q.dma("sp", dst, src, wsem[i], turns[i], busy)
            return i, place, h

        def weights(src, kt, n):
            view = lambda place: place[:, 0:kt * n].rearrange("p (k n) -> p k n", k=kt)
            i, place, h = fill(lambda place: [(view(place), src.rearrange("(k p) n -> p k n", p=128))])
            return i, view(place), h

        load("c", CS[:, :], t["cst"])
        load("c", PV[:, :], t["vecs"])
        load("c", RB[:, :], t["rows"].broadcast_to([128, nrow]))
        load("x", X[:, :, :], t["x"][0].rearrange("(a p) d -> p a d", p=128))
        load("c2", SW[:, :, 0:16], t["gdn_w_in"][0, :, 4096:4112].rearrange("(k p) n -> p k n", p=128))
        load("c2", SW[:, :, 16:40], t["nsa_w_in"][0, :, 2560:2584].rearrange("(k p) n -> p k n", p=128))
        for l in range(2):
            o = 40 + 52 * l
            load("c2", SW[:, :, o:o + 16], t["w_in_2"][l, :, 2048:2064].rearrange("(k p) n -> p k n", p=128))
            load("c2", SW[:, :, o + 16:o + 20], t["w_router_group_2"][l].rearrange("(k p) n -> p k n", p=128))
            load("c2", SW[:, :, o + 20:o + 52], t["w_router_expert_2"][l].rearrange("(k p) n -> p k n", p=128))
        hc, hc2 = loaded("c"), loaded("c2")
        for k in ("pe", "dve", "act", "pool"):
            Q.pending[k] = [hc, hc2, loaded("x")]

        def probe(name, ap, w):
            if dbg is not None and name in dbg:
                h = load("dbg", dbg[name], ap, w)
                for k in ("pe", "dve", "act", "pool"):
                    Q.pending.setdefault(k, []).append(h)

        def power(x, w, y=None):
            if y is None:
                shape = list(x.shape)[1:]
                y = sm(*shape)
                z = sm(*shape)
            else:
                y, z = y
            v(lambda e: e.reciprocal(x, x), w)
            h = act(y, x, ACT.Sqrt, [Q.last["dve"]])
            v(lambda e: e.reciprocal(z, y), [h])
            stt(z, z, 0.5, x, MUL, MUL)
            return stt(x, y, 0.5, z, MUL, ADD)

        def rstd(src, dst, n, junk, w=()):
            hs = None
            for i in range(2):
                acc = dst[:, i:i + 1]
                hs = act(junk, src[:, i, :], ACT.Square, w, accum_out=acc)
            h = ts(dst, dst, 1.0 / n, 1e-6, MUL, ADD, [hs])
            return power(dst, [h])

        def to_features(src, dst, scale, w=()):
            hs = []
            for k in range(0, 8, 2):
                i, ps, busy = PB.get()
                for j in range(2):
                    for m in range(2):
                        h = tp(ps[:, j * 256 + m * 128:j * 256 + m * 128 + 128],
                               src[:, m, (k + j) * 128:(k + j) * 128 + 128], list(w) + busy)
                e = []
                for j in range(2):
                    o, s = dst[:, k + j, :], ps[:, j * 256:j * 256 + 256]
                    if scale is None:
                        e.append(cp(o, s, [h]) if k % 4 else act(o, s, ACT.Copy, [h]))
                    elif k % 4:
                        e.append(ts(o, s, scale(k + j), None, MUL, w=[h]))
                    else:
                        e.append(act(o, s, ACT.Copy, [h], scale=scale(k + j)))
                PB.put(i, e)
                hs += e
            return hs

        def norm_features(src, dst, scale):
            r = sm(2)
            h = rstd(src, r, 1024, XN[:, 0, :])
            for i in range(2):
                h = ts(XN[:, i, :], src[:, i, :], r[:, i:i + 1], None, MUL)
            return to_features(XN, dst, scale, [h])

        def gemm_f(src_w, kt, rhs, evac, w=(), n=None, cols=None, keep=None):
            n = n or src_w.shape[1]
            slot, wt, landed = keep or weights(src_w, kt, n)
            cols = cols or range(0, n, 128)
            h = None
            for c in range(0, len(cols), 2):
                i, ps, busy = PB.get()
                readers = []
                hh = []
                for j, c0 in enumerate(cols[c:c + 2]):
                    for k in range(kt):
                        h = mm(ps[:, j * 256:j * 256 + 256], wt[:, k, c0:c0 + 128], rhs[:, k, :],
                               k == 0, k == kt - 1, list(w) + busy + [landed])
                    hh.append(h)
                for j, c0 in enumerate(cols[c:c + 2]):
                    readers += evac(c0 // 128, ps[:, j * 256:j * 256 + 256], hh[-1])
                PB.put(i, readers)
            if keep is None:
                W.put(slot, [h])
            return h

        def gemm_t(wt, landed, kt, lhs, n, c0, evac, w=()):
            h = None
            for m in range(2):
                i, ps, busy = PB.get()
                for k in range(kt):
                    h = mm(ps[:, 0:n], lhs[:, k, m * 128:m * 128 + 128], wt[:, k, c0:c0 + n],
                           k == 0, k == kt - 1, list(w) + busy + [landed])
                PB.put(i, evac(m, ps[:, 0:n], h))
            return h

        def down(srcs, lhs, evac, w=()):
            got = [PA.get() for _ in range(4)]
            busy = [b for _, _, bs in got for b in bs]
            total = sum(s[1] for s in srcs)
            kk = 0
            for src, kt in srcs:
                slot, wt, landed = weights(src, kt, 1024)
                for k in range(kt):
                    for m in range(2):
                        for c in range(2):
                            h = mm(got[2 * m + c][1][:, :], lhs[:, kk, m * 128:m * 128 + 128],
                                   wt[:, k, c * 512:c * 512 + 512], kk == 0, kk == total - 1,
                                   list(w) + busy + [landed])
                    kk += 1
                W.put(slot, [h])
            for m in range(2):
                for c in range(2):
                    PA.put(got[2 * m + c][0], evac(m, c, got[2 * m + c][1], h))

        def add_x(m, c, ps, h):
            o = X[:, m, c * 512:c * 512 + 512]
            return [tt(o, ps[:, :], o, ADD, [h])]

        def taps(y, ps, name, base, stride, k, center, w=()):
            wc = lambda j: vec(name, base + stride * j)
            h = ts(y, ps, wc(center), None, MUL, w=w)
            for j in range(k):
                d = j - center
                if d < 0:
                    h = stt(y[:, -d:256], ps[:, 0:256 + d], wc(j), y[:, -d:256], MUL, ADD)
                elif d > 0:
                    h = stt(y[:, 0:256 - d], ps[:, d:256], wc(j), y[:, 0:256 - d], MUL, ADD)
            return h

        def attend(ps_s, hs, scale, bias, gate, dst):
            m, s = sm(2), sm(2)
            view = ps_s[:, :].rearrange("p (a b) -> p a b", a=2)
            if bias is None:
                h = red(m, view, MAX, hs)
                h = ts(m, m, -scale, None, MUL)
                for i in range(2):
                    h2 = act(dst[:, i, :], view[:, i, :], ACT.Exp, [h] + list(hs), bias=m[:, i:i + 1], scale=scale,
                             accum_out=s[:, i:i + 1])
                rd = [h2]
            else:
                h = stt(dst, view, scale, bias, MUL, ADD, hs)
                rd = [h]
                h = red(m, dst, MAX)
                h = ts(m, m, FLOOR, -1.0, MAX, MUL)
                for i in range(2):
                    h2 = act(dst[:, i, :], dst[:, i, :], ACT.Exp, [h], bias=m[:, i:i + 1], accum_out=s[:, i:i + 1])
            h = ts(s, s, 1e-30, None, MAX, w=[h2])
            h = v(lambda e: e.reciprocal(s, s))
            if gate is not None:
                h = tt(s, s, gate, MUL)
            for i in range(2):
                h = ts(dst[:, i, :], dst[:, i, :], s[:, i:i + 1], None, MUL)
            return rd, h

        def turn(src, dst, w, n=256):
            i, ps, busy = PB.get()
            for m in range(2):
                for k in range(2):
                    h = tp(ps[:, k * 256 + m * 128:k * 256 + m * 128 + 128], src[:, m, k * 128:k * 128 + 128],
                           list(w) + busy)
            e = act(dst, ps[:, :].rearrange("p (a b) -> p a b", a=2), ACT.Copy, [h])
            PB.put(i, [e])
            return h, e

        def memory_attention(layer, CAT):
            KT = ar.take(4, 256)
            V = ar.take(2, 512)
            S = [ar.take(2, 256) for _ in range(2)]
            T = [ar.take(2, 256) for _ in range(2)]
            hm = norm_features_mem(layer)
            hk = []

            def ek(c, ps, h):
                r = act(KT[:, c, :], ps, ACT.Copy, [h])
                hk.append(r)
                return [r]

            def ev(m, ps, h):
                r = cp(V[:, m, :], ps, [h])
                hk.append(r)
                return [r]

            gemm_f(t["mem_w_kv"][layer, :, 0:512], 8, MN, ek, hm)
            slot, wt, landed = weights(t["mem_w_kv"][layer, :, 512:1024], 8, 512)
            W.put(slot, [gemm_t(wt, landed, 8, MN, 512, 0, ev, hm)])
            ring = Ring(list(zip(S, T)))
            fin = []
            for h4 in range(4):
                r, (s, tr), rb = ring.get()
                i, ps, busy = PB.get()
                for m in range(2):
                    h = mm(ps[:, m * 256:m * 256 + 256], CAT[:, 8 + h4, m * 128:m * 128 + 128], KT[:, h4, :],
                           True, True, busy + hk)
                    hq = h
                rd, hp = attend(ps, [h] + rb, 128.0 ** -0.5, None, None, s)
                PB.put(i, rd)
                h, e = turn(s, tr, [hp])
                i, ps, busy = PB.get()
                for k in range(2):
                    h = mm(ps[:, 0:256], V[:, k, h4 * 128:h4 * 128 + 128], tr[:, k, :], k == 0, k == 1, busy + [e])
                e = act(CAT[:, 8 + h4, :], ps[:, 0:256], ACT.Copy, [h, hq])
                PB.put(i, [e])
                ring.put(r, [h, hp])
                fin.append(e)
            return fin

        def norm_features_mem(layer):
            h = load("mem", XN[:, :, :], t["mem"][0].rearrange("(a p) d -> p a d", p=128), edge())
            Q.pending["act"] = [h]
            Q.pending["dve"] = [h]
            Q.pending["pe"] = [h]
            r = sm(2)
            rstd(XN, r, 1024, MN[:, 0:4, :].rearrange("p a b -> p (a b)"))
            for i in range(2):
                h = ts(XN[:, i, :], XN[:, i, :], r[:, i:i + 1], None, MUL)
            return to_features(XN, MN, lambda k: vec("mem", 8 * layer + k), [h] + [Q.last["act"]])


        def heads_softplus(dst, src, e1, w=()):
            h = ts(e1, src, -1.0, None, MUL, w=w)
            h = tt(e1, src, e1, MAX)
            h = act(e1, e1, ACT.Exp, [h], scale=-1.0)
            h = act(e1, e1, ACT.Ln, bias=1.0)
            return stt(dst, src, 0.0, e1, MAX, ADD, [h])

        def gdn(CAT):
            QK = ar.take(16, 256)
            VB = ar.take(8, 256)
            hT = norm_features(X, HT, lambda k: vec("mix", k))
            ab = ar.take(2, 16)
            sq = [ar.take(256) for _ in range(2)]
            sqr = Ring(sq)
            done = []

            def ab_out(m, ps, h):
                return [cp(ab[:, m, :], ps, [h])]

            gemm_t(SW[:, :, 0:16], None, 8, HT, 16, 0, ab_out, hT)
            hn = []
            for chunk in range(6):
                def ev(c, ps, h, chunk=chunk):
                    f = chunk * 4 + c
                    y = QK[:, f, :] if f < 16 else VB[:, f - 16, :]
                    hv = taps(y, ps, "gconv", f, 24, 4, 3, [h])
                    hs = act(y, y, ACT.Silu, [hv])
                    hn.append(hs)
                    return [hv]
                gemm_f(t["gdn_w_in"][0, :, chunk * 512:chunk * 512 + 512], 8, HT, ev, hT)
            for chunk in range(2):
                def ev(c, ps, h, chunk=chunk):
                    r = act(CAT[:, chunk * 4 + c, :], ps, ACT.Silu, [h])
                    return [r]
                gemm_f(t["gdn_w_in"][0, :, 3072 + chunk * 512:3584 + chunk * 512], 8, HT, ev, hT)

            def ev(c, ps, h):
                return [cp(CAT[:, 8 + c, :], ps, [h])]
            gemm_f(t["gdn_w_in"][0, :, 4112:4624], 8, HT, ev, hT)
            for f in range(16):
                r, s, rb = sqr.get()
                y = QK[:, f, :]
                h = act(s, y, ACT.Square, rb)
                i, ps, busy = PB.get()
                h = mm(ps[:, 0:256], ONES, s, True, True, busy + [h])
                h = ts(s, ps[:, 0:256], 1e-6, None, ADD, w=[h])
                PB.put(i, [h])
                power(s, [h], (XN[:, 0, (f % 2) * 512:(f % 2) * 512 + 256], XN[:, 0, (f % 2) * 512 + 256:(f % 2) * 512 + 512]))
                if f < 8:
                    h = stt(y, y, 128.0 ** -0.5, s, MUL, MUL)
                else:
                    h = tt(y, y, s, MUL)
                sqr.put(r, [h])
            hqk = h
            beta, gg, e1, gc, egc, tot, kd = (sm(2, 8) for _ in range(7))
            h = act(beta, ab[:, :, 0:8], ACT.Sigmoid, [hqk])
            h = tt(gg, ab[:, :, 8:16], RB[:, rat["dt"]:rat["dt"] + 8].unsqueeze(1).broadcast_to([128, 2, 8]), ADD)
            h = heads_softplus(gg, gg, e1)
            ea = sm(8)
            h = act(ea, RB[:, rat["alog"]:rat["alog"] + 8], ACT.Exp)
            h = stt(gg, gg, -1.0, ea.unsqueeze(1).broadcast_to([128, 2, 8]), MUL, MUL, [h])
            hg = h
            UP = C("up", 128)
            i, ps, busy = PB.get()
            for m in range(2):
                h = mm(ps[:, m * 8:m * 8 + 8], UP, gg[:, m, :], True, True, busy + [hg])
            h = mm(ps[:, 16:24], ONES, gg[:, 0, :], True, True)
            h = cp(gc.rearrange("p a b -> p (a b)"), ps[:, 0:16], [h])
            h = tt(kd[:, 0, :], ps[:, 16:24], gc[:, 0, :], SUB)
            PB.put(i, [h])
            h = act(kd[:, 0, :], kd[:, 0, :], ACT.Exp, [h])
            hke = act(egc, gc, ACT.Exp)
            KD = HT[:, 0:4, :].rearrange("p a b -> p (a b)")
            for hd in range(8):
                i, ps, busy = PB.get()
                for m in range(2):
                    h = tp(ps[:, m * 128:m * 128 + 128], VB[:, hd, m * 128:m * 128 + 128], busy + hn + [hqk])
                h = tp(ps[:, 256:384], QK[:, 8 + hd, 0:128], [hqk])
                for m in range(2):
                    hh = ts(XN[:, m, hd * 128:hd * 128 + 128], ps[:, m * 128:m * 128 + 128], beta[:, m, hd:hd + 1],
                            None, MUL, w=[h])
                hh = ts(KD[:, hd * 128:hd * 128 + 128], ps[:, 256:384], kd[:, 0, hd:hd + 1], None, MUL, w=[hke, h])
                PB.put(i, [hh])
            hvb = hh
            probe("vb", XN[:, :, :], [hvb])
            n0 = ar.n
            ST = HT[:, 4:8, :].rearrange("p a b -> p (a b)")
            D, DT, LT, BT, M1 = ([ar.take(4, 128) for _ in range(2)] for _ in range(5))
            AT = [ar.take(4, 128) for _ in range(2)]
            OT = VB
            hst = None
            hprev = [hvb]
            for m in range(2):
                tok = slice(m * 128, m * 128 + 128)
                hD, hDT, hLT, hAT = [None] * 2, [None] * 2, [None] * 2, [None] * 2
                for b in range(2):
                    i, ps, busy = PB.get()
                    for j in range(4):
                        hd = 4 * b + j
                        h = mm(ps[:, j * 128:j * 128 + 128], bc(gg[:, m, hd:hd + 1], 128), UP, True, True,
                               busy + hprev + [hg])
                    for j in range(4):
                        h2 = ts(M1[b][:, j, :], ps[:, j * 128:j * 128 + 128], gc[:, m, 4 * b + j:4 * b + j + 1], 0.0,
                                SUB, MAX, w=[h] + hprev)
                    PB.put(i, [h2])
                    h2 = act(M1[b], M1[b], ACT.Exp, [h2], scale=-1.0)
                    h2 = tt(M1[b], M1[b], C("incl", 128).unsqueeze(1).broadcast_to([128, 4, 128]), MUL, [h2])
                    i, ps, busy = PB.get()
                    i2, ps2, busy2 = PB.get()
                    for j in range(4):
                        hd = 4 * b + j
                        h = mm(ps[:, j * 128:j * 128 + 128], QK[:, 8 + hd, tok], QK[:, 8 + hd, tok], True, True, busy)
                        h = mm(ps2[:, j * 128:j * 128 + 128], QK[:, hd, tok], QK[:, 8 + hd, tok], True, True, busy2)
                    for j in range(4):
                        hl = stt(D[b][:, j, :], ps[:, j * 128:j * 128 + 128], beta[:, m, 4 * b + j:4 * b + j + 1],
                                 M1[b][:, j, :], MUL, MUL, [h])
                    PB.put(i, [hl])
                    ha = tt(BT[b], ps2[:, :].rearrange("p (a b) -> p a b", a=4), M1[b], MUL)
                    PB.put(i2, [ha])
                    i, ps, busy = PB.get()
                    i2, ps2, busy2 = PB.get()
                    for j in range(4):
                        h = tp(ps[:, j * 128:j * 128 + 128], D[b][:, j, :], busy + [hl, ha])
                        h = tp(ps2[:, j * 128:j * 128 + 128], BT[b][:, j, :], busy2)
                    p3 = ps[:, :].rearrange("p (a b) -> p a b", a=4)
                    hLT[b] = act(LT[b], p3, ACT.Copy, [h])
                    hAT[b] = act(AT[b], ps2[:, :].rearrange("p (a b) -> p a b", a=4), ACT.Copy, [h])
                    PB.put(i, [hLT[b]])
                    PB.put(i2, [hAT[b]])
                    ID4 = IDENT.unsqueeze(1).broadcast_to([128, 4, 128])
                    LEV = lambda s: CS[:, cat_["levT"] + 128 * s:cat_["levT"] + 128 * s + 128].unsqueeze(1)\
                        .broadcast_to([128, 4, 128])
                    h2 = tt(D[b], D[b], C("lev1", 128).unsqueeze(1).broadcast_to([128, 4, 128]), MUL, [h])
                    hD[b] = tt(D[b], ID4, D[b], SUB)
                    h2 = tt(DT[b], LT[b], LEV(0), MUL, [hLT[b]])
                    hDT[b] = tt(DT[b], ID4, DT[b], SUB)
                for s in range(1, 7):
                    for b in range(2):
                        hb = tt(BT[b], LT[b], LEV(s), MUL, [hLT[b]])
                        i, ps, busy = PB.get()
                        for j in range(4):
                            h = mm(ps[:, j * 128:j * 128 + 128], BT[b][:, j, :], D[b][:, j, :], True, True,
                                   busy + [hb, hD[b]])
                        hm = act(M1[b], ps[:, :].rearrange("p (a b) -> p a b", a=4), ACT.Copy, [h])
                        PB.put(i, [hm])
                        i, ps, busy = PB.get()
                        for j in range(4):
                            h = mm(ps[:, j * 128:j * 128 + 128], M1[b][:, j, :], DT[b][:, j, :], True, True,
                                   busy + [hm, hDT[b]])
                        if s < 6:
                            i2, ps2, busy2 = PB.get()
                            for j in range(4):
                                h = mm(ps2[:, j * 128:j * 128 + 128], DT[b][:, j, :], M1[b][:, j, :], True, True,
                                       busy2)
                        hDT[b] = tt(DT[b], DT[b], ps[:, :].rearrange("p (a b) -> p a b", a=4), SUB, [h])
                        PB.put(i, [hDT[b]])
                        if s < 6:
                            hD[b] = tt(D[b], D[b], ps2[:, :].rearrange("p (a b) -> p a b", a=4), SUB)
                            PB.put(i2, [hD[b]])
                for b in range(2):
                    o0, r0 = D[b], BT[b]
                    hr = [None] * 4
                    if m == 1:
                        i, ps, busy = PB.get()
                        i2, ps2, busy2 = PB.get()
                        for j in range(4):
                            hd = 4 * b + j
                            S = ST[:, hd * 128:hd * 128 + 128]
                            h = mm(ps[:, j * 128:j * 128 + 128], QK[:, 8 + hd, tok], S, True, True, busy + [hst])
                            h = mm(ps2[:, j * 128:j * 128 + 128], QK[:, hd, tok], S, True, True, busy2)
                        for j in range(4):
                            hd = 4 * b + j
                            e = egc[:, 1, hd:hd + 1]
                            h2 = ts(r0[:, j, :], ps[:, j * 128:j * 128 + 128], e, beta[:, 1, hd:hd + 1], MUL, MUL,
                                    w=[h])
                            h2 = tt(r0[:, j, :], XN[:, 1, hd * 128:hd * 128 + 128], r0[:, j, :], SUB)
                            h2 = ts(o0[:, j, :], ps2[:, j * 128:j * 128 + 128], e, None, MUL)
                        PB.put(i, [h2])
                        PB.put(i2, [h2])
                    i, ps, busy = PB.get()
                    for j in range(4):
                        hd = 4 * b + j
                        rhs = r0[:, j, :] if m else XN[:, 0, hd * 128:hd * 128 + 128]
                        h = mm(ps[:, j * 128:j * 128 + 128], DT[b][:, j, :], rhs, True, True,
                               busy + [hDT[b], h2, hvb])
                    hv = act(M1[b], ps[:, :].rearrange("p (a b) -> p a b", a=4), ACT.Copy, [h])
                    PB.put(i, [hv])
                    if m == 0:
                        i, ps, busy = PB.get()
                        for j in range(4):
                            hd = 4 * b + j
                            h = mm(ps[:, j * 128:j * 128 + 128], KD[:, hd * 128:hd * 128 + 128], M1[b][:, j, :],
                                   True, True, busy + [hv, hvb])
                        hst = cp(ST[:, b * 512:b * 512 + 512], ps[:, :], [h])
                        PB.put(i, [hst])
                    i, ps, busy = PB.get()
                    for j in range(4):
                        h = mm(ps[:, j * 128:j * 128 + 128], AT[b][:, j, :], M1[b][:, j, :], True, True,
                               busy + [hv, hAT[b]])
                    p3 = ps[:, :].rearrange("p (a b) -> p a b", a=4)
                    if m:
                        h2 = tt(o0, p3, o0, ADD, [h])
                    else:
                        h2 = cp(o0, p3, [h])
                    PB.put(i, [h2])
                    rs = sm(4)
                    for j in range(4):
                        h3 = act(r0[:, j, :], o0[:, j, :], ACT.Square, [h2], accum_out=rs[:, j:j + 1])
                    h2 = ts(rs, rs, 1.0 / 128, 1e-6, MUL, ADD, w=[h3])
                    h2 = power(rs, [h2])
                    for j in range(4):
                        h2 = ts(o0[:, j, :], o0[:, j, :], rs[:, j:j + 1], None, MUL)
                    i, ps, busy = PB.get()
                    for j in range(4):
                        h = tp(ps[:, j * 128:j * 128 + 128], o0[:, j, :], busy + [h2])
                    for j in range(4):
                        c = CAT[:, 4 * b + j, tok]
                        h2 = stt(c, ps[:, j * 128:j * 128 + 128], vec("gnorm", 0), c, MUL, MUL, [h])
                    PB.put(i, [h2])
                hprev = edge()
            return edge()

        def conv_glu(layer):
            ar.n = 0
            barrier()
            G = ar.take(22, 256)
            hT = norm_features(X, HT, lambda k: vec("ffn", 8 * layer + k))
            up = t["ffn_w_up"][layer]
            for val in range(2):
                for chunk in range(6):
                    n = 512 if chunk < 5 else 256

                    def ev(c, ps, h, chunk=chunk, val=val):
                        f = chunk * 4 + c
                        y = G[:, f, :]
                        if val:
                            return [tt(y, ps, y, MUL, [h] + hG)]
                        hv = taps(y, ps, "fconv", 66 * layer + f, 22, 3, 2, [h])
                        act(y, y, ACT.Silu, [hv], bias=vec("fconvb", 22 * layer + f))
                        return [hv]
                    hG = edge()
                    gemm_f(up[:, val * 2816 + chunk * 512:val * 2816 + chunk * 512 + n], 8, HT, ev, hT)
            dn = t["ffn_w_down"][layer]
            down([(dn[c * 512:min(c * 512 + 512, 2816)], 4 if c < 5 else 2) for c in range(6)], G, add_x, edge())

        def project_out(src, layer, CAT, kt, evac=add_x):
            down([(src[c * 512:c * 512 + 512], 4) for c in range(kt // 4)], CAT, evac, edge())

        def nsa(CAT):
            ar.n = 12 * 256
            KC = ar.take(4, 256)
            KS = ar.take(4, 256)
            VS = ar.take(2, 512)
            GT = ar.take(2, 24)
            BI = ar.take(8, 512)
            n0 = ar.n
            hT = norm_features(X, HT, lambda k: vec("mix", 8 + k))
            tab, hot = ar.take(8), ar.take(512)
            rep = Ring([ar.take(512) for _ in range(2)])
            load("tab", tab[0:33, :], t["tab"], edge())
            load("tab", hot[0:33, :], t["hot"], edge())
            htab = loaded("tab")
            for hd in range(8):
                r, row, rb = rep.get()
                i, ps, busy = PB.get()
                h = mm(ps[:, :], bc(tab[0:33, hd:hd + 1], 128), hot[0:33, :], True, True, busy + [htab])
                h = cp(row, ps[:, :], [h] + rb)
                PB.put(i, [h])
                h = load(f"row{hd}", scratch[hd], row, [h])
                rep.put(r, [h])
                src = scratch[hd]
                for m in range(2):
                    ap = bass.AP(src.tensor, src.offset + 255 - 128 * m, [[511, 128], [1, 256]])
                    load("bias", BI[:, hd, m * 256:m * 256 + 256], ap, [h])
            hb = loaded("bias")
            hr = []

            def keep(dst):
                def ev(c, ps, h):
                    r = act(dst(c), ps, ACT.Copy, [h])
                    hr.append(r)
                    return [r]
                return ev
            win = t["nsa_w_in"][0]
            for ch in range(2):
                gemm_f(win[:, ch * 512:ch * 512 + 512], 8, HT, keep(lambda c: CAT[:, 4 * ch + c, :]), hT)
            gemm_f(win[:, 1024:1536], 8, HT, keep(lambda c: KC[:, c, :]), hT)
            for ch in range(2):
                slot, wt, landed = weights(win[:, 1536 + 512 * ch:2048 + 512 * ch], 8, 512)
                gemm_f(None, 8, HT, keep(lambda c: KS[:, 2 * ch + c, :]), hT, n=512, cols=[0, 128],
                       keep=(slot, wt, landed))

                def ev(m, ps, h):
                    r = cp(VS[:, m, ch * 256:ch * 256 + 256], ps, [h])
                    hr.append(r)
                    return [r]
                W.put(slot, [gemm_t(wt, landed, 8, HT, 256, 256, ev, hT)])

            def ev(m, ps, h):
                r = act(GT[:, m, :], ps, ACT.Sigmoid, [h])
                hr.append(r)
                return [r]
            gemm_t(SW[:, :, 16:40], None, 8, HT, 24, 0, ev, hT)
            gemm_f(win[:, 2584:3096], 8, HT, keep(lambda c: CAT[:, 8 + c, :]), hT)
            ar.n = n0
            barrier()
            BL = ar.take(32, 32)
            HID = ar.take(32)
            KCT, VC = ar.take(32), ar.take(2, 128)
            for kv in range(2):
                for gr in range(2):
                    src = KC[:, 2 * kv + gr, :]
                    s = bass.AP(src.tensor, src.offset, [list(src.ap[0]), [1, 32], [16, 15]])
                    p = PV[:, vat["posk"] + 32 * kv:vat["posk"] + 32 * kv + 32].unsqueeze(2).broadcast_to([128, 32, 15])
                    h = tt(BL[:, :, gr * 16:gr * 16 + 15], s, p, ADD, [Q.last["pe"], Q.last["act"]])
                h = v(lambda e: e.memset(BL[:, :, 15:32:16], 0.0))
                hbl = h
                i, ps, busy = PB.get()
                w1 = t["nsa_cmp_w1_v" if kv else "nsa_cmp_w1_k"][0]
                slot, wt, landed = weights(w1, 32, 128)
                for l in range(32):
                    h = mm(ps[:, 0:32], wt[:, l, :], BL[:, l, :], l == 0, l == 31, busy + [landed, hbl])
                W.put(slot, [h])
                h = act(HID, ps[:, 0:32], ACT.Silu, [h])
                PB.put(i, [h])
                slot, wt, landed = weights(t["nsa_cmp_w2_v" if kv else "nsa_cmp_w2_k"][0], 1, 128)
                i, ps, busy = PB.get()
                if kv == 0:
                    h = mm(ps[:, 0:32], wt[:, 0, :], HID, True, True, busy + [landed, h])
                    e = cp(KCT, ps[:, 0:32], [h])
                else:
                    for gr in range(2):
                        h = mm(ps[0:15, gr * 128:gr * 128 + 128], HID[:, gr * 16:gr * 16 + 15], wt[:, 0, :], True, True,
                               busy + [landed, h])
                    e = cp(VC[0:15, :, :], ps[0:15, 0:256].rearrange("p (a b) -> p a b", a=2), [h])
                PB.put(i, [e])
                W.put(slot, [h])
            probe("kct", KCT, [e])
            hcmp = e
            bufs = Ring([[ar.take(2, 256), ar.take(2, 256), ar.take(2, 256), ar.take(2, 256)] for _ in range(2)])
            SC = Ring([[ar.take(2, 16), ar.take(256)] for _ in range(2)])
            scale = 128.0 ** -0.5
            for hd in range(8):
                gr = hd // 4
                r, bf, rb = bufs.get()
                bias = BI[:, hd, :].rearrange("p (a b) -> p a b", a=2)
                trs = []
                for br in range(2):
                    i, ps, busy = PB.get()
                    for m in range(2):
                        h = mm(ps[:, m * 256:m * 256 + 256], CAT[:, hd, m * 128:m * 128 + 128], KS[:, 2 * br + gr, :],
                               True, True, busy + hr)
                    rd, hp = attend(ps, [h, hb] + rb, scale, bias, GT[:, :, 3 * hd + 1 + br], bf[br])
                    PB.put(i, rd)
                    h, e = turn(bf[br], bf[2 + br], [hp] + rb)
                    trs.append(e)
                r2, (sc, pt), rb2 = SC.get()
                i, ps, busy = PB.get()
                for m in range(2):
                    hqq = mm(ps[:, m * 16:m * 16 + 15], CAT[:, hd, m * 128:m * 128 + 128],
                             KCT[:, gr * 16:gr * 16 + 15], True, True, busy + [hcmp])
                mx, s = sm(2), sm(2)
                sc15 = sc[:, :, 0:15]
                h = stt(sc15, ps[:, 0:32].rearrange("p (a b) -> p a b", a=2)[:, :, 0:15], scale, bias[:, :, 31:256:16],
                        MUL, ADD, [hqq] + rb2)
                PB.put(i, [h])
                h = red(mx, sc15, MAX)
                h = ts(mx, mx, FLOOR, -1.0, MAX, MUL)
                for m in range(2):
                    h = act(sc15[:, m, :], sc15[:, m, :], ACT.Exp, [h], bias=mx[:, m:m + 1], accum_out=s[:, m:m + 1])
                h = ts(s, s, 1e-30, None, MAX, w=[h])
                h = v(lambda e, s=s: e.reciprocal(s, s))
                h = tt(s, s, GT[:, :, 3 * hd], MUL)
                for m in range(2):
                    h = ts(sc15[:, m, :], sc15[:, m, :], s[:, m:m + 1], None, MUL)
                i, ps, busy = PB.get()
                for m in range(2):
                    h = tp(ps[0:15, m * 128:m * 128 + 128], sc15[:, m, :], busy + [h])
                e = act(pt[0:15, :], ps[0:15, 0:256], ACT.Copy, [h] + rb2)
                PB.put(i, [e])
                i, ps, busy = PB.get()
                mm(ps[:, 0:256], VC[0:15, gr, :], pt[0:15, :], True, False, busy + [e])
                for br in range(2):
                    for k in range(2):
                        h = mm(ps[:, 0:256], VS[:, k, br * 256 + gr * 128:br * 256 + gr * 128 + 128],
                               bf[2 + br][:, k, :], False, br == 1 and k == 1, trs)
                e = cp(CAT[:, hd, :], ps[:, 0:256], [h])
                PB.put(i, [e])
                bufs.put(r, [h, e])
                SC.put(r2, [h, e])

        def modulation(layer, MOD):
            hb = load("ada", MOD, t["b_ada_2"][layer:layer + 1, :].broadcast_to([128, 6144]), edge())
            cc = sm(8)
            hc_ = act(cc, PV[:, vat["c"]:vat["c"] + 8], ACT.Silu)
            for ch in range(12):
                slot, wt, landed = weights(t["w_ada_2"][layer, :, ch * 512:ch * 512 + 512], 8, 512)
                i, ps, busy = PB.get()
                for k in range(8):
                    h = mm(ps[:, :], bc(cc[:, k:k + 1], 128), wt[:, k, :], k == 0, k == 7, busy + [landed, hc_])
                W.put(slot, [h])
                m = MOD[:, ch * 512:ch * 512 + 512]
                h = tt(m, ps[:, :], m, ADD, [h, hb])
                PB.put(i, [h])
            for i, name in ((1, "norm1_g_2"), (4, "norm2_g_2")):
                hl = load("ng", XN[:, 0, :], t[name][layer:layer + 1, :].broadcast_to([128, 1024]), edge())
                m = MOD[:, i * 1024:i * 1024 + 1024]
                stt(m, m, 1.0, XN[:, 0, :], ADD, MUL, [hl])

        def modulated(MOD, which):
            r = sm(2)
            rstd(X, r, 1024, XN[:, 0, :])
            for i in range(2):
                h = stt(XN[:, i, :], X[:, i, :], r[:, i:i + 1], MOD[:, (3 * which + 1) * 1024:(3 * which + 2) * 1024],
                        MUL, MUL)
                h = tt(XN[:, i, :], XN[:, i, :], MOD[:, 3 * which * 1024:(3 * which + 1) * 1024], ADD)
            return to_features(XN, HT, None, [h])

        def gated_add(MOD, which):
            def ev(m, c, ps, h):
                gt = MOD[:, (3 * which + 2) * 1024 + c * 512:(3 * which + 2) * 1024 + c * 512 + 512]
                j = XN[:, m, c * 512:c * 512 + 512]
                o = X[:, m, c * 512:c * 512 + 512]
                h1 = tt(j, ps[:, :], gt, MUL, [h])
                tt(o, o, j, ADD)
                return [h1]
            return ev

        def mixers(layer, MOD):
            n0 = ar.n
            hT = modulated(MOD, 0)
            YM, YA = ar.take(4, 256), ar.take(4, 256)
            n1 = ar.n
            MQK = ar.take(8, 256)
            MV = ar.take(2, 512)
            LG = ar.take(2, 16)
            AQ = ar.take(2, 768)
            BV = AR[:, ar.n:ar.n + 1280]
            win = t["w_in_2"][layer]
            hb = load("bv", BV[:, 0:512], t["b_in_2"][layer:layer + 1, 1024:1536].broadcast_to([128, 512]), edge())
            load("bv", BV[:, 512:1280], t["b_in_2"][layer:layer + 1, 2064:2832].broadcast_to([128, 768]), edge())
            hb = loaded("bv")

            def ev(m, ps, h):
                return [tt(LG[:, m, :], ps, RB[:, rat["bgate"] + 16 * layer:rat["bgate"] + 16 * layer + 16], ADD, [h])]
            o = 40 + 52 * layer
            gemm_t(SW[:, :, o:o + 16], None, 8, HT, 16, 0, ev, hT)
            RAW = [XN[:, 0, j * 256:j * 256 + 256] for j in range(4)]
            rr = Ring(RAW)
            hx = list(hT)
            for ch in range(2):
                def ev(c, ps, h):
                    f = 4 * ch + c
                    i, raw, rb = rr.get()
                    h1 = act(raw, ps, ACT.Identity, [h] + rb + hx, bias=vec("bqk", 8 * layer + f))
                    hv = taps(MQK[:, f, :], raw, "mconv", 40 * layer + f, 8, 5, 2, [h1])
                    rr.put(i, [hv])
                    act(MQK[:, f, :], MQK[:, f, :], ACT.Silu, [hv], bias=vec("mconvb", 8 * layer + f))
                    return [h1]
                gemm_f(win[:, ch * 512:ch * 512 + 512], 8, HT, ev, hT)
            for c0, dst, n, b0 in ((1024, MV, 512, 0), (2064, AQ, 512, 512), (2576, AQ, 256, 1024)):
                slot, wt, landed = weights(win[:, c0:c0 + n], 8, n)

                def ev(m, ps, h):
                    d = dst[:, m, 512:768] if n == 256 else dst[:, m, 0:512]
                    return [tt(d, ps, BV[:, b0:b0 + n], ADD, [h, hb])]
                W.put(slot, [gemm_t(wt, landed, 8, HT, n, 0, ev, hT)])

            def ev(c, ps, h):
                return [act(YM[:, c, :], ps, ACT.Sigmoid, [h], bias=vec("bo", 4 * layer + c))]
            gemm_f(win[:, 1536:2048], 8, HT, ev, hT)
            barrier()
            probe(f"mqk{layer}", MQK, edge())
            probe(f"aq{layer}", AQ, edge())
            n2 = ar.n
            lf, e1, b_, bb = sm(2, 8), sm(2, 8), sm(2, 4), sm(2, 4)
            LG2 = LG.rearrange("p a (b c) -> p a b c", b=4)
            lf4 = lf.rearrange("p a (b c) -> p a b c", b=2)
            neg = sm(2, 8)
            neg4 = neg.rearrange("p a (b c) -> p a b c", b=2)
            h = ts(neg4, LG2[:, :, 1:4:2, :], -1.0, None, MUL)
            heads_softplus(neg, neg, e1)
            i, ps, busy = PB.get()
            hn = Q.last["dve"]
            for m in range(2):
                for d in range(2):
                    U = C("down" if d else "up", 512)
                    for k in range(2):
                        h = mm(ps[:, m * 8 + d * 4:m * 8 + d * 4 + 4], U[:, k * 256 + m * 128:k * 256 + m * 128 + 128],
                               neg[:, k, 4 * d:4 * d + 4], k == 0, k == 1, busy + [hn])
            nb = sm(2, 8)
            h = cp(nb.rearrange("p a b -> p (a b)"), ps[:, 0:16], [h])
            PB.put(i, [h])
            cb = sm(2, 8)
            h = tt(cb.rearrange("p a (b c) -> p a b c", b=2), LG2[:, :, 0:3:2, :], nb.rearrange("p a (b c) -> p a b c", b=2),
                   ADD)
            hcb = h
            E = Ring([[ar.take(2, 256), ar.take(2, 256), ar.take(2, 256)] for _ in range(2)])
            hmx = []
            for hd in range(4):
                r, (dwf, dwb, st), rb = E.get()
                i, pq, busy = PB.get()
                for m in range(2):
                    hq = mm(pq[:, m * 256:m * 256 + 256], MQK[:, hd, m * 128:m * 128 + 128], MQK[:, 4 + hd, :],
                            True, True, busy)
                dens = sm(2, 2)
                nm = sm(2, 2)
                for d in range(2):
                    dw = (dwf, dwb)[d]
                    i2, ps, busy2 = PB.get()
                    for k in range(2):
                        h = mm(ps[:, 0:256], bc(cb[:, k, 4 * d + hd:4 * d + hd + 1], 128),
                               C("id2", 512)[:, k * 256:k * 256 + 256], k == 0, k == 1, busy2 + [hcb])
                    mask = C("mbwd" if d else "mfwd", 512).rearrange("p (a b) -> p a b", a=2)
                    h = tt(dw, mask, ps[:, 0:256].unsqueeze(1).broadcast_to([128, 2, 256]), ADD, [h] + rb)
                    PB.put(i2, [h])
                    mm_ = nm[:, d, :]
                    h = red(mm_, dw, MAX)
                    h = ts(mm_, mm_, 0.0, -1.0, MAX, MUL)
                    for m in range(2):
                        h1 = act(dw[:, m, :], dw[:, m, :], ACT.Exp, [h], bias=mm_[:, m:m + 1])
                    for m in range(2):
                        h = v(lambda e, dw=dw, m=m, d=d, pq=pq, dens=dens: e.tensor_tensor_reduce(
                            dw[:, m, :], pq[:, m * 256:m * 256 + 256], dw[:, m, :], 128.0 ** -0.5, 0.0, MUL, ADD,
                            dens[:, d, m:m + 1]), [h1, hq])
                PB.put(i, [h])
                em = sm(2, 2)
                h = tt(em, nm, nb.rearrange("p a (b c) -> p b c a", b=2)[:, :, hd, :], ADD)
                h1 = act(em, em, ACT.Exp, [h])
                h = stt(em, dens, -1.0, em, MUL, MAX, [h1])
                h = tt(dens, dens, em, MAX)
                h = v(lambda e, dens=dens: e.reciprocal(dens, dens))
                for m in range(2):
                    h = ts(dwf[:, m, :], dwf[:, m, :], dens[:, 0, m:m + 1], None, MUL)
                    h = stt(dwf[:, m, :], dwb[:, m, :], dens[:, 1, m:m + 1], dwf[:, m, :], MUL, ADD)
                h, e = turn(dwf, dwb, [h])
                i, ps, busy = PB.get()
                for m in range(2):
                    for k in range(2):
                        h = mm(ps[:, m * 128:m * 128 + 128], dwb[:, k, m * 128:m * 128 + 128],
                               MV[:, k, hd * 128:hd * 128 + 128], k == 0, k == 1, busy + [e])
                rs = sm(2)
                s3 = st[:, :, 0:128]
                p3 = ps[:, 0:256].rearrange("p (a b) -> p a b", a=2)
                for m in range(2):
                    h1 = act(s3[:, m, :], p3[:, m, :], ACT.Square, [h] + rb, accum_out=rs[:, m:m + 1])
                h = ts(rs, rs, 1.0 / 128, 1e-6, MUL, ADD, w=[h1])
                h = power(rs, [h])
                for m in range(2):
                    h = ts(s3[:, m, :], p3[:, m, :], rs[:, m:m + 1], None, MUL)
                PB.put(i, [h])
                i, ps, busy = PB.get()
                for m in range(2):
                    h = tp(ps[:, m * 128:m * 128 + 128], s3[:, m, :], busy + [h])
                E.put(r, [h])
                h = stt(YM[:, hd, :], ps[:, 0:256], vec("mnorm", 4 * layer + hd), YM[:, hd, :], MUL, MUL, [h])
                PB.put(i, [h])
            probe(f"ym{layer}", YM, edge())
            ar.n = n1
            ar.n = n2
            barrier()
            sqb = AR[:, n1:n1 + 640]
            rs = sm(2, 10)
            for m in range(2):
                h = tt(sqb, AQ[:, m, 0:640], AQ[:, m, 0:640], MUL)
                h = red(rs[:, m, :], sqb.rearrange("p (h d) -> p h d", d=64), ADD)
            h = ts(rs, rs, 1.0 / 64, 1e-6, MUL, ADD)
            h = power(rs, [h])
            QR = ar.take(2, 640)
            T2 = AR[:, n1:n1 + 640]
            for m in range(2):
                x3 = AQ[:, m, 0:640].rearrange("p (h d) -> p h d", d=64)
                h = tt(x3, x3, rs[:, m, :].unsqueeze(2).broadcast_to([128, 10, 64]), MUL)
                for nme, h0, h1 in (("qg", 0, 8), ("kg", 8, 10)):
                    gn = RB[:, rat[nme] + 64 * layer:rat[nme] + 64 * layer + 64].unsqueeze(1)\
                        .broadcast_to([128, h1 - h0, 64])
                    h = tt(x3[:, h0:h1, :], x3[:, h0:h1, :], gn, MUL)
                cos = CS[:, cat_["ropec"] + 64 * m:cat_["ropec"] + 64 * m + 64]
                sin = CS[:, cat_["ropes"] + 64 * m:cat_["ropes"] + 64 * m + 64]
                x4 = AQ[:, m, 0:640].rearrange("p (h u d) -> p h u d", u=4, d=16)
                t4 = T2.rearrange("p (h u d) -> p h u d", u=4, d=16)
                s4 = sin.rearrange("p (u d) -> p u d", u=4)
                for u in range(4):
                    h = tt(t4[:, :, u, :], x4[:, :, u ^ 1, :], s4[:, u, :].unsqueeze(1).broadcast_to([128, 10, 16]), MUL)
                o3 = QR[:, m, :].rearrange("p (h d) -> p h d", d=64)
                h = tt(o3, x3, cos.unsqueeze(1).broadcast_to([128, 10, 64]), MUL)
                h = tt(QR[:, m, :], QR[:, m, :], T2, ADD)
            QT = AR[:, n1:n1 + 1280].rearrange("p (a b) -> p a b", a=5)
            PR = AR[:, n1 + 1280:n1 + 1536].rearrange("p (a b) -> p a b", a=2)
            hq = []
            for pr in range(5):
                i, ps, busy = PB.get()
                if pr < 4:
                    for m in range(2):
                        q3 = QR[:, m, 0:512].rearrange("p (u h d) -> p h u d", u=2, d=64)
                        h = cp(PR[:, m, :].rearrange("p (u d) -> p u d", u=2), q3[:, pr, :, :], hq[-1:] + [Q.last["pe"]])
                    for m in range(2):
                        h = tp(ps[:, m * 128:m * 128 + 128], PR[:, m, :], busy + [h])
                else:
                    for m in range(2):
                        h = tp(ps[:, m * 128:m * 128 + 128], QR[:, m, 512:640], busy)
                e = act(QT[:, pr, :], ps[:, 0:256], ACT.Copy, [h])
                PB.put(i, [e])
                hq.append(e)
            hq.append(h)
            E = Ring([[ar.take(2, 256), ar.take(2, 256)] for _ in range(2)])
            for hd in range(8):
                pr, u = hd % 4, hd // 4
                p0 = slice(64 * u, 64 * u + 64)
                r, (s, tr), rb = E.get()
                i, ps, busy = PB.get()
                for m in range(2):
                    h = mm(ps[:, m * 256:m * 256 + 256], QT[p0, pr, m * 128:m * 128 + 128], QT[p0, 4, :], True, True,
                           busy + hq)
                rd, hp = attend(ps, [h] + rb, 64.0 ** -0.5, None, None, s)
                PB.put(i, rd)
                h, e = turn(s, tr, [hp] + rb)
                i, ps, busy = PB.get()
                for k in range(2):
                    h = mm(ps[p0, 0:256], AQ[:, k, 640 + 64 * u:704 + 64 * u], tr[:, k, :], k == 0, k == 1, busy + [e])
                e = cp(YA[p0, pr, :], ps[p0, 0:256], [h])
                PB.put(i, [e])
                E.put(r, [h, e])
            probe(f"ya{layer}", YA, edge())
            barrier()
            ar.n = n1
            MG = ar.take(8, 256)
            SG = Ring([ar.take(2, 256) for _ in range(2)])
            wb = []
            for half in range(2):
                cs = slice(half * 512, half * 512 + 512)
                gmw = weights(win[:, 2832 + half * 512:3344 + half * 512], 8, 512)
                gaw = weights(win[:, 3856 + half * 512:4368 + half * 512], 8, 512)
                srcm = t["w_branch_m_2"][layer, :, cs].rearrange("(k p) n -> p k n", p=128)
                srca = t["w_branch_a_2"][layer, :, cs].rearrange("(u k p) n -> u p k n", u=2, p=64)
                half_slot = lambda place, j: place[:, 2048 * j:2048 * j + 2048].rearrange("p (k n) -> p k n", k=4)
                i3, place, hbr = fill(lambda place: [(half_slot(place, 0), srcm), (half_slot(place, 1)[0:64], srca[0]),
                                                     (half_slot(place, 1)[64:128], srca[1])])
                wm, wa = half_slot(place, 0), half_slot(place, 1)
                for c in range(4):
                    f = 4 * half + c
                    r, sg, rb = SG.get()
                    i, ps, busy = PB.get()
                    i2, ps2, busy2 = PB.get()
                    for j, (sl, wt, landed) in enumerate((gmw, gaw)):
                        for k in range(8):
                            h = mm(ps[:, j * 256:j * 256 + 256], wt[:, k, c * 128:c * 128 + 128], HT[:, k, :],
                                   k == 0, k == 7, busy + [landed])
                    for j, (wt, y) in enumerate(((wm, YM), (wa, YA))):
                        for k in range(4):
                            h2 = mm(ps2[:, j * 256:j * 256 + 256], wt[:, k, c * 128:c * 128 + 128], y[:, k, :],
                                    k == 0, k == 3, busy2 + [hbr])
                    for j in range(2):
                        e = act(sg[:, j, :], ps[:, j * 256:j * 256 + 256], ACT.Sigmoid, [h] + rb,
                                bias=vec("bga" if j else "bgm", 8 * layer + f))
                    PB.put(i, [e])
                    e = tt(sg, ps2[:, :].rearrange("p (a b) -> p a b", a=2), sg, MUL, [h2, e])
                    PB.put(i2, [e])
                    e = tt(MG[:, f, :], sg[:, 0, :], sg[:, 1, :], ADD)
                    SG.put(r, [e])
                W.put(gmw[0], [h])
                W.put(gaw[0], [h])
                W.put(i3, [h2])
            project_out(t["w_out_2"][layer], layer, MG, 8, gated_add(MOD, 0))

        def moe(layer, MOD):
            hT = modulated(MOD, 1)
            o = 56 + 52 * layer
            LGT = ar.take(2, 40)
            CB = ar.take(2, 32)

            def ev(m, ps, h):
                h1 = tt(LGT[:, m, 0:4], ps[:, 0:4], RB[:, rat["brg"] + 4 * layer:rat["brg"] + 4 * layer + 4], ADD, [h])
                h1 = tt(LGT[:, m, 8:40], ps[:, 4:36], RB[:, rat["bre"] + 32 * layer:rat["bre"] + 32 * layer + 32], ADD)
                return [h1]
            gemm_t(SW[:, :, o:o + 36], None, 8, HT, 36, 0, ev, hT)
            probe(f"lgt{layer}", LGT, edge())
            v(lambda e: e.memset(LGT[:, :, 4:8], NEG))
            IO = C("iota", 8)
            for m in range(2):
                mx, s, pg, top, ix, ixf, gm = sm(1), sm(1), sm(8), sm(8), sm(8), sm(8), sm(8)
                el, w1, one, sel = sm(8), sm(2), sm(8), sm(4, 8)
                ixu = ix.bitcast(U32)
                red(mx, LGT[:, m, 0:8], MAX)
                h = ts(mx, mx, -1.0, None, MUL)
                h = act(pg, LGT[:, m, 0:8], ACT.Exp, [h], bias=mx, accum_out=s)
                v(lambda e, s=s: e.reciprocal(s, s), [h])
                ts(pg, pg, s, None, MUL)
                v(lambda e, pg=pg: e.memset(pg[:, 4:8], -1.0))
                v(lambda e, top=top, pg=pg: e.max(top, pg))
                v(lambda e, top=top, pg=pg, ixu=ixu: e.max_index(ixu, top, pg))
                cp(ixf, ixu)
                ptop = sm(1)
                cp(ptop, top[:, 0:1])
                ts(gm, IO, ixf[:, 0:1], None, ALU.is_equal)
                e3 = LGT[:, m, 8:40].rearrange("p (a b) -> p a b", a=4)
                tt(sel, e3, gm[:, 0:4].unsqueeze(2).broadcast_to([128, 4, 8]), MUL)
                tt(sel[:, 0:2, :], sel[:, 0:2, :], sel[:, 2:4, :], ADD)
                tt(el, sel[:, 0, :], sel[:, 1, :], ADD)
                red(mx, el, MAX)
                h = ts(mx, mx, -1.0, None, MUL)
                h = act(el, el, ACT.Exp, [h], bias=mx, accum_out=s)
                v(lambda e, s=s: e.reciprocal(s, s), [h])
                ts(el, el, s, None, MUL)
                v(lambda e, top=top, el=el: e.max(top, el))
                v(lambda e, top=top, el=el, ixu=ixu: e.max_index(ixu, top, el))
                cp(ixf, ixu)
                tt(s, top[:, 0:1], top[:, 1:2], ADD)
                v(lambda e, s=s: e.reciprocal(s, s))
                tt(s, s, ptop, MUL)
                ts(w1, top[:, 0:2], s, None, MUL)
                ts(one, IO, ixf[:, 0:1], w1[:, 0:1], ALU.is_equal, MUL)
                ts(el, IO, ixf[:, 1:2], w1[:, 1:2], ALU.is_equal, MUL)
                tt(one, one, el, ADD)
                for gr in range(4):
                    h = ts(CB[:, m, gr * 8:gr * 8 + 8], one, gm[:, gr:gr + 1], None, MUL)
            hcb = h
            probe(f"cb{layer}", CB, [h])
            GA = Ring([ar.take(4, 256) for _ in range(2)])
            CR = Ring([ar.take(256) for _ in range(2)])
            got = [PA.get() for _ in range(4)]
            busyA = [b for _, _, bs in got for b in bs]
            hd_ = None
            for ex in range(32):
                wg = weights(t["w_gate_2"][layer, ex], 8, 512)
                wu = weights(t["w_up_2"][layer, ex], 8, 512)
                wd = weights(t["w_down_2"][layer, ex], 4, 1024)
                r, ga, rb = GA.get()
                r2, cr, rb2 = CR.get()
                i, ps, busy = PB.get()
                for k in range(2):
                    h = mm(ps[:, 0:256], bc(CB[:, k, ex:ex + 1], 128), C("id2", 512)[:, k * 256:k * 256 + 256],
                           k == 0, k == 1, busy + [hcb])
                hc_ = act(cr, ps[:, 0:256], ACT.Copy, [h] + rb2)
                PB.put(i, [hc_])
                ops = []
                for f in range(4):
                    i, ps, busy = PB.get()
                    for j, (sl, wt, landed) in enumerate((wg, wu)):
                        for k in range(8):
                            h = mm(ps[:, j * 256:j * 256 + 256], wt[:, k, f * 128:f * 128 + 128], HT[:, k, :],
                                   k == 0, k == 7, busy + [landed] + hT)
                    e = act(ga[:, f, :], ps[:, 0:256], ACT.Silu, [h] + rb)
                    e = tt(ga[:, f, :], ps[:, 256:512], ga[:, f, :], MUL, [h, e])
                    PB.put(i, [e])
                    e = tt(ga[:, f, :], ga[:, f, :], cr, MUL, [hc_])
                    ops.append(e)
                W.put(wg[0], [h])
                W.put(wu[0], [h])
                for f in range(4):
                    for m in range(2):
                        for c in range(2):
                            h = mm(got[2 * m + c][1][:, :], ga[:, f, m * 128:m * 128 + 128],
                                   wd[1][:, f, c * 512:c * 512 + 512], ex == 0 and f == 0, ex == 31 and f == 3,
                                   [ops[f], wd[2]] + busyA)
                W.put(wd[0], [h])
                GA.put(r, [h])
                CR.put(r2, [ops[-1]])
            ev = gated_add(MOD, 1)
            for m in range(2):
                for c in range(2):
                    PA.put(got[2 * m + c][0], ev(m, c, got[2 * m + c][1], h))

        ar.n = 0
        CAT = ar.take(12, 256)
        gdn(CAT)
        probe("mix0", CAT, edge())
        ar.n = 12 * 256
        barrier()
        memory_attention(0, CAT)
        probe("cat0", CAT, edge())
        project_out(t["w_out"][0], 0, CAT, 12)
        probe("xa0", X[:, :, :], edge())
        conv_glu(0)
        probe("xb0", X[:, :, :], edge())
        barrier()
        nsa(CAT)
        ar.n = 12 * 256
        barrier()
        memory_attention(1, CAT)
        probe("cat1", CAT, edge())
        project_out(t["w_out"][1], 1, CAT, 12)
        conv_glu(1)
        barrier()

        def last_norm(src):
            hl = load("fn", MN[:, 0:4, :].rearrange("p a b -> p (a b)"), src.broadcast_to([128, 1024]), edge())
            r = sm(2)
            rstd(X, r, 1024, XN[:, 0, :])
            for i in range(2):
                h = stt(X[:, i, :], X[:, i, :], r[:, i:i + 1], MN[:, 0:4, :].rearrange("p a b -> p (a b)"), MUL, MUL,
                        [hl])
            return h
        last_norm(t["final_norm_w"])
        probe("x1", X[:, :, :], edge())
        for layer in range(2):
            barrier()
            ar.n = 0
            MOD = ar.take(6144)
            modulation(layer, MOD)
            probe(f"mod{layer}", MOD, edge())
            barrier()
            mixers(layer, MOD)
            probe(f"xm{layer}", X[:, :, :], edge())
            barrier()
            ar.n = 6144
            moe(layer, MOD)
            probe(f"xe{layer}", X[:, :, :], edge())
        barrier()
        h = last_norm(t["final_norm_g_2"])
        h = load("out", out[0].rearrange("(a p) d -> p a d", p=128), X[:, :, :], [h])
        finals = [h] + ([loaded("dbg")] if dbg is not None else [])

        Q.count()
        block = ctx.enter_context(nc.Block())

        @block.sync
        def _(eng):
            Q.write("sp", eng)
            for x in finals:
                eng.wait_ge(x.sem, x.value)

        @block.tensor
        def _(eng):
            Q.write("pe", eng)

        @block.vector
        def _(eng):
            Q.write("dve", eng)

        @block.scalar
        def _(eng):
            Q.write("act", eng)

        @block.gpsimd
        def _(eng):
            Q.write("pool", eng)


_BIG = ["x", "mem", "mem_w_kv", "w_out", "gdn_w_in", "nsa_w_in", "nsa_cmp_w1_k", "nsa_cmp_w2_k", "nsa_cmp_w1_v",
        "nsa_cmp_w2_v", "ffn_w_up", "ffn_w_down", "w_ada_2", "b_ada_2", "norm1_g_2", "norm2_g_2", "w_in_2", "b_in_2",
        "w_branch_m_2", "w_branch_a_2", "w_out_2", "w_router_group_2", "w_router_expert_2", "w_gate_2", "w_up_2",
        "w_down_2"]


def lay_out(inputs):
    a = {k: np.ascontiguousarray(inputs[k]) for k in _BIG}
    i = {k: np.asarray(v) for k, v in inputs.items()}
    cols = lambda z: np.asarray(z).reshape(-1, 128)
    b = i["b_in_2"]
    parts = [i["norm_mix_w"], i["norm_ffn_w"], i["mem_norm_w"], i["gdn_conv_w"], i["gdn_norm_w"], i["ffn_conv_w"],
             i["ffn_conv_b"], i["nsa_cmp_pos_k"], i["nsa_cmp_pos_v"], b[:, 0:1024], b[:, 1536:2048], b[:, 2832:3856],
             b[:, 3856:4880], i["conv_w_2"], i["conv_b_2"], i["mlstm_norm_g_2"], i["c_2"]]
    a["vecs"] = np.ascontiguousarray(np.concatenate([cols(z) for z in parts], 0).T)
    rows = [i["gdn_a_log"], i["gdn_dt_bias"], i["b_router_group_2"], i["b_router_expert_2"], i["q_norm_g_2"],
            i["k_norm_g_2"], b[:, 2048:2064]]
    a["rows"] = np.ascontiguousarray(np.concatenate([np.asarray(z).reshape(-1) for z in rows])[None])
    table, _, _, hot = constants()
    a["cst"] = table
    a["hot"] = hot
    a["tab"] = np.ascontiguousarray(np.concatenate([i["rel_bias"], np.full((1, 8), NEG, np.float32)], 0))
    a["final_norm_w"] = i["final_norm_w"].reshape(1, 1024)
    a["final_norm_g_2"] = i["final_norm_g_2"].reshape(1, 1024)
    return a


def kernel(**inputs):
    import concourse.bacc as _bacc
    from concourse.bass_utils import run_bass_kernel_spmd as _run

    nc = _bacc.Bacc("TRN2", target_bir_lowering=False, num_devices=1)
    arrays, t = {}, {}
    for name, a in lay_out(inputs).items():
        arrays[f"in_{name}"] = a
        t[name] = nc.dram_tensor(f"in_{name}", a.shape, F32, kind="ExternalInput").ap()
    out = nc.dram_tensor("out_x", (1, 256, 1024), F32, kind="ExternalOutput").ap()
    build(nc, t, out)
    r = _run(nc, [arrays], core_ids=[0])
    return r.results[0]["out_x"]
```

```python
from contextlib import ExitStack

import numpy as np

import concourse.bass as bass
from concourse import mybir

F32 = mybir.dt.float32
I32 = mybir.dt.int32
U32 = mybir.dt.uint32
ALU = mybir.AluOpType
ACT = mybir.ActivationFunctionType
AX = mybir.AxisListType
MUL, ADD, SUB, MAX, MIN = ALU.mult, ALU.add, ALU.subtract, ALU.max, ALU.min
NEG = -1e30
FLOOR = -1e28
NSLOT = 5
SLOT = 4096
ARENA = 16384
CAP = 64
LIMIT = CAP


class Handle:

    def __init__(self, sem, step, value=None):
        self.sem, self.step, self.value, self.used, self.free = sem, step, value, value is not None, None


class Queues:

    def __init__(self, nc, ctx):
        self.nc = nc
        self.sems = {k: ctx.enter_context(nc.semaphore(f"s_{k}")) for k in ("pe", "dve", "act", "pool")}
        self.q = {k: [] for k in ("pe", "dve", "act", "pool", "sp")}
        self.last = {}
        self.pending = {}

    def add(self, k, fn, w=(), chain=False):
        w = [x for x in w if x is not None] + self.pending.pop(k, [])
        if chain and k in self.last:
            w.append(self.last[k])
        for x in w:
            x.used = True
        h = Handle(self.sems[k], 1)
        self.q[k].append((fn, w, h))
        self.last[k] = h
        return h

    def dma(self, k, out, in_, sem, value, w=(), **kw):
        for x in w:
            x.used = True
        h = Handle(sem, 16, value)
        self.q[k].append((lambda e: e.dma_start(out, in_, **kw), list(w), h))
        return h

    def free(self, k, sem):
        self.q[k].append(("free", sem))

    def part(self, flag, limit, w):
        for x in w:
            x.used = True
        self.trunk, self.ways, self.before = self.q, [], dict(self.last)
        self.flag, self.limit, self.flag_w = flag, limit, list(w)
        self.way()

    def way(self):
        self.last = dict(self.before)
        self.pending = {}
        new = {k: [] for k in ("pe", "dve", "act")}
        self.ways.append(new)
        self.q = dict(self.trunk) | new

    def meet(self):
        self.q = self.trunk
        self.last = dict(self.before)
        out = []
        for k in ("pe", "dve", "act"):
            j = Handle(self.sems[k], 1)
            j.used = True
            self.q[k].append(("ways", self.flag, self.limit, self.flag_w, self.ways[0][k], self.ways[1][k], j))
            self.last[k] = j
            out.append(j)
        return out

    def count_list(self, items, n):
        free = []
        before = None
        ends = [it[2] for it in items if len(it) == 3]
        if ends:
            ends[-1].used = True
        for it in items:
            if it[0] == "free":
                if before is not None and not before.used and before.free is None:
                    before.free = it[1]
                else:
                    free.append(it[1])
            elif it[0] == "ways":
                assert not free
                ends = [self.count_list(x, n) for x in it[4:6]]
                it[6].value = n = max(ends) + 1
                for x, end in zip(it[4:6], ends):
                    x.append(("raise", n - end, end, None))
            else:
                before = h = it[2]
                if h.step == 1 and h.used:
                    n += 1
                    h.value = n
                elif h.step == 1 and free:
                    h.free = free.pop(0)
        if free:
            items.append(("rest", free, None, n))
        return n

    def count(self):
        for k in self.sems:
            self.count_list(self.q[k], 0)

    def write(self, k, eng, items=None, seen=None):
        seen = {} if seen is None else seen

        def wait(handles):
            need = {}
            for x in handles:
                need[id(x.sem)] = max(need.get(id(x.sem), (0, None))[0], x.value), x.sem
            for i, (val, sem) in need.items():
                if seen.get(i, 0) < val:
                    eng.wait_ge(sem, val)
                    seen[i] = val

        for it in self.q[k] if items is None else items:
            if it[0] == "free":
                continue
            if it[0] == "rest":
                eng.wait_ge(self.sems[k], it[3])
                for sem in it[1]:
                    eng.sem_inc(sem, 1)
                continue
            if it[0] == "raise":
                if it[2]:
                    eng.wait_ge(self.sems[k], it[2])
                eng.sem_inc(self.sems[k], it[1])
                continue
            if it[0] == "ways":
                wait(it[3])
                val = eng.value_load(it[1], min_val=0, max_val=256)
                with eng.If(val < it[2] + 1):
                    self.write(k, eng, it[4], dict(seen))
                with eng.Else():
                    self.write(k, eng, it[5], dict(seen))
                continue
            fn, w, h = it
            wait(w)
            ins = fn(eng)
            if h.used:
                ins.then_inc(h.sem, h.step)
            elif h.free is not None:
                ins.then_inc(h.free, 1)


class Ring:

    def __init__(self, places):
        self.places, self.busy, self.n = places, [[] for _ in places], 0

    def get(self):
        i = self.n % len(self.places)
        self.n += 1
        return i, self.places[i], self.busy[i]

    def put(self, i, readers):
        self.busy[i] = list(readers)


def vector_columns():
    at, n = {}, 0
    for name, cols in (("mix", 16), ("ffn", 16), ("mem", 16), ("gconv", 96), ("gnorm", 1), ("fconv", 132),
                       ("fconvb", 44), ("posk", 32), ("posv", 32), ("bqk", 16), ("bo", 8), ("bgm", 16), ("bga", 16),
                       ("mconv", 80), ("mconvb", 16), ("mnorm", 8), ("c", 8)):
        at[name] = n
        n += cols
    return at, n


def row_columns():
    at, n = {}, 0
    for name, cols in (("alog", 8), ("dt", 8), ("brg", 8), ("bre", 64), ("qg", 128), ("kg", 128), ("bgate", 32)):
        at[name] = n
        n += cols
    return at, n


def constants():
    p = np.arange(128)
    t = np.arange(256)
    parts = {}
    parts["ident"] = np.eye(128)
    parts["ones"] = np.ones((128, 128))
    parts["up"] = np.stack([(p[:, None] + 128 * k <= t[None]) for k in range(2)], 1).reshape(128, 512)
    parts["down"] = np.stack([(p[:, None] + 128 * k >= t[None]) for k in range(2)], 1).reshape(128, 512)
    parts["id2"] = np.stack([(p[:, None] + 128 * k == t[None]) for k in range(2)], 1).reshape(128, 512)
    parts["incl"] = p[:, None] >= p[None]
    levels = []
    for s in (1, 2, 4, 8, 16, 32, 64):
        m = (p[:, None] // (2 * s) == p[None] // (2 * s)) & (p[:, None] // s > p[None] // s)
        if s == 1:
            parts["lev1"] = m
        levels.append(m.T)
    parts["levT"] = np.stack(levels, 1).reshape(128, 7 * 128)
    parts["mfwd"] = np.stack([np.where(t[None] <= p[:, None] + 128 * k, 0.0, NEG) for k in range(2)], 1).reshape(128, 512)
    parts["mbwd"] = np.stack([np.where(t[None] >= p[:, None] + 128 * k, 0.0, NEG) for k in range(2)], 1).reshape(128, 512)
    half = 32
    inv = (10000.0 ** (-np.arange(0, half, 2, dtype=np.float32) / half)).astype(np.float32)
    row = np.repeat(np.arange(4, dtype=np.float32), 64)
    col = np.tile(np.arange(64, dtype=np.float32), 4)
    ar, ac = row[:, None] * inv, col[:, None] * inv
    c = np.concatenate([np.cos(ar), np.cos(ar), np.cos(ac), np.cos(ac)], 1)
    s = np.concatenate([-np.sin(ar), np.sin(ar), -np.sin(ac), np.sin(ac)], 1)
    parts["ropec"] = c.reshape(2, 128, 64).transpose(1, 0, 2).reshape(128, 128)
    parts["ropes"] = s.reshape(2, 128, 64).transpose(1, 0, 2).reshape(128, 128)
    parts["iota"] = np.broadcast_to(np.arange(8.0), (128, 8))
    parts["slots"] = np.broadcast_to(np.arange(1.0, CAP + 1), (128, CAP))
    at, n = {}, 0
    for k, v in parts.items():
        at[k] = n
        n += v.shape[1]
    table = np.concatenate([np.asarray(v, np.float32) for v in parts.values()], 1)
    d = 255 - np.arange(512)
    exact, f = 16, np.float32
    lg = np.log(np.maximum(d, 1).astype(f) / f(exact)) / f(np.log(128 / exact))
    big = np.minimum(exact + (lg * f(16)).astype(np.int32), 31)
    bucket = np.where(d < exact, np.maximum(d, 0), big)
    hot = np.zeros((33, 512), np.float32)
    hot[bucket[d >= 0], np.nonzero(d >= 0)[0]] = 1.0
    hot[32, d < 0] = 1.0
    return np.ascontiguousarray(table), at, n, hot


def build(nc, t, out, dbg=None):
    vat, nvec = vector_columns()
    rat, nrow = row_columns()
    _, cat_, ncst, _ = constants()
    with ExitStack() as ctx:
        def sb(name, shape, dt=F32):
            return ctx.enter_context(nc.sbuf_tensor(name, shape, dt))

        Q = Queues(nc, ctx)
        wring = sb("wring", [128, NSLOT * SLOT])
        X = sb("X", [128, 2, 1024])
        XN = sb("XN", [128, 2, 1024])
        HT = sb("HT", [128, 8, 256])
        MN = sb("MN", [128, 8, 256])
        PV = sb("PV", [128, nvec])
        RB = sb("RB", [128, nrow])
        CS = sb("CS", [128, ncst])
        SW = sb("SW", [128, 8, 144])
        AR = sb("AR", [128, ARENA])
        SM = sb("SM", [128, 1024])
        banks = [ctx.enter_context(nc.psum_tensor(f"ps{i}", [128, 512], F32)) for i in range(8)]
        scratch = nc.dram_tensor("bias_rows", [8, 128, 512], F32, kind="Internal").ap()

        wsem = [ctx.enter_context(nc.semaphore(f"w{i}")) for i in range(NSLOT)]
        dsems = {}

        def dsem(name):
            if name not in dsems:
                dsems[name] = [ctx.enter_context(nc.semaphore(f"d_{name}")), 0]
            return dsems[name]

        def load(group, dst, src, w=(), k="sp", **kw):
            s = dsem(group)
            s[1] += 16
            return Q.dma(k, dst, src, s[0], s[1], w, **kw)

        def loaded(group):
            s = dsem(group)
            h = Handle(s[0], 16)
            h.value, h.used = s[1], True
            return h

        def pe(fn, w=()):
            return Q.add("pe", fn, w)

        def v(fn, w=()):
            return Q.add("dve", fn, w, chain=True)

        def a(fn, w=()):
            return Q.add("act", fn, w, chain=True)

        def g(fn, w=()):
            return Q.add("pool", fn, w, chain=True)

        def mm(o, l, r, start, stop, w=()):
            return pe(lambda e: e.matmul(o, l, r, start=start, stop=stop), w)

        def tp(o, i, w=(), n=128):
            return pe(lambda e: e.transpose(o, i, IDENT[0:n, 0:n]), w)

        def act(o, i, f, w=(), **kw):
            return a(lambda e: e.activation(o, i, f, **kw), w)

        def ts(o, i, s1, s2, op0, op1=None, w=(), q=v):
            if op1 is None:
                return q(lambda e: e.tensor_scalar(o, i, s1, None, op0), w)
            return q(lambda e: e.tensor_scalar(o, i, s1, s2, op0, op1), w)

        def tt(o, i0, i1, op, w=(), q=v):
            return q(lambda e: e.tensor_tensor(o, i0, i1, op), w)

        def stt(o, i0, s, i1, op0, op1, w=()):
            return v(lambda e: e.scalar_tensor_tensor(o, i0, s, i1, op0, op1), w)

        def cp(o, i, w=(), q=v):
            return q(lambda e: e.tensor_copy(o, i), w)

        def red(o, i, op, w=()):
            return v(lambda e: e.tensor_reduce(o, i, AX.X, op), w)

        def barrier():
            last = list(Q.last.values())
            for k in ("pe", "dve", "act", "pool"):
                if k in Q.last:
                    Q.pending[k] = list(last)

        def edge():
            return list(Q.last.values())

        class Arena:
            n = 0

            def take(self, *shape):
                k = int(np.prod(shape))
                ap = AR[:, self.n:self.n + k]
                self.n += k
                assert self.n <= ARENA, self.n
                if len(shape) == 2:
                    return ap.rearrange("p (a b) -> p a b", a=shape[0])
                if len(shape) == 3:
                    return ap.rearrange("p (a b c) -> p a b c", a=shape[0], b=shape[1])
                return ap

        ar = Arena()
        small = [0]

        def sm(*shape):
            k = int(np.prod(shape))
            if small[0] + k > 1024:
                small[0] = 0
            ap = SM[:, small[0]:small[0] + k]
            small[0] += k
            if len(shape) == 2:
                return ap.rearrange("p (a b) -> p a b", a=shape[0])
            return ap

        def C(name, n, rows=128):
            return CS[0:rows, cat_[name]:cat_[name] + n]

        def bc(ap, n):
            return ap.broadcast_to([ap.shape[0], n])

        IDENT = C("ident", 128)
        ONES = C("ones", 128)

        def vec(name, i):
            return PV[:, vat[name] + i:vat[name] + i + 1]

        PA = Ring([banks[i] for i in range(4)])
        PB = Ring([banks[i] for i in range(4, 8)])
        places = [wring[:, i * SLOT:(i + 1) * SLOT] for i in range(NSLOT)]
        fsem = [ctx.enter_context(nc.semaphore(f"f{i}")) for i in range(NSLOT)]
        turns, freed = [0] * NSLOT, [0] * NSLOT
        stream = {"n": 0, "said": None, "replay": None}

        def fill(parts):
            if stream["replay"] is not None:
                return stream["replay"].pop(0)
            n = stream["n"]
            stream["n"] += 1
            i = n % NSLOT
            busy = [Handle(fsem[i], 1, n // NSLOT)] if n >= NSLOT else []
            for dst, src in parts(places[i]):
                turns[i] += 16
                h = Q.dma("sp", dst, src, wsem[i], turns[i], busy)
            if stream["said"] is not None:
                stream["said"].append((i, places[i], h))
            return i, places[i], h

        def weights(src, kt, n):
            view = lambda place: place[:, 0:kt * n].rearrange("p (k n) -> p k n", k=kt)
            i, place, h = fill(lambda place: [(view(place), src.rearrange("(k p) n -> p k n", p=128))])
            return i, view(place), h

        def done_with(slot, k="pe"):
            Q.free(k, fsem[slot])

        load("c", CS[:, :], t["cst"])
        load("c", PV[:, :], t["vecs"])
        load("c", RB[:, :], t["rows"].broadcast_to([128, nrow]))
        load("x", X[:, :, :], t["x"][0].rearrange("(a p) d -> p a d", p=128))
        load("c2", SW[:, :, 0:16], t["gdn_w_in"][0, :, 4096:4112].rearrange("(k p) n -> p k n", p=128))
        load("c2", SW[:, :, 16:40], t["nsa_w_in"][0, :, 2560:2584].rearrange("(k p) n -> p k n", p=128))
        for l in range(2):
            o = 40 + 52 * l
            load("c2", SW[:, :, o:o + 16], t["w_in_2"][l, :, 2048:2064].rearrange("(k p) n -> p k n", p=128))
            load("c2", SW[:, :, o + 16:o + 20], t["w_router_group_2"][l].rearrange("(k p) n -> p k n", p=128))
            load("c2", SW[:, :, o + 20:o + 52], t["w_router_expert_2"][l].rearrange("(k p) n -> p k n", p=128))
        hc, hc2 = loaded("c"), loaded("c2")
        for k in ("pe", "dve", "act", "pool"):
            Q.pending[k] = [hc, hc2, loaded("x")]

        def probe(name, ap, w):
            if dbg is not None and name in dbg:
                h = load("dbg", dbg[name], ap, w)
                for k in ("pe", "dve", "act", "pool"):
                    Q.pending.setdefault(k, []).append(h)

        def power(x, w, y=None):
            if y is None:
                shape = list(x.shape)[1:]
                y = sm(*shape)
                z = sm(*shape)
            else:
                y, z = y
            v(lambda e: e.reciprocal(x, x), w)
            h = act(y, x, ACT.Sqrt, [Q.last["dve"]])
            v(lambda e: e.reciprocal(z, y), [h])
            stt(z, z, 0.5, x, MUL, MUL)
            return stt(x, y, 0.5, z, MUL, ADD)

        def rstd(src, dst, n, junk, w=()):
            hs = None
            for i in range(2):
                acc = dst[:, i:i + 1]
                hs = act(junk, src[:, i, :], ACT.Square, w, accum_out=acc)
            h = ts(dst, dst, 1.0 / n, 1e-6, MUL, ADD, [hs])
            return power(dst, [h])

        def to_features(src, dst, scale, w=()):
            hs = []
            for k in range(0, 8, 2):
                i, ps, busy = PB.get()
                for j in range(2):
                    for m in range(2):
                        h = tp(ps[:, j * 256 + m * 128:j * 256 + m * 128 + 128],
                               src[:, m, (k + j) * 128:(k + j) * 128 + 128], list(w) + busy)
                e = []
                for j in range(2):
                    o, s = dst[:, k + j, :], ps[:, j * 256:j * 256 + 256]
                    if scale is None:
                        e.append(cp(o, s, [h]) if k % 4 else act(o, s, ACT.Copy, [h]))
                    elif k % 4:
                        e.append(ts(o, s, scale(k + j), None, MUL, w=[h]))
                    else:
                        e.append(act(o, s, ACT.Copy, [h], scale=scale(k + j)))
                PB.put(i, e)
                hs += e
            return hs

        def norm_features(src, dst, scale):
            r = sm(2)
            h = rstd(src, r, 1024, XN[:, 0, :])
            for i in range(2):
                h = ts(XN[:, i, :], src[:, i, :], r[:, i:i + 1], None, MUL)
            return to_features(XN, dst, scale, [h])

        def gemm_f(src_w, kt, rhs, evac, w=(), n=None, cols=None, keep=None):
            n = n or src_w.shape[1]
            slot, wt, landed = keep or weights(src_w, kt, n)
            cols = cols or range(0, n, 128)
            h = None
            for c in range(0, len(cols), 2):
                i, ps, busy = PB.get()
                readers = []
                hh = []
                for j, c0 in enumerate(cols[c:c + 2]):
                    for k in range(kt):
                        h = mm(ps[:, j * 256:j * 256 + 256], wt[:, k, c0:c0 + 128], rhs[:, k, :],
                               k == 0, k == kt - 1, list(w) + busy + [landed])
                    hh.append(h)
                for j, c0 in enumerate(cols[c:c + 2]):
                    readers += evac(c0 // 128, ps[:, j * 256:j * 256 + 256], hh[-1])
                PB.put(i, readers)
            if keep is None:
                done_with(slot)
            return h

        def gemm_t(wt, landed, kt, lhs, n, c0, evac, w=()):
            h = None
            for m in range(2):
                i, ps, busy = PB.get()
                for k in range(kt):
                    h = mm(ps[:, 0:n], lhs[:, k, m * 128:m * 128 + 128], wt[:, k, c0:c0 + n],
                           k == 0, k == kt - 1, list(w) + busy + [landed])
                PB.put(i, evac(m, ps[:, 0:n], h))
            return h

        def down(srcs, lhs, evac, w=()):
            got = [PA.get() for _ in range(4)]
            busy = [b for _, _, bs in got for b in bs]
            total = sum(s[1] for s in srcs)
            kk = 0
            for src, kt in srcs:
                slot, wt, landed = weights(src, kt, 1024)
                for k in range(kt):
                    for m in range(2):
                        for c in range(2):
                            h = mm(got[2 * m + c][1][:, :], lhs[:, kk, m * 128:m * 128 + 128],
                                   wt[:, k, c * 512:c * 512 + 512], kk == 0, kk == total - 1,
                                   list(w) + busy + [landed])
                    kk += 1
                done_with(slot)
            for m in range(2):
                for c in range(2):
                    PA.put(got[2 * m + c][0], evac(m, c, got[2 * m + c][1], h))

        def add_x(m, c, ps, h):
            o = X[:, m, c * 512:c * 512 + 512]
            return [tt(o, ps[:, :], o, ADD, [h])]

        def taps(y, ps, name, base, stride, k, center, w=()):
            wc = lambda j: vec(name, base + stride * j)
            h = ts(y, ps, wc(center), None, MUL, w=w)
            for j in range(k):
                d = j - center
                if d < 0:
                    h = stt(y[:, -d:256], ps[:, 0:256 + d], wc(j), y[:, -d:256], MUL, ADD)
                elif d > 0:
                    h = stt(y[:, 0:256 - d], ps[:, d:256], wc(j), y[:, 0:256 - d], MUL, ADD)
            return h

        def attend(ps_s, hs, scale, bias, gate, dst):
            m, s = sm(2), sm(2)
            view = ps_s[:, :].rearrange("p (a b) -> p a b", a=2)
            if bias is None:
                h = red(m, view, MAX, hs)
                h = ts(m, m, -scale, None, MUL)
                for i in range(2):
                    h2 = act(dst[:, i, :], view[:, i, :], ACT.Exp, [h] + list(hs), bias=m[:, i:i + 1], scale=scale,
                             accum_out=s[:, i:i + 1])
                rd = [h2]
            else:
                h = stt(dst, view, scale, bias, MUL, ADD, hs)
                rd = [h]
                h = red(m, dst, MAX)
                h = ts(m, m, FLOOR, -1.0, MAX, MUL)
                for i in range(2):
                    h2 = act(dst[:, i, :], dst[:, i, :], ACT.Exp, [h], bias=m[:, i:i + 1], accum_out=s[:, i:i + 1])
            h = ts(s, s, 1e-30, None, MAX, w=[h2])
            h = v(lambda e: e.reciprocal(s, s))
            if gate is not None:
                h = tt(s, s, gate, MUL)
            for i in range(2):
                h = ts(dst[:, i, :], dst[:, i, :], s[:, i:i + 1], None, MUL)
            return rd, h

        def turn(src, dst, w, n=256):
            i, ps, busy = PB.get()
            for m in range(2):
                for k in range(2):
                    h = tp(ps[:, k * 256 + m * 128:k * 256 + m * 128 + 128], src[:, m, k * 128:k * 128 + 128],
                           list(w) + busy)
            e = act(dst, ps[:, :].rearrange("p (a b) -> p a b", a=2), ACT.Copy, [h])
            PB.put(i, [e])
            return h, e

        def memory_attention(layer, CAT):
            KT = ar.take(4, 256)
            V = ar.take(2, 512)
            S = [ar.take(2, 256) for _ in range(2)]
            T = [ar.take(2, 256) for _ in range(2)]
            hm = norm_features_mem(layer)
            hk = []

            def ek(c, ps, h):
                r = act(KT[:, c, :], ps, ACT.Copy, [h])
                hk.append(r)
                return [r]

            def ev(m, ps, h):
                r = cp(V[:, m, :], ps, [h])
                hk.append(r)
                return [r]

            gemm_f(t["mem_w_kv"][layer, :, 0:512], 8, MN, ek, hm)
            slot, wt, landed = weights(t["mem_w_kv"][layer, :, 512:1024], 8, 512)
            gemm_t(wt, landed, 8, MN, 512, 0, ev, hm)
            done_with(slot)
            ring = Ring(list(zip(S, T)))
            fin = []
            for h4 in range(4):
                r, (s, tr), rb = ring.get()
                i, ps, busy = PB.get()
                for m in range(2):
                    h = mm(ps[:, m * 256:m * 256 + 256], CAT[:, 8 + h4, m * 128:m * 128 + 128], KT[:, h4, :],
                           True, True, busy + hk)
                    hq = h
                rd, hp = attend(ps, [h] + rb, 128.0 ** -0.5, None, None, s)
                PB.put(i, rd)
                h, e = turn(s, tr, [hp])
                i, ps, busy = PB.get()
                for k in range(2):
                    h = mm(ps[:, 0:256], V[:, k, h4 * 128:h4 * 128 + 128], tr[:, k, :], k == 0, k == 1, busy + [e])
                e = act(CAT[:, 8 + h4, :], ps[:, 0:256], ACT.Copy, [h, hq])
                PB.put(i, [e])
                ring.put(r, [h, hp])
                fin.append(e)
            return fin

        def norm_features_mem(layer):
            h = load("mem", XN[:, :, :], t["mem"][0].rearrange("(a p) d -> p a d", p=128), edge())
            Q.pending["act"] = [h]
            Q.pending["dve"] = [h]
            Q.pending["pe"] = [h]
            r = sm(2)
            rstd(XN, r, 1024, MN[:, 0:4, :].rearrange("p a b -> p (a b)"))
            for i in range(2):
                h = ts(XN[:, i, :], XN[:, i, :], r[:, i:i + 1], None, MUL)
            return to_features(XN, MN, lambda k: vec("mem", 8 * layer + k), [h] + [Q.last["act"]])


        def heads_softplus(dst, src, e1, w=()):
            h = ts(e1, src, -1.0, None, MUL, w=w)
            h = tt(e1, src, e1, MAX)
            h = act(e1, e1, ACT.Exp, [h], scale=-1.0)
            h = act(e1, e1, ACT.Ln, bias=1.0)
            return stt(dst, src, 0.0, e1, MAX, ADD, [h])

        def gdn(CAT):
            QK = ar.take(16, 256)
            VB = ar.take(8, 256)
            hT = norm_features(X, HT, lambda k: vec("mix", k))
            ab = ar.take(2, 16)
            sq = [ar.take(256) for _ in range(2)]
            sqr = Ring(sq)
            done = []

            def ab_out(m, ps, h):
                return [cp(ab[:, m, :], ps, [h])]

            gemm_t(SW[:, :, 0:16], None, 8, HT, 16, 0, ab_out, hT)
            hn = []
            for chunk in range(6):
                def ev(c, ps, h, chunk=chunk):
                    f = chunk * 4 + c
                    y = QK[:, f, :] if f < 16 else VB[:, f - 16, :]
                    hv = taps(y, ps, "gconv", f, 24, 4, 3, [h])
                    hs = act(y, y, ACT.Silu, [hv])
                    hn.append(hs)
                    return [hv]
                gemm_f(t["gdn_w_in"][0, :, chunk * 512:chunk * 512 + 512], 8, HT, ev, hT)
            for chunk in range(2):
                def ev(c, ps, h, chunk=chunk):
                    r = act(CAT[:, chunk * 4 + c, :], ps, ACT.Silu, [h])
                    return [r]
                gemm_f(t["gdn_w_in"][0, :, 3072 + chunk * 512:3584 + chunk * 512], 8, HT, ev, hT)

            def ev(c, ps, h):
                return [cp(CAT[:, 8 + c, :], ps, [h])]
            gemm_f(t["gdn_w_in"][0, :, 4112:4624], 8, HT, ev, hT)
            for f in range(16):
                r, s, rb = sqr.get()
                y = QK[:, f, :]
                h = act(s, y, ACT.Square, rb)
                i, ps, busy = PB.get()
                h = mm(ps[:, 0:256], ONES, s, True, True, busy + [h])
                h = ts(s, ps[:, 0:256], 1e-6, None, ADD, w=[h])
                PB.put(i, [h])
                power(s, [h], (XN[:, 0, (f % 2) * 512:(f % 2) * 512 + 256], XN[:, 0, (f % 2) * 512 + 256:(f % 2) * 512 + 512]))
                if f < 8:
                    h = stt(y, y, 128.0 ** -0.5, s, MUL, MUL)
                else:
                    h = tt(y, y, s, MUL)
                sqr.put(r, [h])
            hqk = h
            beta, gg, e1, gc, egc, tot, kd = (sm(2, 8) for _ in range(7))
            h = act(beta, ab[:, :, 0:8], ACT.Sigmoid, [hqk])
            h = tt(gg, ab[:, :, 8:16], RB[:, rat["dt"]:rat["dt"] + 8].unsqueeze(1).broadcast_to([128, 2, 8]), ADD)
            h = heads_softplus(gg, gg, e1)
            ea = sm(8)
            h = act(ea, RB[:, rat["alog"]:rat["alog"] + 8], ACT.Exp)
            h = stt(gg, gg, -1.0, ea.unsqueeze(1).broadcast_to([128, 2, 8]), MUL, MUL, [h])
            hg = h
            UP = C("up", 128)
            i, ps, busy = PB.get()
            for m in range(2):
                h = mm(ps[:, m * 8:m * 8 + 8], UP, gg[:, m, :], True, True, busy + [hg])
            h = mm(ps[:, 16:24], ONES, gg[:, 0, :], True, True)
            h = cp(gc.rearrange("p a b -> p (a b)"), ps[:, 0:16], [h])
            h = tt(kd[:, 0, :], ps[:, 16:24], gc[:, 0, :], SUB)
            PB.put(i, [h])
            h = act(kd[:, 0, :], kd[:, 0, :], ACT.Exp, [h])
            hke = act(egc, gc, ACT.Exp)
            KD = HT[:, 0:4, :].rearrange("p a b -> p (a b)")
            for hd in range(8):
                i, ps, busy = PB.get()
                for m in range(2):
                    h = tp(ps[:, m * 128:m * 128 + 128], VB[:, hd, m * 128:m * 128 + 128], busy + hn + [hqk])
                h = tp(ps[:, 256:384], QK[:, 8 + hd, 0:128], [hqk])
                for m in range(2):
                    hh = ts(XN[:, m, hd * 128:hd * 128 + 128], ps[:, m * 128:m * 128 + 128], beta[:, m, hd:hd + 1],
                            None, MUL, w=[h])
                hh = ts(KD[:, hd * 128:hd * 128 + 128], ps[:, 256:384], kd[:, 0, hd:hd + 1], None, MUL, w=[hke, h])
                PB.put(i, [hh])
            hvb = hh
            probe("vb", XN[:, :, :], [hvb])
            n0 = ar.n
            ST = HT[:, 4:8, :].rearrange("p a b -> p (a b)")
            D, DT, LT, BT, M1 = ([ar.take(4, 128) for _ in range(2)] for _ in range(5))
            AT = [ar.take(4, 128) for _ in range(2)]
            OT = VB
            hst = None
            hprev = [hvb]
            for m in range(2):
                tok = slice(m * 128, m * 128 + 128)
                hD, hDT, hLT, hAT = [None] * 2, [None] * 2, [None] * 2, [None] * 2
                for b in range(2):
                    i, ps, busy = PB.get()
                    for j in range(4):
                        hd = 4 * b + j
                        h = mm(ps[:, j * 128:j * 128 + 128], bc(gg[:, m, hd:hd + 1], 128), UP, True, True,
                               busy + hprev + [hg])
                    for j in range(4):
                        h2 = ts(M1[b][:, j, :], ps[:, j * 128:j * 128 + 128], gc[:, m, 4 * b + j:4 * b + j + 1], 0.0,
                                SUB, MAX, w=[h] + hprev)
                    PB.put(i, [h2])
                    h2 = act(M1[b], M1[b], ACT.Exp, [h2], scale=-1.0)
                    h2 = tt(M1[b], M1[b], C("incl", 128).unsqueeze(1).broadcast_to([128, 4, 128]), MUL, [h2])
                    i, ps, busy = PB.get()
                    i2, ps2, busy2 = PB.get()
                    for j in range(4):
                        hd = 4 * b + j
                        h = mm(ps[:, j * 128:j * 128 + 128], QK[:, 8 + hd, tok], QK[:, 8 + hd, tok], True, True, busy)
                        h = mm(ps2[:, j * 128:j * 128 + 128], QK[:, hd, tok], QK[:, 8 + hd, tok], True, True, busy2)
                    for j in range(4):
                        hl = stt(D[b][:, j, :], ps[:, j * 128:j * 128 + 128], beta[:, m, 4 * b + j:4 * b + j + 1],
                                 M1[b][:, j, :], MUL, MUL, [h])
                    PB.put(i, [hl])
                    ha = tt(BT[b], ps2[:, :].rearrange("p (a b) -> p a b", a=4), M1[b], MUL)
                    PB.put(i2, [ha])
                    i, ps, busy = PB.get()
                    i2, ps2, busy2 = PB.get()
                    for j in range(4):
                        h = tp(ps[:, j * 128:j * 128 + 128], D[b][:, j, :], busy + [hl, ha])
                        h = tp(ps2[:, j * 128:j * 128 + 128], BT[b][:, j, :], busy2)
                    p3 = ps[:, :].rearrange("p (a b) -> p a b", a=4)
                    hLT[b] = act(LT[b], p3, ACT.Copy, [h])
                    hAT[b] = act(AT[b], ps2[:, :].rearrange("p (a b) -> p a b", a=4), ACT.Copy, [h])
                    PB.put(i, [hLT[b]])
                    PB.put(i2, [hAT[b]])
                    ID4 = IDENT.unsqueeze(1).broadcast_to([128, 4, 128])
                    LEV = lambda s: CS[:, cat_["levT"] + 128 * s:cat_["levT"] + 128 * s + 128].unsqueeze(1)\
                        .broadcast_to([128, 4, 128])
                    h2 = tt(D[b], D[b], C("lev1", 128).unsqueeze(1).broadcast_to([128, 4, 128]), MUL, [h])
                    hD[b] = tt(D[b], ID4, D[b], SUB)
                    h2 = tt(DT[b], LT[b], LEV(0), MUL, [hLT[b]])
                    hDT[b] = tt(DT[b], ID4, DT[b], SUB)
                for s in range(1, 7):
                    for b in range(2):
                        hb = tt(BT[b], LT[b], LEV(s), MUL, [hLT[b]])
                        i, ps, busy = PB.get()
                        for j in range(4):
                            h = mm(ps[:, j * 128:j * 128 + 128], BT[b][:, j, :], D[b][:, j, :], True, True,
                                   busy + [hb, hD[b]])
                        hm = act(M1[b], ps[:, :].rearrange("p (a b) -> p a b", a=4), ACT.Copy, [h])
                        PB.put(i, [hm])
                        i, ps, busy = PB.get()
                        for j in range(4):
                            h = mm(ps[:, j * 128:j * 128 + 128], M1[b][:, j, :], DT[b][:, j, :], True, True,
                                   busy + [hm, hDT[b]])
                        if s < 6:
                            i2, ps2, busy2 = PB.get()
                            for j in range(4):
                                h = mm(ps2[:, j * 128:j * 128 + 128], DT[b][:, j, :], M1[b][:, j, :], True, True,
                                       busy2)
                        hDT[b] = tt(DT[b], DT[b], ps[:, :].rearrange("p (a b) -> p a b", a=4), SUB, [h])
                        PB.put(i, [hDT[b]])
                        if s < 6:
                            hD[b] = tt(D[b], D[b], ps2[:, :].rearrange("p (a b) -> p a b", a=4), SUB)
                            PB.put(i2, [hD[b]])
                for b in range(2):
                    o0, r0 = D[b], BT[b]
                    hr = [None] * 4
                    if m == 1:
                        i, ps, busy = PB.get()
                        i2, ps2, busy2 = PB.get()
                        for j in range(4):
                            hd = 4 * b + j
                            S = ST[:, hd * 128:hd * 128 + 128]
                            h = mm(ps[:, j * 128:j * 128 + 128], QK[:, 8 + hd, tok], S, True, True, busy + [hst])
                            h = mm(ps2[:, j * 128:j * 128 + 128], QK[:, hd, tok], S, True, True, busy2)
                        for j in range(4):
                            hd = 4 * b + j
                            e = egc[:, 1, hd:hd + 1]
                            h2 = ts(r0[:, j, :], ps[:, j * 128:j * 128 + 128], e, beta[:, 1, hd:hd + 1], MUL, MUL,
                                    w=[h])
                            h2 = tt(r0[:, j, :], XN[:, 1, hd * 128:hd * 128 + 128], r0[:, j, :], SUB)
                            h2 = ts(o0[:, j, :], ps2[:, j * 128:j * 128 + 128], e, None, MUL)
                        PB.put(i, [h2])
                        PB.put(i2, [h2])
                    i, ps, busy = PB.get()
                    for j in range(4):
                        hd = 4 * b + j
                        rhs = r0[:, j, :] if m else XN[:, 0, hd * 128:hd * 128 + 128]
                        h = mm(ps[:, j * 128:j * 128 + 128], DT[b][:, j, :], rhs, True, True,
                               busy + [hDT[b], h2, hvb])
                    hv = act(M1[b], ps[:, :].rearrange("p (a b) -> p a b", a=4), ACT.Copy, [h])
                    PB.put(i, [hv])
                    if m == 0:
                        i, ps, busy = PB.get()
                        for j in range(4):
                            hd = 4 * b + j
                            h = mm(ps[:, j * 128:j * 128 + 128], KD[:, hd * 128:hd * 128 + 128], M1[b][:, j, :],
                                   True, True, busy + [hv, hvb])
                        hst = cp(ST[:, b * 512:b * 512 + 512], ps[:, :], [h])
                        PB.put(i, [hst])
                    i, ps, busy = PB.get()
                    for j in range(4):
                        h = mm(ps[:, j * 128:j * 128 + 128], AT[b][:, j, :], M1[b][:, j, :], True, True,
                               busy + [hv, hAT[b]])
                    p3 = ps[:, :].rearrange("p (a b) -> p a b", a=4)
                    if m:
                        h2 = tt(o0, p3, o0, ADD, [h])
                    else:
                        h2 = cp(o0, p3, [h])
                    PB.put(i, [h2])
                    rs = sm(4)
                    for j in range(4):
                        h3 = act(r0[:, j, :], o0[:, j, :], ACT.Square, [h2], accum_out=rs[:, j:j + 1])
                    h2 = ts(rs, rs, 1.0 / 128, 1e-6, MUL, ADD, w=[h3])
                    h2 = power(rs, [h2])
                    for j in range(4):
                        h2 = ts(o0[:, j, :], o0[:, j, :], rs[:, j:j + 1], None, MUL)
                    i, ps, busy = PB.get()
                    for j in range(4):
                        h = tp(ps[:, j * 128:j * 128 + 128], o0[:, j, :], busy + [h2])
                    for j in range(4):
                        c = CAT[:, 4 * b + j, tok]
                        h2 = stt(c, ps[:, j * 128:j * 128 + 128], vec("gnorm", 0), c, MUL, MUL, [h])
                    PB.put(i, [h2])
                hprev = edge()
            return edge()

        def conv_glu(layer):
            ar.n = 0
            barrier()
            G = ar.take(22, 256)
            hT = norm_features(X, HT, lambda k: vec("ffn", 8 * layer + k))
            up = t["ffn_w_up"][layer]
            for val in range(2):
                for chunk in range(6):
                    n = 512 if chunk < 5 else 256

                    def ev(c, ps, h, chunk=chunk, val=val):
                        f = chunk * 4 + c
                        y = G[:, f, :]
                        if val:
                            return [tt(y, ps, y, MUL, [h] + hG)]
                        hv = taps(y, ps, "fconv", 66 * layer + f, 22, 3, 2, [h])
                        act(y, y, ACT.Silu, [hv], bias=vec("fconvb", 22 * layer + f))
                        return [hv]
                    hG = edge()
                    gemm_f(up[:, val * 2816 + chunk * 512:val * 2816 + chunk * 512 + n], 8, HT, ev, hT)
            dn = t["ffn_w_down"][layer]
            down([(dn[c * 512:min(c * 512 + 512, 2816)], 4 if c < 5 else 2) for c in range(6)], G, add_x, edge())

        def project_out(src, layer, CAT, kt, evac=add_x):
            down([(src[c * 512:c * 512 + 512], 4) for c in range(kt // 4)], CAT, evac, edge())

        def nsa(CAT):
            ar.n = 12 * 256
            KC = ar.take(4, 256)
            KS = ar.take(4, 256)
            VS = ar.take(2, 512)
            GT = ar.take(2, 24)
            BI = ar.take(8, 512)
            n0 = ar.n
            hT = norm_features(X, HT, lambda k: vec("mix", 8 + k))
            tab, hot = ar.take(8), ar.take(512)
            rep = Ring([ar.take(512) for _ in range(2)])
            load("tab", tab[0:33, :], t["tab"], edge())
            load("tab", hot[0:33, :], t["hot"], edge())
            htab = loaded("tab")
            for hd in range(8):
                r, row, rb = rep.get()
                i, ps, busy = PB.get()
                h = mm(ps[:, :], bc(tab[0:33, hd:hd + 1], 128), hot[0:33, :], True, True, busy + [htab])
                h = cp(row, ps[:, :], [h] + rb)
                PB.put(i, [h])
                h = load(f"row{hd}", scratch[hd], row, [h])
                rep.put(r, [h])
                src = scratch[hd]
                for m in range(2):
                    ap = bass.AP(src.tensor, src.offset + 255 - 128 * m, [[511, 128], [1, 256]])
                    load("bias", BI[:, hd, m * 256:m * 256 + 256], ap, [h])
            hb = loaded("bias")
            hr = []

            def keep(dst):
                def ev(c, ps, h):
                    r = act(dst(c), ps, ACT.Copy, [h])
                    hr.append(r)
                    return [r]
                return ev
            win = t["nsa_w_in"][0]
            for ch in range(2):
                gemm_f(win[:, ch * 512:ch * 512 + 512], 8, HT, keep(lambda c: CAT[:, 4 * ch + c, :]), hT)
            gemm_f(win[:, 1024:1536], 8, HT, keep(lambda c: KC[:, c, :]), hT)
            for ch in range(2):
                slot, wt, landed = weights(win[:, 1536 + 512 * ch:2048 + 512 * ch], 8, 512)
                gemm_f(None, 8, HT, keep(lambda c: KS[:, 2 * ch + c, :]), hT, n=512, cols=[0, 128],
                       keep=(slot, wt, landed))

                def ev(m, ps, h):
                    r = cp(VS[:, m, ch * 256:ch * 256 + 256], ps, [h])
                    hr.append(r)
                    return [r]
                gemm_t(wt, landed, 8, HT, 256, 256, ev, hT)
                done_with(slot)

            def ev(m, ps, h):
                r = act(GT[:, m, :], ps, ACT.Sigmoid, [h])
                hr.append(r)
                return [r]
            gemm_t(SW[:, :, 16:40], None, 8, HT, 24, 0, ev, hT)
            gemm_f(win[:, 2584:3096], 8, HT, keep(lambda c: CAT[:, 8 + c, :]), hT)
            ar.n = n0
            barrier()
            BL = ar.take(32, 32)
            HID = ar.take(32)
            KCT, VC = ar.take(32), ar.take(2, 128)
            for kv in range(2):
                for gr in range(2):
                    src = KC[:, 2 * kv + gr, :]
                    s = bass.AP(src.tensor, src.offset, [list(src.ap[0]), [1, 32], [16, 15]])
                    p = PV[:, vat["posk"] + 32 * kv:vat["posk"] + 32 * kv + 32].unsqueeze(2).broadcast_to([128, 32, 15])
                    h = tt(BL[:, :, gr * 16:gr * 16 + 15], s, p, ADD, [Q.last["pe"], Q.last["act"]])
                h = v(lambda e: e.memset(BL[:, :, 15:32:16], 0.0))
                hbl = h
                i, ps, busy = PB.get()
                w1 = t["nsa_cmp_w1_v" if kv else "nsa_cmp_w1_k"][0]
                slot, wt, landed = weights(w1, 32, 128)
                for l in range(32):
                    h = mm(ps[:, 0:32], wt[:, l, :], BL[:, l, :], l == 0, l == 31, busy + [landed, hbl])
                done_with(slot)
                h = act(HID, ps[:, 0:32], ACT.Silu, [h])
                PB.put(i, [h])
                slot, wt, landed = weights(t["nsa_cmp_w2_v" if kv else "nsa_cmp_w2_k"][0], 1, 128)
                i, ps, busy = PB.get()
                if kv == 0:
                    h = mm(ps[:, 0:32], wt[:, 0, :], HID, True, True, busy + [landed, h])
                    e = cp(KCT, ps[:, 0:32], [h])
                else:
                    for gr in range(2):
                        h = mm(ps[0:15, gr * 128:gr * 128 + 128], HID[:, gr * 16:gr * 16 + 15], wt[:, 0, :], True, True,
                               busy + [landed, h])
                    e = cp(VC[0:15, :, :], ps[0:15, 0:256].rearrange("p (a b) -> p a b", a=2), [h])
                PB.put(i, [e])
                done_with(slot)
            probe("kct", KCT, [e])
            hcmp = e
            bufs = Ring([[ar.take(2, 256), ar.take(2, 256), ar.take(2, 256), ar.take(2, 256)] for _ in range(2)])
            SC = Ring([[ar.take(2, 16), ar.take(256)] for _ in range(2)])
            scale = 128.0 ** -0.5
            for hd in range(8):
                gr = hd // 4
                r, bf, rb = bufs.get()
                bias = BI[:, hd, :].rearrange("p (a b) -> p a b", a=2)
                trs = []
                for br in range(2):
                    i, ps, busy = PB.get()
                    for m in range(2):
                        h = mm(ps[:, m * 256:m * 256 + 256], CAT[:, hd, m * 128:m * 128 + 128], KS[:, 2 * br + gr, :],
                               True, True, busy + hr)
                    rd, hp = attend(ps, [h, hb] + rb, scale, bias, GT[:, :, 3 * hd + 1 + br], bf[br])
                    PB.put(i, rd)
                    h, e = turn(bf[br], bf[2 + br], [hp] + rb)
                    trs.append(e)
                r2, (sc, pt), rb2 = SC.get()
                i, ps, busy = PB.get()
                for m in range(2):
                    hqq = mm(ps[:, m * 16:m * 16 + 15], CAT[:, hd, m * 128:m * 128 + 128],
                             KCT[:, gr * 16:gr * 16 + 15], True, True, busy + [hcmp])
                mx, s = sm(2), sm(2)
                sc15 = sc[:, :, 0:15]
                h = stt(sc15, ps[:, 0:32].rearrange("p (a b) -> p a b", a=2)[:, :, 0:15], scale, bias[:, :, 31:256:16],
                        MUL, ADD, [hqq] + rb2)
                PB.put(i, [h])
                h = red(mx, sc15, MAX)
                h = ts(mx, mx, FLOOR, -1.0, MAX, MUL)
                for m in range(2):
                    h = act(sc15[:, m, :], sc15[:, m, :], ACT.Exp, [h], bias=mx[:, m:m + 1], accum_out=s[:, m:m + 1])
                h = ts(s, s, 1e-30, None, MAX, w=[h])
                h = v(lambda e, s=s: e.reciprocal(s, s))
                h = tt(s, s, GT[:, :, 3 * hd], MUL)
                for m in range(2):
                    h = ts(sc15[:, m, :], sc15[:, m, :], s[:, m:m + 1], None, MUL)
                i, ps, busy = PB.get()
                for m in range(2):
                    h = tp(ps[0:15, m * 128:m * 128 + 128], sc15[:, m, :], busy + [h])
                e = act(pt[0:15, :], ps[0:15, 0:256], ACT.Copy, [h] + rb2)
                PB.put(i, [e])
                i, ps, busy = PB.get()
                mm(ps[:, 0:256], VC[0:15, gr, :], pt[0:15, :], True, False, busy + [e])
                for br in range(2):
                    for k in range(2):
                        h = mm(ps[:, 0:256], VS[:, k, br * 256 + gr * 128:br * 256 + gr * 128 + 128],
                               bf[2 + br][:, k, :], False, br == 1 and k == 1, trs)
                e = cp(CAT[:, hd, :], ps[:, 0:256], [h])
                PB.put(i, [e])
                bufs.put(r, [h, e])
                SC.put(r2, [h, e])

        def modulation(layer, MOD):
            hb = load("ada", MOD, t["b_ada_2"][layer:layer + 1, :].broadcast_to([128, 6144]), edge())
            cc = sm(8)
            hc_ = act(cc, PV[:, vat["c"]:vat["c"] + 8], ACT.Silu)
            for ch in range(12):
                slot, wt, landed = weights(t["w_ada_2"][layer, :, ch * 512:ch * 512 + 512], 8, 512)
                i, ps, busy = PB.get()
                for k in range(8):
                    h = mm(ps[:, :], bc(cc[:, k:k + 1], 128), wt[:, k, :], k == 0, k == 7, busy + [landed, hc_])
                done_with(slot)
                m = MOD[:, ch * 512:ch * 512 + 512]
                h = tt(m, ps[:, :], m, ADD, [h, hb])
                PB.put(i, [h])
            for i, name in ((1, "norm1_g_2"), (4, "norm2_g_2")):
                hl = load("ng", XN[:, 0, :], t[name][layer:layer + 1, :].broadcast_to([128, 1024]), edge())
                m = MOD[:, i * 1024:i * 1024 + 1024]
                stt(m, m, 1.0, XN[:, 0, :], ADD, MUL, [hl])

        def modulated(MOD, which):
            r = sm(2)
            rstd(X, r, 1024, XN[:, 0, :])
            for i in range(2):
                h = stt(XN[:, i, :], X[:, i, :], r[:, i:i + 1], MOD[:, (3 * which + 1) * 1024:(3 * which + 2) * 1024],
                        MUL, MUL)
                h = tt(XN[:, i, :], XN[:, i, :], MOD[:, 3 * which * 1024:(3 * which + 1) * 1024], ADD)
            return to_features(XN, HT, None, [h])

        def gated_add(MOD, which):
            def ev(m, c, ps, h):
                gt = MOD[:, (3 * which + 2) * 1024 + c * 512:(3 * which + 2) * 1024 + c * 512 + 512]
                j = XN[:, m, c * 512:c * 512 + 512]
                o = X[:, m, c * 512:c * 512 + 512]
                h1 = tt(j, ps[:, :], gt, MUL, [h])
                tt(o, o, j, ADD)
                return [h1]
            return ev

        def mixers(layer, MOD):
            n0 = ar.n
            hT = modulated(MOD, 0)
            YM, YA = ar.take(4, 256), ar.take(4, 256)
            n1 = ar.n
            MQK = ar.take(8, 256)
            MV = ar.take(2, 512)
            LG = ar.take(2, 16)
            AQ = ar.take(2, 768)
            BV = AR[:, ar.n:ar.n + 1280]
            win = t["w_in_2"][layer]
            hb = load("bv", BV[:, 0:512], t["b_in_2"][layer:layer + 1, 1024:1536].broadcast_to([128, 512]), edge())
            load("bv", BV[:, 512:1280], t["b_in_2"][layer:layer + 1, 2064:2832].broadcast_to([128, 768]), edge())
            hb = loaded("bv")

            def ev(m, ps, h):
                return [tt(LG[:, m, :], ps, RB[:, rat["bgate"] + 16 * layer:rat["bgate"] + 16 * layer + 16], ADD, [h])]
            o = 40 + 52 * layer
            gemm_t(SW[:, :, o:o + 16], None, 8, HT, 16, 0, ev, hT)
            RAW = [XN[:, 0, j * 256:j * 256 + 256] for j in range(4)]
            rr = Ring(RAW)
            hx = list(hT)
            for ch in range(2):
                def ev(c, ps, h):
                    f = 4 * ch + c
                    i, raw, rb = rr.get()
                    h1 = act(raw, ps, ACT.Identity, [h] + rb + hx, bias=vec("bqk", 8 * layer + f))
                    hv = taps(MQK[:, f, :], raw, "mconv", 40 * layer + f, 8, 5, 2, [h1])
                    rr.put(i, [hv])
                    act(MQK[:, f, :], MQK[:, f, :], ACT.Silu, [hv], bias=vec("mconvb", 8 * layer + f))
                    return [h1]
                gemm_f(win[:, ch * 512:ch * 512 + 512], 8, HT, ev, hT)
            for c0, dst, n, b0 in ((1024, MV, 512, 0), (2064, AQ, 512, 512), (2576, AQ, 256, 1024)):
                slot, wt, landed = weights(win[:, c0:c0 + n], 8, n)

                def ev(m, ps, h):
                    d = dst[:, m, 512:768] if n == 256 else dst[:, m, 0:512]
                    return [tt(d, ps, BV[:, b0:b0 + n], ADD, [h, hb])]
                gemm_t(wt, landed, 8, HT, n, 0, ev, hT)
                done_with(slot)

            def ev(c, ps, h):
                return [act(YM[:, c, :], ps, ACT.Sigmoid, [h], bias=vec("bo", 4 * layer + c))]
            gemm_f(win[:, 1536:2048], 8, HT, ev, hT)
            barrier()
            probe(f"mqk{layer}", MQK, edge())
            probe(f"aq{layer}", AQ, edge())
            n2 = ar.n
            lf, e1, b_, bb = sm(2, 8), sm(2, 8), sm(2, 4), sm(2, 4)
            LG2 = LG.rearrange("p a (b c) -> p a b c", b=4)
            lf4 = lf.rearrange("p a (b c) -> p a b c", b=2)
            neg = sm(2, 8)
            neg4 = neg.rearrange("p a (b c) -> p a b c", b=2)
            h = ts(neg4, LG2[:, :, 1:4:2, :], -1.0, None, MUL)
            heads_softplus(neg, neg, e1)
            i, ps, busy = PB.get()
            hn = Q.last["dve"]
            for m in range(2):
                for d in range(2):
                    U = C("down" if d else "up", 512)
                    for k in range(2):
                        h = mm(ps[:, m * 8 + d * 4:m * 8 + d * 4 + 4], U[:, k * 256 + m * 128:k * 256 + m * 128 + 128],
                               neg[:, k, 4 * d:4 * d + 4], k == 0, k == 1, busy + [hn])
            nb = sm(2, 8)
            h = cp(nb.rearrange("p a b -> p (a b)"), ps[:, 0:16], [h])
            PB.put(i, [h])
            cb = sm(2, 8)
            h = tt(cb.rearrange("p a (b c) -> p a b c", b=2), LG2[:, :, 0:3:2, :], nb.rearrange("p a (b c) -> p a b c", b=2),
                   ADD)
            hcb = h
            E = Ring([[ar.take(2, 256), ar.take(2, 256), ar.take(2, 256)] for _ in range(2)])
            hmx = []
            for hd in range(4):
                r, (dwf, dwb, st), rb = E.get()
                i, pq, busy = PB.get()
                for m in range(2):
                    hq = mm(pq[:, m * 256:m * 256 + 256], MQK[:, hd, m * 128:m * 128 + 128], MQK[:, 4 + hd, :],
                            True, True, busy)
                dens = sm(2, 2)
                nm = sm(2, 2)
                for d in range(2):
                    dw = (dwf, dwb)[d]
                    i2, ps, busy2 = PB.get()
                    for k in range(2):
                        h = mm(ps[:, 0:256], bc(cb[:, k, 4 * d + hd:4 * d + hd + 1], 128),
                               C("id2", 512)[:, k * 256:k * 256 + 256], k == 0, k == 1, busy2 + [hcb])
                    mask = C("mbwd" if d else "mfwd", 512).rearrange("p (a b) -> p a b", a=2)
                    h = tt(dw, mask, ps[:, 0:256].unsqueeze(1).broadcast_to([128, 2, 256]), ADD, [h] + rb)
                    PB.put(i2, [h])
                    mm_ = nm[:, d, :]
                    h = red(mm_, dw, MAX)
                    h = ts(mm_, mm_, 0.0, -1.0, MAX, MUL)
                    for m in range(2):
                        h1 = act(dw[:, m, :], dw[:, m, :], ACT.Exp, [h], bias=mm_[:, m:m + 1])
                    for m in range(2):
                        h = v(lambda e, dw=dw, m=m, d=d, pq=pq, dens=dens: e.tensor_tensor_reduce(
                            dw[:, m, :], pq[:, m * 256:m * 256 + 256], dw[:, m, :], 128.0 ** -0.5, 0.0, MUL, ADD,
                            dens[:, d, m:m + 1]), [h1, hq])
                PB.put(i, [h])
                em = sm(2, 2)
                h = tt(em, nm, nb.rearrange("p a (b c) -> p b c a", b=2)[:, :, hd, :], ADD)
                h1 = act(em, em, ACT.Exp, [h])
                h = stt(em, dens, -1.0, em, MUL, MAX, [h1])
                h = tt(dens, dens, em, MAX)
                h = v(lambda e, dens=dens: e.reciprocal(dens, dens))
                for m in range(2):
                    h = ts(dwf[:, m, :], dwf[:, m, :], dens[:, 0, m:m + 1], None, MUL)
                    h = stt(dwf[:, m, :], dwb[:, m, :], dens[:, 1, m:m + 1], dwf[:, m, :], MUL, ADD)
                h, e = turn(dwf, dwb, [h])
                i, ps, busy = PB.get()
                for m in range(2):
                    for k in range(2):
                        h = mm(ps[:, m * 128:m * 128 + 128], dwb[:, k, m * 128:m * 128 + 128],
                               MV[:, k, hd * 128:hd * 128 + 128], k == 0, k == 1, busy + [e])
                rs = sm(2)
                s3 = st[:, :, 0:128]
                p3 = ps[:, 0:256].rearrange("p (a b) -> p a b", a=2)
                for m in range(2):
                    h1 = act(s3[:, m, :], p3[:, m, :], ACT.Square, [h] + rb, accum_out=rs[:, m:m + 1])
                h = ts(rs, rs, 1.0 / 128, 1e-6, MUL, ADD, w=[h1])
                h = power(rs, [h])
                for m in range(2):
                    h = ts(s3[:, m, :], p3[:, m, :], rs[:, m:m + 1], None, MUL)
                PB.put(i, [h])
                i, ps, busy = PB.get()
                for m in range(2):
                    h = tp(ps[:, m * 128:m * 128 + 128], s3[:, m, :], busy + [h])
                E.put(r, [h])
                h = stt(YM[:, hd, :], ps[:, 0:256], vec("mnorm", 4 * layer + hd), YM[:, hd, :], MUL, MUL, [h])
                PB.put(i, [h])
            probe(f"ym{layer}", YM, edge())
            ar.n = n1
            ar.n = n2
            barrier()
            sqb = AR[:, n1:n1 + 640]
            rs = sm(2, 10)
            for m in range(2):
                h = tt(sqb, AQ[:, m, 0:640], AQ[:, m, 0:640], MUL)
                h = red(rs[:, m, :], sqb.rearrange("p (h d) -> p h d", d=64), ADD)
            h = ts(rs, rs, 1.0 / 64, 1e-6, MUL, ADD)
            h = power(rs, [h])
            QR = ar.take(2, 640)
            T2 = AR[:, n1:n1 + 640]
            for m in range(2):
                x3 = AQ[:, m, 0:640].rearrange("p (h d) -> p h d", d=64)
                h = tt(x3, x3, rs[:, m, :].unsqueeze(2).broadcast_to([128, 10, 64]), MUL)
                for nme, h0, h1 in (("qg", 0, 8), ("kg", 8, 10)):
                    gn = RB[:, rat[nme] + 64 * layer:rat[nme] + 64 * layer + 64].unsqueeze(1)\
                        .broadcast_to([128, h1 - h0, 64])
                    h = tt(x3[:, h0:h1, :], x3[:, h0:h1, :], gn, MUL)
                cos = CS[:, cat_["ropec"] + 64 * m:cat_["ropec"] + 64 * m + 64]
                sin = CS[:, cat_["ropes"] + 64 * m:cat_["ropes"] + 64 * m + 64]
                x4 = AQ[:, m, 0:640].rearrange("p (h u d) -> p h u d", u=4, d=16)
                t4 = T2.rearrange("p (h u d) -> p h u d", u=4, d=16)
                s4 = sin.rearrange("p (u d) -> p u d", u=4)
                for u in range(4):
                    h = tt(t4[:, :, u, :], x4[:, :, u ^ 1, :], s4[:, u, :].unsqueeze(1).broadcast_to([128, 10, 16]), MUL)
                o3 = QR[:, m, :].rearrange("p (h d) -> p h d", d=64)
                h = tt(o3, x3, cos.unsqueeze(1).broadcast_to([128, 10, 64]), MUL)
                h = tt(QR[:, m, :], QR[:, m, :], T2, ADD)
            QT = AR[:, n1:n1 + 1280].rearrange("p (a b) -> p a b", a=5)
            PR = AR[:, n1 + 1280:n1 + 1536].rearrange("p (a b) -> p a b", a=2)
            hq = []
            for pr in range(5):
                i, ps, busy = PB.get()
                if pr < 4:
                    for m in range(2):
                        q3 = QR[:, m, 0:512].rearrange("p (u h d) -> p h u d", u=2, d=64)
                        h = cp(PR[:, m, :].rearrange("p (u d) -> p u d", u=2), q3[:, pr, :, :], hq[-1:] + [Q.last["pe"]])
                    for m in range(2):
                        h = tp(ps[:, m * 128:m * 128 + 128], PR[:, m, :], busy + [h])
                else:
                    for m in range(2):
                        h = tp(ps[:, m * 128:m * 128 + 128], QR[:, m, 512:640], busy)
                e = act(QT[:, pr, :], ps[:, 0:256], ACT.Copy, [h])
                PB.put(i, [e])
                hq.append(e)
            hq.append(h)
            E = Ring([[ar.take(2, 256), ar.take(2, 256)] for _ in range(2)])
            for hd in range(8):
                pr, u = hd % 4, hd // 4
                p0 = slice(64 * u, 64 * u + 64)
                r, (s, tr), rb = E.get()
                i, ps, busy = PB.get()
                for m in range(2):
                    h = mm(ps[:, m * 256:m * 256 + 256], QT[p0, pr, m * 128:m * 128 + 128], QT[p0, 4, :], True, True,
                           busy + hq)
                rd, hp = attend(ps, [h] + rb, 64.0 ** -0.5, None, None, s)
                PB.put(i, rd)
                h, e = turn(s, tr, [hp] + rb)
                i, ps, busy = PB.get()
                for k in range(2):
                    h = mm(ps[p0, 0:256], AQ[:, k, 640 + 64 * u:704 + 64 * u], tr[:, k, :], k == 0, k == 1, busy + [e])
                e = cp(YA[p0, pr, :], ps[p0, 0:256], [h])
                PB.put(i, [e])
                E.put(r, [h, e])
            probe(f"ya{layer}", YA, edge())
            barrier()
            ar.n = n1
            MG = ar.take(8, 256)
            SG = Ring([ar.take(2, 256) for _ in range(2)])
            wb = []
            for half in range(2):
                cs = slice(half * 512, half * 512 + 512)
                gmw = weights(win[:, 2832 + half * 512:3344 + half * 512], 8, 512)
                gaw = weights(win[:, 3856 + half * 512:4368 + half * 512], 8, 512)
                srcm = t["w_branch_m_2"][layer, :, cs].rearrange("(k p) n -> p k n", p=128)
                srca = t["w_branch_a_2"][layer, :, cs].rearrange("(u k p) n -> u p k n", u=2, p=64)
                half_slot = lambda place, j: place[:, 2048 * j:2048 * j + 2048].rearrange("p (k n) -> p k n", k=4)
                i3, place, hbr = fill(lambda place: [(half_slot(place, 0), srcm), (half_slot(place, 1)[0:64], srca[0]),
                                                     (half_slot(place, 1)[64:128], srca[1])])
                wm, wa = half_slot(place, 0), half_slot(place, 1)
                for c in range(4):
                    f = 4 * half + c
                    r, sg, rb = SG.get()
                    i, ps, busy = PB.get()
                    i2, ps2, busy2 = PB.get()
                    for j, (sl, wt, landed) in enumerate((gmw, gaw)):
                        for k in range(8):
                            h = mm(ps[:, j * 256:j * 256 + 256], wt[:, k, c * 128:c * 128 + 128], HT[:, k, :],
                                   k == 0, k == 7, busy + [landed])
                    for j, (wt, y) in enumerate(((wm, YM), (wa, YA))):
                        for k in range(4):
                            h2 = mm(ps2[:, j * 256:j * 256 + 256], wt[:, k, c * 128:c * 128 + 128], y[:, k, :],
                                    k == 0, k == 3, busy2 + [hbr])
                    for j in range(2):
                        e = act(sg[:, j, :], ps[:, j * 256:j * 256 + 256], ACT.Sigmoid, [h] + rb,
                                bias=vec("bga" if j else "bgm", 8 * layer + f))
                    PB.put(i, [e])
                    e = tt(sg, ps2[:, :].rearrange("p (a b) -> p a b", a=2), sg, MUL, [h2, e])
                    PB.put(i2, [e])
                    e = tt(MG[:, f, :], sg[:, 0, :], sg[:, 1, :], ADD)
                    SG.put(r, [e])
                done_with(gmw[0])
                done_with(gaw[0])
                done_with(i3)
            project_out(t["w_out_2"][layer], layer, MG, 8, gated_add(MOD, 0))

        def moe(layer, MOD):
            hT = modulated(MOD, 1)
            o = 56 + 52 * layer
            LGT = ar.take(2, 40)
            CB = ar.take(2, 32)

            def ev(m, ps, h):
                h1 = tt(LGT[:, m, 0:4], ps[:, 0:4], RB[:, rat["brg"] + 4 * layer:rat["brg"] + 4 * layer + 4], ADD, [h])
                h1 = tt(LGT[:, m, 8:40], ps[:, 4:36], RB[:, rat["bre"] + 32 * layer:rat["bre"] + 32 * layer + 32], ADD)
                return [h1]
            gemm_t(SW[:, :, o:o + 36], None, 8, HT, 36, 0, ev, hT)
            probe(f"lgt{layer}", LGT, edge())
            v(lambda e: e.memset(LGT[:, :, 4:8], NEG))
            IO = C("iota", 8)
            for m in range(2):
                mx, s, pg, top, ix, ixf, gm = sm(1), sm(1), sm(8), sm(8), sm(8), sm(8), sm(8)
                el, w1, one, sel = sm(8), sm(2), sm(8), sm(4, 8)
                ixu = ix.bitcast(U32)
                red(mx, LGT[:, m, 0:8], MAX)
                h = ts(mx, mx, -1.0, None, MUL)
                h = act(pg, LGT[:, m, 0:8], ACT.Exp, [h], bias=mx, accum_out=s)
                v(lambda e, s=s: e.reciprocal(s, s), [h])
                ts(pg, pg, s, None, MUL)
                v(lambda e, pg=pg: e.memset(pg[:, 4:8], -1.0))
                v(lambda e, top=top, pg=pg: e.max(top, pg))
                v(lambda e, top=top, pg=pg, ixu=ixu: e.max_index(ixu, top, pg))
                cp(ixf, ixu)
                ptop = sm(1)
                cp(ptop, top[:, 0:1])
                ts(gm, IO, ixf[:, 0:1], None, ALU.is_equal)
                e3 = LGT[:, m, 8:40].rearrange("p (a b) -> p a b", a=4)
                tt(sel, e3, gm[:, 0:4].unsqueeze(2).broadcast_to([128, 4, 8]), MUL)
                tt(sel[:, 0:2, :], sel[:, 0:2, :], sel[:, 2:4, :], ADD)
                tt(el, sel[:, 0, :], sel[:, 1, :], ADD)
                red(mx, el, MAX)
                h = ts(mx, mx, -1.0, None, MUL)
                h = act(el, el, ACT.Exp, [h], bias=mx, accum_out=s)
                v(lambda e, s=s: e.reciprocal(s, s), [h])
                ts(el, el, s, None, MUL)
                v(lambda e, top=top, el=el: e.max(top, el))
                v(lambda e, top=top, el=el, ixu=ixu: e.max_index(ixu, top, el))
                cp(ixf, ixu)
                tt(s, top[:, 0:1], top[:, 1:2], ADD)
                v(lambda e, s=s: e.reciprocal(s, s))
                tt(s, s, ptop, MUL)
                ts(w1, top[:, 0:2], s, None, MUL)
                ts(one, IO, ixf[:, 0:1], w1[:, 0:1], ALU.is_equal, MUL)
                ts(el, IO, ixf[:, 1:2], w1[:, 1:2], ALU.is_equal, MUL)
                tt(one, one, el, ADD)
                for gr in range(4):
                    h = ts(CB[:, m, gr * 8:gr * 8 + 8], one, gm[:, gr:gr + 1], None, MUL)
            hcb = h
            probe(f"cb{layer}", CB, [h])
            MK, RK = ar.take(2, 32), ar.take(2, 32)
            FL = ar.take(2)
            flag = FL[0:1, 1:2].bitcast(I32)
            h = ts(MK, CB, 0.0, None, ALU.is_gt, w=[hcb])
            i, ps, busy = PB.get()
            for m in range(2):
                for k in range(2):
                    hh = mm(ps[:, m * 32:m * 32 + 32], C("up", 512)[:, k * 256 + m * 128:k * 256 + m * 128 + 128],
                            MK[:, k, :], k == 0, k == 1, busy + [h])
            for k in range(2):
                hh = mm(ps[:, 64:96], ONES, MK[:, k, :], k == 0, k == 1)
            tt(RK, ps[:, 0:64].rearrange("p (a b) -> p a b", a=2), MK, MUL, [hh])
            h = red(FL[:, 0:1], ps[:, 64:96], MAX)
            PB.put(i, [h])
            hrk = cp(flag, FL[0:1, 0:1])
            barrier()
            n0 = ar.n
            got = [PA.get() for _ in range(4)]
            busyA = [b for _, _, bs in got for b in bs]
            acc = [bank for _, bank, _ in got]
            SL = C("slots", CAP)
            Q.part(flag, LIMIT, [hrk])
            stream["said"] = []

            SEL = Ring([(ar.take(2, 128), ar.take(2, 128)) for _ in range(2)])
            HG = Ring([ar.take(8, 128) for _ in range(2)])
            SWT = Ring([ar.take(256) for _ in range(2)])
            AC = Ring([ar.take(512)])
            AT = Ring([ar.take(4, 128) for _ in range(2)])
            YS = Ring([ar.take(1024) for _ in range(2)])

            def gather(pair):
                r, (sel, sw), rb = SEL.get()
                pick = lambda x: x[:, :, 2 * pair:2 * pair + 2].unsqueeze(3).broadcast_to([128, 2, 2, CAP])
                s4, w4 = (x.rearrange("p m (e s) -> p m e s", e=2) for x in (sel, sw))
                h = None
                for m in range(2):
                    pm = lambda x: x[:, m, 2 * pair:2 * pair + 2].unsqueeze(2).broadcast_to([128, 2, CAP])
                    h = tt(s4[:, m], SL.unsqueeze(1).broadcast_to([128, 2, CAP]), pm(RK), ALU.is_equal, rb)
                hsel = h
                for m in range(2):
                    pm = lambda x: x[:, m, 2 * pair:2 * pair + 2].unsqueeze(2).broadcast_to([128, 2, CAP])
                    hw = tt(w4[:, m], s4[:, m], pm(CB), MUL)
                r2, hg, rb2 = HG.get()
                he = []
                for half in range(2):
                    i, ps, busy = PB.get()
                    for j in range(4):
                        for m in range(2):
                            k = half * 4 + j
                            h = mm(ps[:, j * 128:j * 128 + 128], XN[:, m, k * 128:k * 128 + 128], sel[:, m, :],
                                   m == 0, m == 1, busy + [hsel])
                    o = hg[:, half * 4:half * 4 + 4, :]
                    src = ps[:, :].rearrange("p (a b) -> p a b", a=4)
                    e = cp(o, src, [h] + rb2) if half else act(o, src, ACT.Copy, [h] + rb2)
                    PB.put(i, [e])
                    he.append(e)
                r3, swt, rb3 = SWT.get()
                i, ps, busy = PB.get()
                for m in range(2):
                    h = tp(ps[:, m * 128:m * 128 + 128], sw[:, m, :], busy + [hw])
                e = act(swt, ps[:, 0:256], ACT.Copy, [h] + rb3)
                PB.put(i, [e])
                SEL.put(r, [h])
                return (r2, hg, he), (r3, swt, e)

            def up(pair, g_):
                r2, hg, he = g_
                wg = [weights(t["w_gate_2"][layer, 2 * pair + e], 8, 512) for e in range(2)]
                wu = [weights(t["w_up_2"][layer, 2 * pair + e], 8, 512) for e in range(2)]
                wd = [weights(t["w_down_2"][layer, 2 * pair + e], 4, 1024) for e in range(2)]
                r, ac, rb = AC.get()
                banks_ = []
                for wx in (wg, wu):
                    i, ps, busy = PB.get()
                    for k in range(8):
                        for e in range(2):
                            h = mm(ps[64 * e:64 * e + 64, :], hg[:, k, 64 * e:64 * e + 64], wx[e][1][:, k, :],
                                   k == 0, k == 7, busy + he + [wx[e][2]])
                    done_with(wx[0][0])
                    done_with(wx[1][0])
                    banks_.append((i, ps, h))
                HG.put(r2, [h])
                i, ps, h = banks_[0]
                e1 = act(ac, ps[:, :], ACT.Silu, [h] + rb)
                PB.put(i, [e1])
                i, ps, h = banks_[1]
                e2 = tt(ac, ps[:, :], ac, MUL, [h, e1])
                PB.put(i, [e2])
                return wd, r, ac, e2

            def lower(u_):
                wd, r, ac, e2 = u_
                i, ps, busy = PB.get()
                for f in range(4):
                    h = tp(ps[:, f * 128:f * 128 + 128], ac[:, f * 128:f * 128 + 128], busy + [e2])
                AC.put(r, [h])
                r, at, rb = AT.get()
                hat = act(at, ps[:, :].rearrange("p (a b) -> p a b", a=4), ACT.Copy, [h] + rb)
                PB.put(i, [hat])
                y = [PB.get() for _ in range(2)]
                for f in range(4):
                    for c in range(2):
                        for e in range(2):
                            h = mm(y[c][1][64 * e:64 * e + 64, :], at[:, f, 64 * e:64 * e + 64],
                                   wd[e][1][:, f, c * 512:c * 512 + 512], f == 0, f == 3,
                                   y[0][2] + y[1][2] + [hat, wd[e][2]])
                done_with(wd[0][0])
                done_with(wd[1][0])
                AT.put(r, [h])
                r, ys, rb = YS.get()
                e1 = act(ys[:, 0:512], y[0][1][:, :], ACT.Copy, [h] + rb)
                e2 = cp(ys[:, 512:1024], y[1][1][:, :], [h] + rb)
                PB.put(y[0][0], [e1])
                PB.put(y[1][0], [e2])
                return r, ys, [e1, e2]

            def scatter(pair, s_, y_):
                r3, swt, e = s_
                r, ys, he = y_
                for m in range(2):
                    for c in range(2):
                        h = mm(acc[2 * m + c][:, :], swt[:, m * 128:m * 128 + 128], ys[:, c * 512:c * 512 + 512],
                               pair == 0, pair == 15, busyA + he + [e])
                SWT.put(r3, [h])
                YS.put(r, [h])

            g_, s_ = gather(0)
            y_ = None
            for pair in range(16):
                u_ = up(pair, g_)
                if y_ is not None:
                    scatter(pair - 1, s_old, y_)
                s_old = s_
                if pair < 15:
                    g_, s_ = gather(pair + 1)
                y_ = lower(u_)
            scatter(15, s_old, y_)

            stream["replay"], stream["said"] = stream["said"], None
            Q.way()
            ar.n = n0
            for ring in (PA, PB):
                ring.busy = [[] for _ in ring.busy]
            GA = Ring([ar.take(4, 256) for _ in range(2)])
            CR = Ring([ar.take(256) for _ in range(2)])
            for pair in range(16):
                wg = [weights(t["w_gate_2"][layer, 2 * pair + e], 8, 512) for e in range(2)]
                wu = [weights(t["w_up_2"][layer, 2 * pair + e], 8, 512) for e in range(2)]
                wd = [weights(t["w_down_2"][layer, 2 * pair + e], 4, 1024) for e in range(2)]
                outs = []
                for e_ in range(2):
                    ex = 2 * pair + e_
                    r, ga, rb = GA.get()
                    r2, cr, rb2 = CR.get()
                    i, ps, busy = PB.get()
                    for k in range(2):
                        h = mm(ps[:, 0:256], bc(CB[:, k, ex:ex + 1], 128), C("id2", 512)[:, k * 256:k * 256 + 256],
                               k == 0, k == 1, busy)
                    hc_ = act(cr, ps[:, 0:256], ACT.Copy, [h] + rb2)
                    PB.put(i, [hc_])
                    for f in range(4):
                        i, ps, busy = PB.get()
                        for j, (sl, wt, landed) in enumerate((wg[e_], wu[e_])):
                            for k in range(8):
                                h = mm(ps[:, j * 256:j * 256 + 256], wt[:, k, f * 128:f * 128 + 128], HT[:, k, :],
                                       k == 0, k == 7, busy + [landed])
                        e = act(ga[:, f, :], ps[:, 0:256], ACT.Silu, [h] + rb)
                        e = tt(ga[:, f, :], ps[:, 256:512], ga[:, f, :], MUL, [h, e])
                        PB.put(i, [e])
                        e = tt(ga[:, f, :], ga[:, f, :], cr, MUL, [hc_])
                    CR.put(r2, [e])
                    outs.append((r, ga, e))
                for x in (wg, wu):
                    done_with(x[0][0])
                    done_with(x[1][0])
                for e_ in range(2):
                    r, ga, e = outs[e_]
                    for f in range(4):
                        for m in range(2):
                            for c in range(2):
                                h = mm(acc[2 * m + c][:, :], ga[:, f, m * 128:m * 128 + 128],
                                       wd[e_][1][:, f, c * 512:c * 512 + 512], pair == 0 and e_ == 0 and f == 0,
                                       pair == 15 and e_ == 1 and f == 3, [e, wd[e_][2]])
                    GA.put(r, [h])
                done_with(wd[0][0])
                done_with(wd[1][0])
            stream["replay"] = None
            joined = Q.meet()
            for ring in (PA, PB):
                ring.busy = [list(joined) for _ in ring.busy]
            for k in ("pe", "dve", "act", "pool"):
                Q.pending[k] = list(joined)
            ev = gated_add(MOD, 1)
            for m in range(2):
                for c in range(2):
                    PA.put(got[2 * m + c][0], ev(m, c, acc[2 * m + c], joined[0]))

        ar.n = 0
        CAT = ar.take(12, 256)
        gdn(CAT)
        probe("mix0", CAT, edge())
        ar.n = 12 * 256
        barrier()
        memory_attention(0, CAT)
        probe("cat0", CAT, edge())
        project_out(t["w_out"][0], 0, CAT, 12)
        probe("xa0", X[:, :, :], edge())
        conv_glu(0)
        probe("xb0", X[:, :, :], edge())
        barrier()
        nsa(CAT)
        ar.n = 12 * 256
        barrier()
        memory_attention(1, CAT)
        probe("cat1", CAT, edge())
        project_out(t["w_out"][1], 1, CAT, 12)
        conv_glu(1)
        barrier()

        def last_norm(src):
            hl = load("fn", MN[:, 0:4, :].rearrange("p a b -> p (a b)"), src.broadcast_to([128, 1024]), edge())
            r = sm(2)
            rstd(X, r, 1024, XN[:, 0, :])
            for i in range(2):
                h = stt(X[:, i, :], X[:, i, :], r[:, i:i + 1], MN[:, 0:4, :].rearrange("p a b -> p (a b)"), MUL, MUL,
                        [hl])
            return h
        last_norm(t["final_norm_w"])
        probe("x1", X[:, :, :], edge())
        for layer in range(2):
            barrier()
            ar.n = 0
            MOD = ar.take(6144)
            modulation(layer, MOD)
            probe(f"mod{layer}", MOD, edge())
            barrier()
            mixers(layer, MOD)
            probe(f"xm{layer}", X[:, :, :], edge())
            barrier()
            ar.n = 6144
            moe(layer, MOD)
            probe(f"xe{layer}", X[:, :, :], edge())
        barrier()
        h = last_norm(t["final_norm_g_2"])
        h = load("out", out[0].rearrange("(a p) d -> p a d", p=128), X[:, :, :], [h])
        finals = [h] + ([loaded("dbg")] if dbg is not None else [])

        Q.count()
        block = ctx.enter_context(nc.Block())

        @block.sync
        def _(eng):
            Q.write("sp", eng)
            for x in finals:
                eng.wait_ge(x.sem, x.value)

        @block.tensor
        def _(eng):
            Q.write("pe", eng)

        @block.vector
        def _(eng):
            Q.write("dve", eng)

        @block.scalar
        def _(eng):
            Q.write("act", eng)

        @block.gpsimd
        def _(eng):
            Q.write("pool", eng)


_BIG = ["x", "mem", "mem_w_kv", "w_out", "gdn_w_in", "nsa_w_in", "nsa_cmp_w1_k", "nsa_cmp_w2_k", "nsa_cmp_w1_v",
        "nsa_cmp_w2_v", "ffn_w_up", "ffn_w_down", "w_ada_2", "b_ada_2", "norm1_g_2", "norm2_g_2", "w_in_2", "b_in_2",
        "w_branch_m_2", "w_branch_a_2", "w_out_2", "w_router_group_2", "w_router_expert_2", "w_gate_2", "w_up_2",
        "w_down_2"]


def lay_out(inputs):
    a = {k: np.ascontiguousarray(inputs[k]) for k in _BIG}
    i = {k: np.asarray(v) for k, v in inputs.items()}
    cols = lambda z: np.asarray(z).reshape(-1, 128)
    b = i["b_in_2"]
    parts = [i["norm_mix_w"], i["norm_ffn_w"], i["mem_norm_w"], i["gdn_conv_w"], i["gdn_norm_w"], i["ffn_conv_w"],
             i["ffn_conv_b"], i["nsa_cmp_pos_k"], i["nsa_cmp_pos_v"], b[:, 0:1024], b[:, 1536:2048], b[:, 2832:3856],
             b[:, 3856:4880], i["conv_w_2"], i["conv_b_2"], i["mlstm_norm_g_2"], i["c_2"]]
    a["vecs"] = np.ascontiguousarray(np.concatenate([cols(z) for z in parts], 0).T)
    rows = [i["gdn_a_log"], i["gdn_dt_bias"], i["b_router_group_2"], i["b_router_expert_2"], i["q_norm_g_2"],
            i["k_norm_g_2"], b[:, 2048:2064]]
    a["rows"] = np.ascontiguousarray(np.concatenate([np.asarray(z).reshape(-1) for z in rows])[None])
    table, _, _, hot = constants()
    a["cst"] = table
    a["hot"] = hot
    a["tab"] = np.ascontiguousarray(np.concatenate([i["rel_bias"], np.full((1, 8), NEG, np.float32)], 0))
    a["final_norm_w"] = i["final_norm_w"].reshape(1, 1024)
    a["final_norm_g_2"] = i["final_norm_g_2"].reshape(1, 1024)
    return a


def kernel(**inputs):
    import concourse.bacc as _bacc
    from concourse.bass_utils import run_bass_kernel_spmd as _run

    nc = _bacc.Bacc("TRN2", target_bir_lowering=False, num_devices=1)
    arrays, t = {}, {}
    for name, a in lay_out(inputs).items():
        arrays[f"in_{name}"] = a
        t[name] = nc.dram_tensor(f"in_{name}", a.shape, F32, kind="ExternalInput").ap()
    out = nc.dram_tensor("out_x", (1, 256, 1024), F32, kind="ExternalOutput").ap()
    build(nc, t, out)
    r = _run(nc, [arrays], core_ids=[0])
    return r.results[0]["out_x"]
```

```python
from contextlib import ExitStack

import numpy as np

import concourse.bass as bass
from concourse import mybir

F32 = mybir.dt.float32
I32 = mybir.dt.int32
U32 = mybir.dt.uint32
ALU = mybir.AluOpType
ACT = mybir.ActivationFunctionType
AX = mybir.AxisListType
MUL, ADD, SUB, MAX, MIN = ALU.mult, ALU.add, ALU.subtract, ALU.max, ALU.min
NEG = -1e30
FLOOR = -1e28
NSLOT = 5
SLOT = 4096
ARENA = 16384
CAP = 64
LIMIT = CAP


class Handle:

    def __init__(self, sem, step, value=None):
        self.sem, self.step, self.value, self.used, self.free = sem, step, value, value is not None, None


class Queues:

    def __init__(self, nc, ctx):
        self.nc = nc
        self.sems = {k: ctx.enter_context(nc.semaphore(f"s_{k}")) for k in ("pe", "dve", "act", "pool")}
        self.q = {k: [] for k in ("pe", "dve", "act", "pool", "sp")}
        self.last = {}
        self.pending = {}

    def add(self, k, fn, w=(), chain=False):
        w = [x for x in w if x is not None] + self.pending.pop(k, [])
        if chain and k in self.last:
            w.append(self.last[k])
        for x in w:
            x.used = True
        h = Handle(self.sems[k], 1)
        self.q[k].append((fn, w, h))
        self.last[k] = h
        return h

    def dma(self, k, out, in_, sem, value, w=(), **kw):
        for x in w:
            x.used = True
        h = Handle(sem, 16, value)
        self.q[k].append((lambda e: e.dma_start(out, in_, **kw), list(w), h))
        return h

    def free(self, k, sem):
        self.q[k].append(("free", sem))

    def part(self, flag, limit, w):
        for x in w:
            x.used = True
        self.trunk, self.ways, self.before = self.q, [], dict(self.last)
        self.flag, self.limit, self.flag_w = flag, limit, list(w)
        self.way()

    def way(self):
        self.last = dict(self.before)
        self.pending = {}
        new = {k: [] for k in ("pe", "dve", "act")}
        self.ways.append(new)
        self.q = dict(self.trunk) | new

    def meet(self):
        self.q = self.trunk
        self.last = dict(self.before)
        out = []
        for k in ("pe", "dve", "act"):
            j = Handle(self.sems[k], 1)
            j.used = True
            self.q[k].append(("ways", self.flag, self.limit, self.flag_w, self.ways[0][k], self.ways[1][k], j))
            self.last[k] = j
            out.append(j)
        return out

    def count_list(self, items, n):
        free = []
        before = None
        ends = [it[2] for it in items if len(it) == 3]
        if ends:
            ends[-1].used = True
        for it in items:
            if it[0] == "free":
                if before is not None and not before.used and before.free is None:
                    before.free = it[1]
                else:
                    free.append(it[1])
            elif it[0] == "ways":
                assert not free
                ends = [self.count_list(x, n) for x in it[4:6]]
                it[6].value = n = max(ends) + 1
                for x, end in zip(it[4:6], ends):
                    x.append(("raise", n - end, end, None))
            else:
                before = h = it[2]
                if h.step == 1 and h.used:
                    n += 1
                    h.value = n
                elif h.step == 1 and free:
                    h.free = free.pop(0)
        if free:
            items.append(("rest", free, None, n))
        return n

    def count(self):
        for k in self.sems:
            self.count_list(self.q[k], 0)

    def write(self, k, eng, items=None, seen=None):
        seen = {} if seen is None else seen

        def wait(handles):
            need = {}
            for x in handles:
                need[id(x.sem)] = max(need.get(id(x.sem), (0, None))[0], x.value), x.sem
            for i, (val, sem) in need.items():
                if seen.get(i, 0) < val:
                    eng.wait_ge(sem, val)
                    seen[i] = val

        for it in self.q[k] if items is None else items:
            if it[0] == "free":
                continue
            if it[0] == "rest":
                eng.wait_ge(self.sems[k], it[3])
                for sem in it[1]:
                    eng.sem_inc(sem, 1)
                continue
            if it[0] == "raise":
                if it[2]:
                    eng.wait_ge(self.sems[k], it[2])
                eng.sem_inc(self.sems[k], it[1])
                continue
            if it[0] == "ways":
                wait(it[3])
                val = eng.value_load(it[1], min_val=0, max_val=256)
                with eng.If(val < it[2] + 1):
                    self.write(k, eng, it[4], dict(seen))
                with eng.Else():
                    self.write(k, eng, it[5], dict(seen))
                continue
            fn, w, h = it
            wait(w)
            ins = fn(eng)
            if h.used:
                ins.then_inc(h.sem, h.step)
            elif h.free is not None:
                ins.then_inc(h.free, 1)


class Ring:

    def __init__(self, places):
        self.places, self.busy, self.n = places, [[] for _ in places], 0

    def get(self):
        i = self.n % len(self.places)
        self.n += 1
        return i, self.places[i], self.busy[i]

    def put(self, i, readers):
        self.busy[i] = list(readers)


def vector_columns():
    at, n = {}, 0
    for name, cols in (("mix", 16), ("ffn", 16), ("mem", 16), ("gconv", 96), ("gnorm", 1), ("fconv", 132),
                       ("fconvb", 44), ("posk", 32), ("posv", 32), ("bqk", 16), ("bo", 8), ("bgm", 16), ("bga", 16),
                       ("mconv", 80), ("mconvb", 16), ("mnorm", 8), ("c", 8)):
        at[name] = n
        n += cols
    return at, n


def row_columns():
    at, n = {}, 0
    for name, cols in (("alog", 8), ("dt", 8), ("brg", 8), ("bre", 64), ("qg", 128), ("kg", 128), ("bgate", 32)):
        at[name] = n
        n += cols
    return at, n


def constants():
    p = np.arange(128)
    t = np.arange(256)
    parts = {}
    parts["ident"] = np.eye(128)
    parts["ones"] = np.ones((128, 128))
    parts["up"] = np.stack([(p[:, None] + 128 * k <= t[None]) for k in range(2)], 1).reshape(128, 512)
    parts["down"] = np.stack([(p[:, None] + 128 * k >= t[None]) for k in range(2)], 1).reshape(128, 512)
    parts["id2"] = np.stack([(p[:, None] + 128 * k == t[None]) for k in range(2)], 1).reshape(128, 512)
    parts["incl"] = p[:, None] >= p[None]
    levels = []
    for s in (1, 2, 4, 8, 16, 32, 64):
        m = (p[:, None] // (2 * s) == p[None] // (2 * s)) & (p[:, None] // s > p[None] // s)
        if s == 1:
            parts["lev1"] = m
        levels.append(m.T)
    parts["levT"] = np.stack(levels, 1).reshape(128, 7 * 128)
    parts["mfwd"] = np.stack([np.where(t[None] <= p[:, None] + 128 * k, 0.0, NEG) for k in range(2)], 1).reshape(128, 512)
    parts["mbwd"] = np.stack([np.where(t[None] >= p[:, None] + 128 * k, 0.0, NEG) for k in range(2)], 1).reshape(128, 512)
    half = 32
    inv = (10000.0 ** (-np.arange(0, half, 2, dtype=np.float32) / half)).astype(np.float32)
    row = np.repeat(np.arange(4, dtype=np.float32), 64)
    col = np.tile(np.arange(64, dtype=np.float32), 4)
    ar, ac = row[:, None] * inv, col[:, None] * inv
    c = np.concatenate([np.cos(ar), np.cos(ar), np.cos(ac), np.cos(ac)], 1)
    s = np.concatenate([-np.sin(ar), np.sin(ar), -np.sin(ac), np.sin(ac)], 1)
    parts["ropec"] = c.reshape(2, 128, 64).transpose(1, 0, 2).reshape(128, 128)
    parts["ropes"] = s.reshape(2, 128, 64).transpose(1, 0, 2).reshape(128, 128)
    parts["strip"] = np.broadcast_to(np.arange(31) == 15, (128, 31))
    parts["iota"] = np.broadcast_to(np.arange(8.0), (128, 8))
    parts["slots"] = np.broadcast_to(np.arange(1.0, CAP + 1), (128, CAP))
    at, n = {}, 0
    for k, v in parts.items():
        at[k] = n
        n += v.shape[1]
    table = np.concatenate([np.asarray(v, np.float32) for v in parts.values()], 1)
    d = 255 - np.arange(512)
    exact, f = 16, np.float32
    lg = np.log(np.maximum(d, 1).astype(f) / f(exact)) / f(np.log(128 / exact))
    big = np.minimum(exact + (lg * f(16)).astype(np.int32), 31)
    bucket = np.where(d < exact, np.maximum(d, 0), big)
    hot = np.zeros((33, 512), np.float32)
    hot[bucket[d >= 0], np.nonzero(d >= 0)[0]] = 1.0
    hot[32, d < 0] = 1.0
    return np.ascontiguousarray(table), at, n, hot


def build(nc, t, out, dbg=None):
    vat, nvec = vector_columns()
    rat, nrow = row_columns()
    _, cat_, ncst, _ = constants()
    with ExitStack() as ctx:
        def sb(name, shape, dt=F32):
            return ctx.enter_context(nc.sbuf_tensor(name, shape, dt))

        Q = Queues(nc, ctx)
        wring = sb("wring", [128, NSLOT * SLOT])
        X = sb("X", [128, 2, 1024])
        XN = sb("XN", [128, 2, 1024])
        HT = sb("HT", [128, 8, 256])
        MN = sb("MN", [128, 8, 256])
        PV = sb("PV", [128, nvec])
        RB = sb("RB", [128, nrow])
        CS = sb("CS", [128, ncst])
        SW = sb("SW", [128, 8, 144])
        AR = sb("AR", [128, ARENA])
        SM = sb("SM", [128, 1024])
        banks = [ctx.enter_context(nc.psum_tensor(f"ps{i}", [128, 512], F32)) for i in range(8)]
        ADR = sb("ADR", [96, 512])
        CC = sb("CC", [128, 8])
        mods = nc.dram_tensor("modulations", [2, 6144], F32, kind="Internal").ap()
        scratch = nc.dram_tensor("bias_rows", [8, 128, 512], F32, kind="Internal").ap()

        wsem = [ctx.enter_context(nc.semaphore(f"w{i}")) for i in range(NSLOT)]
        dsems = {}

        def dsem(name):
            if name not in dsems:
                dsems[name] = [ctx.enter_context(nc.semaphore(f"d_{name}")), 0]
            return dsems[name]

        def load(group, dst, src, w=(), k="pool", **kw):
            s = dsem(group)
            s[1] += 16
            return Q.dma(k, dst, src, s[0], s[1], w, **kw)

        def loaded(group):
            s = dsem(group)
            h = Handle(s[0], 16)
            h.value, h.used = s[1], True
            return h

        def pe(fn, w=()):
            return Q.add("pe", fn, w)

        def v(fn, w=()):
            return Q.add("dve", fn, w, chain=True)

        def a(fn, w=()):
            return Q.add("act", fn, w, chain=True)

        def g(fn, w=()):
            return Q.add("pool", fn, w, chain=True)

        def mm(o, l, r, start, stop, w=()):
            return pe(lambda e: e.matmul(o, l, r, start=start, stop=stop), w)

        def tp(o, i, w=(), n=128):
            return pe(lambda e: e.transpose(o, i, IDENT[0:n, 0:n]), w)

        def act(o, i, f, w=(), **kw):
            return a(lambda e: e.activation(o, i, f, **kw), w)

        def ts(o, i, s1, s2, op0, op1=None, w=(), q=v):
            if op1 is None:
                return q(lambda e: e.tensor_scalar(o, i, s1, None, op0), w)
            return q(lambda e: e.tensor_scalar(o, i, s1, s2, op0, op1), w)

        def tt(o, i0, i1, op, w=(), q=v):
            return q(lambda e: e.tensor_tensor(o, i0, i1, op), w)

        def stt(o, i0, s, i1, op0, op1, w=()):
            return v(lambda e: e.scalar_tensor_tensor(o, i0, s, i1, op0, op1), w)

        def cp(o, i, w=(), q=v):
            return q(lambda e: e.tensor_copy(o, i), w)

        def red(o, i, op, w=()):
            return v(lambda e: e.tensor_reduce(o, i, AX.X, op), w)

        def barrier():
            last = list(Q.last.values())
            for k in ("pe", "dve", "act", "pool"):
                if k in Q.last:
                    Q.pending[k] = list(last)

        def edge():
            return list(Q.last.values())

        class Arena:
            n = 0

            def take(self, *shape):
                k = int(np.prod(shape))
                ap = AR[:, self.n:self.n + k]
                self.n += k
                assert self.n <= ARENA, self.n
                if len(shape) == 2:
                    return ap.rearrange("p (a b) -> p a b", a=shape[0])
                if len(shape) == 3:
                    return ap.rearrange("p (a b c) -> p a b c", a=shape[0], b=shape[1])
                return ap

        ar = Arena()
        small = [0]

        def sm(*shape):
            k = int(np.prod(shape))
            if small[0] + k > 1024:
                small[0] = 0
            ap = SM[:, small[0]:small[0] + k]
            small[0] += k
            if len(shape) == 2:
                return ap.rearrange("p (a b) -> p a b", a=shape[0])
            return ap

        def C(name, n, rows=128):
            return CS[0:rows, cat_[name]:cat_[name] + n]

        def bc(ap, n):
            return ap.broadcast_to([ap.shape[0], n])

        IDENT = C("ident", 128)
        ONES = C("ones", 128)

        def vec(name, i):
            return PV[:, vat[name] + i:vat[name] + i + 1]

        PA = Ring([banks[i] for i in range(4)])
        PB = Ring([banks[i] for i in range(4, 8)])
        places = [wring[:, i * SLOT:(i + 1) * SLOT] for i in range(NSLOT)]
        fsem = [ctx.enter_context(nc.semaphore(f"f{i}")) for i in range(NSLOT)]
        turns, freed = [0] * NSLOT, [0] * NSLOT
        stream = {"n": 0, "said": None, "replay": None}

        def fill(parts):
            if stream["replay"] is not None:
                return stream["replay"].pop(0)
            n = stream["n"]
            stream["n"] += 1
            i = n % NSLOT
            busy = [Handle(fsem[i], 1, n // NSLOT)] if n >= NSLOT else []
            for dst, src in parts(places[i]):
                turns[i] += 16
                h = Q.dma("sp", dst, src, wsem[i], turns[i], busy)
            if stream["said"] is not None:
                stream["said"].append((i, places[i], h))
            return i, places[i], h

        def weights(src, kt, n):
            view = lambda place: place[:, 0:kt * n].rearrange("p (k n) -> p k n", k=kt)
            i, place, h = fill(lambda place: [(view(place), src.rearrange("(k p) n -> p k n", p=128))])
            return i, view(place), h

        def done_with(slot, k="pe"):
            Q.free(k, fsem[slot])

        load("x", X[:, :, :], t["x"][0].rearrange("(a p) d -> p a d", p=128), k="sp")
        load("c", PV[:, :], t["vecs"], k="sp")
        load("c", CS[:, 0:128], t["cst"][:, 0:128], k="sp")

        def load_rest():
            load("c1", CS[:, 128:ncst], t["cst"][:, 128:ncst], k="sp")
            load("c2", RB[:, :], t["rows"].broadcast_to([128, nrow]), k="sp")
            load("c2", SW[:, :, 0:16], t["gdn_w_in"][0, :, 4096:4112].rearrange("(k p) n -> p k n", p=128), k="sp")
            load("c2", SW[:, :, 16:40], t["nsa_w_in"][0, :, 2560:2584].rearrange("(k p) n -> p k n", p=128), k="sp")
            for l in range(2):
                o = 40 + 52 * l
                load("c2", SW[:, :, o:o + 16], t["w_in_2"][l, :, 2048:2064].rearrange("(k p) n -> p k n", p=128), k="sp")
                load("c2", SW[:, :, o + 16:o + 20], t["w_router_group_2"][l].rearrange("(k p) n -> p k n", p=128), k="sp")
                load("c2", SW[:, :, o + 20:o + 52], t["w_router_expert_2"][l].rearrange("(k p) n -> p k n", p=128), k="sp")
            return loaded("c1"), loaded("c2")

        hc = loaded("c")
        for k in ("pe", "dve", "act", "pool"):
            Q.pending[k] = [loaded("x")]

        def probe(name, ap, w):
            if dbg is not None and name in dbg:
                h = load("dbg", dbg[name], ap, w)
                for k in ("pe", "dve", "act", "pool"):
                    Q.pending.setdefault(k, []).append(h)

        def power(x, w, y=None):
            if y is None:
                shape = list(x.shape)[1:]
                y = sm(*shape)
                z = sm(*shape)
            else:
                y, z = y
            v(lambda e: e.reciprocal(x, x), w)
            h = act(y, x, ACT.Sqrt, [Q.last["dve"]])
            v(lambda e: e.reciprocal(z, y), [h])
            stt(z, z, 0.5, x, MUL, MUL)
            return stt(x, y, 0.5, z, MUL, ADD)

        MF = MN[:, :, :].rearrange("p a b -> p (a b)")

        def norm_part(m):
            r = sm(1)
            h = act(XN[:, m, :], X[:, m, :], ACT.Square, edge() if m == 0 else [Q.last["dve"]], accum_out=r)
            h = ts(r, r, 1.0 / 1024, 1e-6, MUL, ADD, [h])
            power(r, [h])
            normed[m] = ts(XN[:, m, :], X[:, m, :], r, None, MUL)

        normed = [None, None]

        def norm_features(dst, scale):
            got = [PB.get() for _ in range(4)]
            for m in range(2):
                for k in range(8):
                    h = tp(got[k // 2][1][:, (k % 2) * 256 + m * 128:(k % 2) * 256 + m * 128 + 128],
                           XN[:, m, k * 128:k * 128 + 128], [normed[m]] + got[k // 2][2])
                    if m:
                        normed.append(h)
            hs, ht = [], normed[2:]
            del normed[2:]
            for k in range(8):
                i, ps, _ = got[k // 2]
                o, p = dst[:, k, :], ps[:, (k % 2) * 256:(k % 2) * 256 + 256]
                q = [ht[k + 1 - k % 2]]
                if k // 2 % 2:
                    e = act(o, p, ACT.Copy, q, **({"scale": scale(k)} if scale else {}))
                else:
                    e = ts(o, p, scale(k), None, MUL, w=q) if scale else cp(o, p, q)
                hs.append(e)
                PB.put(i, [e])
            return hs

        def gemm_f(src_w, kt, rhs, evac, w=(), n=None, cols=None, keep=None):
            n = n or src_w.shape[1]
            slot, wt, landed = keep or weights(src_w, kt, n)
            cols = cols or range(0, n, 128)
            h = None
            for c in range(0, len(cols), 2):
                i, ps, busy = PB.get()
                readers = []
                hh = []
                for j, c0 in enumerate(cols[c:c + 2]):
                    for k in range(kt):
                        h = mm(ps[:, j * 256:j * 256 + 256], wt[:, k, c0:c0 + 128], rhs[:, k, :],
                               k == 0, k == kt - 1, list(w) + busy + [landed])
                    hh.append(h)
                for j, c0 in enumerate(cols[c:c + 2]):
                    readers += evac(c0 // 128, ps[:, j * 256:j * 256 + 256], hh[-1])
                PB.put(i, readers)
            if keep is None:
                done_with(slot)
            return h

        def gemm_t(wt, landed, kt, lhs, n, c0, evac, w=(), ms=(0, 1)):
            h = None
            for m in ms:
                i, ps, busy = PB.get()
                for k in range(kt):
                    h = mm(ps[:, 0:n], lhs[:, k, m * 128:m * 128 + 128], wt[:, k, c0:c0 + n],
                           k == 0, k == kt - 1, list(w) + busy + [landed])
                PB.put(i, evac(m, ps[:, 0:n], h))
            return h

        def down(srcs, lhs, evac, w=(), between=(), then=None):
            got = [PA.get() for _ in range(4)]
            busy = [b for _, _, bs in got for b in bs]
            groups = [[x] for x in srcs[:-2]] + [srcs[-2:]]
            for n, group in enumerate(groups):
                held = [weights(src, kt, 1024) + (k0, kt) for src, k0, kt in group]
                last = n == len(groups) - 1
                for m in range(2):
                    for c in range(2):
                        for slot, wt, landed, k0, kt in held:
                            for k in range(kt):
                                h = mm(got[2 * m + c][1][:, :], lhs[:, k0 + k, m * 128:m * 128 + 128],
                                       wt[:, k, c * 512:c * 512 + 512], n == 0 and k == 0 and slot == held[0][0],
                                       last and k == kt - 1 and slot == held[-1][0],
                                       list(w) + busy + [landed])
                        if last:
                            PA.put(got[2 * m + c][0], evac(m, c, got[2 * m + c][1], h))
                    if last and then:
                        then(m)
                for x in held:
                    done_with(x[0])
                if n < len(between):
                    between[n]()

        def add_x(m, c, ps, h):
            o = X[:, m, c * 512:c * 512 + 512]
            return [tt(o, ps[:, :], o, ADD, [h])]

        def taps(y, ps, name, base, stride, k, center, w=()):
            wc = lambda j: vec(name, base + stride * j)
            h = ts(y, ps, wc(center), None, MUL, w=w)
            for j in range(k):
                d = j - center
                if d < 0:
                    h = stt(y[:, -d:256], ps[:, 0:256 + d], wc(j), y[:, -d:256], MUL, ADD)
                elif d > 0:
                    h = stt(y[:, 0:256 - d], ps[:, d:256], wc(j), y[:, 0:256 - d], MUL, ADD)
            return h

        def softmax_top(ps_s, hs, scale, bias, dst):
            m, s = sm(2), sm(2)
            view = ps_s[:, :].rearrange("p (a b) -> p a b", a=2)
            if bias is None:
                h = red(m, view, MAX, hs)
                h = ts(m, m, -scale, None, MUL)
                return view, scale, m, s, h, list(hs), dst
            rd = stt(dst, view, scale, bias, MUL, ADD, hs)
            red(m, dst, MAX)
            h = ts(m, m, FLOOR, -1.0, MAX, MUL)
            return dst, 1.0, m, s, h, [rd], dst

        def softmax_exp(o):
            src, scale, m, s, h, hs, dst = o
            for i in range(2):
                e = act(dst[:, i, :], src[:, i, :], ACT.Exp, [h] + hs, bias=m[:, i:i + 1], scale=scale,
                        accum_out=s[:, i:i + 1])
            return e

        def softmax_end(o, e, gate):
            s, dst = o[3], o[6]
            ts(s, s, 1e-30, None, MAX, w=[e])
            v(lambda e, s=s: e.reciprocal(s, s))
            if gate is not None:
                tt(s, s, gate, MUL)
            for i in range(2):
                h = ts(dst[:, i, :], dst[:, i, :], s[:, i:i + 1], None, MUL)
            return h

        def turn(src, dst, w, n=256):
            i, ps, busy = PA.get()
            for m in range(2):
                for k in range(2):
                    h = tp(ps[:, k * 256 + m * 128:k * 256 + m * 128 + 128], src[:, m, k * 128:k * 128 + 128],
                           list(w) + busy)
            e = act(dst, ps[:, :].rearrange("p (a b) -> p a b", a=2), ACT.Copy, [h])
            PA.put(i, [e])
            return h, e

        def pipeline(n, stages, between=()):
            for i in range(max(n + max(s[0] for s in stages if s), len(between))):
                for s in stages:
                    if s is None:
                        if i < len(between):
                            between[i]()
                    elif 0 <= i - s[0] < n:
                        s[1](i - s[0])

        def memory_steps(layer):
            slot, place, landed = fill(lambda place: [(place[:, 2048:4096].rearrange("p (a d) -> p a d", a=2),
                                                       t["mem"][0].rearrange("(a p) d -> p a d", p=128))])
            MS = place[:, 0:2048].rearrange("p (a b) -> p a b", a=8)
            raw = place[:, 2048:4096].rearrange("p (a b) -> p a b", a=2)
            KT = place[:, 2048:3072].rearrange("p (a b) -> p a b", a=4)
            V = place[:, 3072:4096].rearrange("p (a b) -> p a b", a=2)
            hk, held = [], {}
            r = sm(2)
            for m in range(2):
                h = act(MS[:, 4 * m:4 * m + 4, :].rearrange("p a b -> p (a b)"), raw[:, m, :], ACT.Square, [landed],
                        accum_out=r[:, m:m + 1])
            h = ts(r, r, 1.0 / 1024, 1e-6, MUL, ADD, [h])
            power(r, [h])
            for m in range(2):
                hn = ts(raw[:, m, :], raw[:, m, :], r[:, m:m + 1], None, MUL)

            def features():
                for k in range(0, 8, 2):
                    i, ps, busy = PB.get()
                    for j in range(2):
                        for m in range(2):
                            h = tp(ps[:, j * 256 + m * 128:j * 256 + m * 128 + 128],
                                   raw[:, m, (k + j) * 128:(k + j) * 128 + 128], busy + [hn])
                    for j in range(2):
                        e = act(MS[:, k + j, :], ps[:, j * 256:j * 256 + 256], ACT.Copy, [h],
                                scale=vec("mem", 8 * layer + k + j))
                    PB.put(i, [e])
                held["m"] = [e]

            def ek(c, ps, h):
                hk.append(act(KT[:, c, :], ps, ACT.Copy, [h]))
                return hk[-1:]

            def ev(m, ps, h):
                hk.append(act(V[:, m, :], ps, ACT.Copy, [h]))
                return hk[-1:]

            def go(n):
                if n in (0, 2):
                    held["w"] = weights(t["mem_w_kv"][layer, :, 256 * n:256 * n + 512], 8, 512)
                sl, wt, wl = held["w"]
                if n < 2:
                    gemm_f(None, 8, MS, ek, held["m"], n=512, cols=[256 * n, 256 * n + 128], keep=held["w"])
                else:
                    gemm_t(wt, wl, 8, MS, 512, 0, ev, held["m"], (n - 2,))
                if n % 2:
                    done_with(sl)
            return [features] + [lambda n=n: go(n) for n in range(4)], (slot, KT, V, hk)

        def memory_attention(CAT, memory):
            slot, KT, V, hk = memory
            SR = Ring([ar.take(2, 256) for _ in range(3)])
            TR = Ring([ar.take(2, 256) for _ in range(2)])
            st = [{} for _ in range(4)]

            def scores(hd):
                o = st[hd]
                o["r"], s, rb = SR.get()
                o["i"], ps, busy = PB.get()
                for m in range(2):
                    h = mm(ps[:, m * 256:m * 256 + 256], CAT[:, 8 + hd, m * 128:m * 128 + 128], KT[:, hd, :],
                           True, True, busy + hk)
                o["o"] = softmax_top(ps, [h] + rb, 128.0 ** -0.5, None, s)

            def exps(hd):
                o = st[hd]
                o["e"] = softmax_exp(o["o"])
                PB.put(o["i"], [o["e"]])

            def norm(hd):
                o = st[hd]
                o["h"] = softmax_end(o["o"], o["e"], None)

            def turned(hd):
                o = st[hd]
                o["r2"], o["tr"], rb = TR.get()
                h, o["t"] = turn(o["o"][6], o["tr"], [o["h"]] + rb)
                SR.put(o["r"], [h])

            def out_(hd):
                o = st[hd]
                i, ps, busy = PA.get()
                for k in range(2):
                    h = mm(ps[:, 0:256], V[:, k, hd * 128:hd * 128 + 128], o["tr"][:, k, :], k == 0, k == 1,
                           busy + [o["t"]])
                TR.put(o["r2"], [h])
                PA.put(i, [cp(CAT[:, 8 + hd, :], ps[:, 0:256], [h])])

            pipeline(4, [(2, turned), (0, scores), (0, exps), (1, norm), (2, out_)])
            done_with(slot)

        def heads_softplus(dst, src, e1, w=()):
            h = ts(e1, src, -1.0, None, MUL, w=w)
            h = tt(e1, src, e1, MAX)
            h = act(e1, e1, ACT.Exp, [h], scale=-1.0)
            h = act(e1, e1, ACT.Ln, bias=1.0)
            return stt(dst, src, 0.0, e1, MAX, ADD, [h])

        def gdn(CAT):
            QK = ar.take(16, 256)
            ab = ar.take(2, 16)
            VB = ar.take(8, 256)
            norm_part(0)
            norm_part(1)
            for k in ("dve", "act", "pe"):
                Q.pending[k] = [hc]
            hT = norm_features(HT, lambda k: vec("mix", k))

            def ab_out(m, ps, h):
                return [cp(ab[:, m, :], ps, [h])]

            XF = XN[:, :, :].rearrange("p a b -> p (a b)")
            SQ = Ring([XF[:, 256 * j:256 * j + 256] for j in range(8)])
            iss, pss, busyss = PA.get()
            squares = []
            hn = []

            def sums():
                h = None
                for f, r, s, hs in squares:
                    h = mm(pss[0:16, 0:256], C("strip", 31)[:, 15 - f:31 - f], s, f == 0, f == 15, busyss + [hs])
                    SQ.put(r, [h])
                del squares[:]
                return h

            for chunk in range(6):
                def ev(c, ps, h, chunk=chunk):
                    f = chunk * 4 + c
                    y = QK[:, f, :] if f < 16 else VB[:, f - 16, :]
                    hv = taps(y, ps, "gconv", f, 24, 4, 3, [h])
                    hs = act(y, y, ACT.Silu, [hv])
                    hn.append(hs)
                    if f < 16:
                        r, s, rb = SQ.get()
                        squares.append((f, r, s, act(s, y, ACT.Square, rb + hT)))
                    return [hv]
                gemm_f(t["gdn_w_in"][0, :, chunk * 512:chunk * 512 + 512], 8, HT, ev, hT)
                if chunk == 0:
                    hc1, hc2 = load_rest()
                    Q.pending["pe"] = [hc1]
                if chunk in (1, 2, 3, 4):
                    if chunk == 1:
                        rest = squares[4:]
                        del squares[4:]
                        sums()
                        squares.extend(rest)
                    elif chunk < 4:
                        rest = squares[4:]
                        del squares[4:]
                        sums()
                        squares.extend(rest)
                    else:
                        hss = sums()
            for k in ("pe", "dve", "act"):
                Q.pending[k] = [hc1, hc2]
            gemm_t(SW[:, :, 0:16], None, 8, HT, 16, 0, ab_out, hT)
            for chunk in range(2):
                def ev(c, ps, h, chunk=chunk):
                    r = act(CAT[:, chunk * 4 + c, :], ps, ACT.Silu, [h])
                    return [r]
                gemm_f(t["gdn_w_in"][0, :, 3072 + chunk * 512:3584 + chunk * 512], 8, HT, ev, hT)
            beta, gg, e1, gc, egc, tot, kd = (sm(2, 8) for _ in range(7))
            RN = ar.take(256)
            h = act(beta, ab[:, :, 0:8], ACT.Sigmoid, [Q.last["dve"]])
            h = tt(gg, ab[:, :, 8:16], RB[:, rat["dt"]:rat["dt"] + 8].unsqueeze(1).broadcast_to([128, 2, 8]), ADD)
            h = heads_softplus(gg, gg, e1)
            ea = sm(8)
            h = act(ea, RB[:, rat["alog"]:rat["alog"] + 8], ACT.Exp)
            h = stt(gg, gg, -1.0, ea.unsqueeze(1).broadcast_to([128, 2, 8]), MUL, MUL, [h])
            hg = h
            h = ts(RN[0:16, :], pss[0:16, 0:256], 1e-6, None, ADD, w=[hss])
            PA.put(iss, [h])
            hrn = power(RN[0:16, :], [h], (ar.take(256)[0:16, :], ar.take(256)[0:16, :]))

            def ev(c, ps, h):
                return [cp(CAT[:, 8 + c, :], ps, [h])]
            gemm_f(t["gdn_w_in"][0, :, 4112:4624], 8, HT, ev, hT)
            UP = C("up", 128)
            i, ps, busy = PB.get()
            for m in range(2):
                h = mm(ps[:, m * 8:m * 8 + 8], UP, gg[:, m, :], True, True, busy + [hg])
            h = mm(ps[:, 16:24], ONES, gg[:, 0, :], True, True)
            h = cp(gc.rearrange("p a b -> p (a b)"), ps[:, 0:16], [h])
            h = tt(kd[:, 0, :], ps[:, 16:24], gc[:, 0, :], SUB)
            PB.put(i, [h])
            h = act(kd[:, 0, :], kd[:, 0, :], ACT.Exp, [h])
            hke = act(egc, gc, ACT.Exp)
            rq = sm(2, 16)
            i, ps, busy = PB.get()
            for m in range(2):
                h = tp(ps[:, m * 16:m * 16 + 16], RN[0:16, m * 128:m * 128 + 128], busy + [hrn], 16)
            h = ts(rq.rearrange("p a b -> p (a b)"), ps[:, 0:32], 128.0 ** -0.5, None, MUL, w=[h])
            PB.put(i, [h])
            hk = []
            for hd in range(8):
                i, ps, busy = PA.get()
                h = mm(ps[:, 0:256], bc(IDENT[0:16, 8 + hd:9 + hd], 128), RN[0:16, :], True, True, busy + [hrn])
                y = QK[:, 8 + hd, :]
                h = tt(y, ps[:, 0:256], y, MUL, [h] + hn)
                PA.put(i, [h])
                hk.append(h)
            KD = HT[:, 0:4, :].rearrange("p a b -> p (a b)")
            for hd in range(8):
                i, ps, busy = PB.get()
                for m in range(2):
                    h = tp(ps[:, m * 128:m * 128 + 128], VB[:, hd, m * 128:m * 128 + 128], busy)
                h = tp(ps[:, 256:384], QK[:, 8 + hd, 0:128], [hk[hd]])
                for m in range(2):
                    hh = ts(XN[:, m, hd * 128:hd * 128 + 128], ps[:, m * 128:m * 128 + 128], beta[:, m, hd:hd + 1],
                            None, MUL, w=[h])
                hh = ts(KD[:, hd * 128:hd * 128 + 128], ps[:, 256:384], kd[:, 0, hd:hd + 1], None, MUL, w=[hke, h])
                PB.put(i, [hh])
            hvb = hh
            steps, memory = memory_steps(0)
            ar.n -= 8 * 256 + 3 * 256
            ST = HT[:, 4:8, :].rearrange("p a b -> p (a b)")
            D, DT, LT, BT = ([ar.take(4, 128) for _ in range(4)] for _ in range(4))
            AT = [MF[:, 512 * j:512 * j + 512].rearrange("p (a b) -> p a b", a=4) for j in range(4)]
            four = lambda ps: ps[:, :].rearrange("p (a b) -> p a b", a=4)
            spread = lambda x: x.unsqueeze(1).broadcast_to([128, 4, 128])
            LEV = lambda s: spread(CS[:, cat_["levT"] + 128 * s:cat_["levT"] + 128 * s + 128])
            ID4 = spread(IDENT)
            hD, hDT, hLT, hAT, hbt = ([None] * 4 for _ in range(5))
            level = lambda s, q: tt(BT[q], LT[q], LEV(s), MUL, [hLT[q]])
            dec = [None] * 4
            for q in range(4):
                m, b = q // 2, q % 2
                i, ps, busy = PB.get()
                for j in range(4):
                    h = mm(ps[:, j * 128:j * 128 + 128], bc(gg[:, m, 4 * b + j:4 * b + j + 1], 128), UP, True, True,
                           busy + [hg])
                for j in range(4):
                    h2 = ts(DT[q][:, j, :], ps[:, j * 128:j * 128 + 128], gc[:, m, 4 * b + j:4 * b + j + 1], 0.0,
                            SUB, MAX, w=[h, hvb])
                PB.put(i, [h2])
                h2 = act(DT[q], DT[q], ACT.Exp, [h2], scale=-1.0)
                dec[q] = h2
            for q in range(4):
                m, b = q // 2, q % 2
                tok = slice(m * 128, m * 128 + 128)
                h2 = tt(DT[q], DT[q], spread(C("incl", 128)), MUL, [dec[q]])
                i, ps, busy = PB.get()
                i2, ps2, busy2 = PA.get()
                for j in range(4):
                    hd = 4 * b + j
                    h = mm(ps[:, j * 128:j * 128 + 128], QK[:, 8 + hd, tok], QK[:, 8 + hd, tok], True, True,
                           busy + [hk[hd]])
                    h = mm(ps2[:, j * 128:j * 128 + 128], QK[:, hd, tok], QK[:, 8 + hd, tok], True, True, busy2)
                for j in range(4):
                    hl = stt(D[q][:, j, :], ps[:, j * 128:j * 128 + 128], beta[:, m, 4 * b + j:4 * b + j + 1],
                             DT[q][:, j, :], MUL, MUL, [h])
                PB.put(i, [hl])
                ha = tt(BT[q], four(ps2), DT[q], MUL)
                PA.put(i2, [ha])
                if q:
                    steps.pop(0)()
                i, ps, busy = PB.get()
                i2, ps2, busy2 = PA.get()
                for j in range(4):
                    h = tp(ps[:, j * 128:j * 128 + 128], D[q][:, j, :], busy + [hl, ha])
                    h = tp(ps2[:, j * 128:j * 128 + 128], BT[q][:, j, :], busy2)
                hLT[q] = act(LT[q], four(ps), ACT.Copy, [h])
                hAT[q] = act(AT[q], four(ps2), ACT.Copy, [h])
                PB.put(i, [hLT[q]])
                PA.put(i2, [hAT[q]])
                h2 = tt(D[q], D[q], spread(C("lev1", 128)), MUL, [h])
                hD[q] = tt(D[q], ID4, D[q], SUB)
                h2 = tt(DT[q], LT[q], LEV(0), MUL, [hLT[q]])
                hDT[q] = tt(DT[q], ID4, DT[q], SUB)
                hbt[q] = level(1, q)
            for s in range(1, 7):
                hm = [None] * 4
                for q in range(4):
                    hb = hbt[q]
                    i, ps, busy = PB.get()
                    for j in range(4):
                        h = mm(ps[:, j * 128:j * 128 + 128], BT[q][:, j, :], D[q][:, j, :], True, True,
                               busy + [hb, hD[q]])
                    hm[q] = act(BT[q], four(ps), ACT.Copy, [h])
                    PB.put(i, [hm[q]])
                for q in range(4):
                    i, ps, busy = PB.get()
                    for j in range(4):
                        h = mm(ps[:, j * 128:j * 128 + 128], BT[q][:, j, :], DT[q][:, j, :], True, True,
                               busy + [hm[q], hDT[q]])
                    if s < 6:
                        i2, ps2, busy2 = PA.get()
                        for j in range(4):
                            h = mm(ps2[:, j * 128:j * 128 + 128], DT[q][:, j, :], BT[q][:, j, :], True, True, busy2)
                    hDT[q] = tt(DT[q], DT[q], four(ps), SUB, [h])
                    PB.put(i, [hDT[q]])
                    if s < 6:
                        hD[q] = tt(D[q], D[q], four(ps2), SUB)
                        PA.put(i2, [hD[q]])
                        hbt[q] = level(s + 1, q)
            hst = [None] * 2

            def gated(m, rs, h3):
                h2 = ts(rs, rs, 1.0 / 128, 1e-6, MUL, ADD, w=[h3])
                h2 = power(rs, [h2])
                h2 = tt(rs, rs, rq[:, m, 0:8].rearrange("p (a b) -> p a b", a=2), MUL)
                return [tt(D[2 * m + b], D[2 * m + b], rs[:, b, :].unsqueeze(2).broadcast_to([128, 4, 128]), MUL)
                        for b in range(2)]

            def into_cat(m, hs):
                tok = slice(m * 128, m * 128 + 128)
                for b in range(2):
                    o0, h2 = D[2 * m + b], hs[b]
                    i, ps, busy = PB.get()
                    for j in range(4):
                        h = tp(ps[:, j * 128:j * 128 + 128], o0[:, j, :], busy + [h2])
                    c = CAT[:, 4 * b:4 * b + 4, tok]
                    h2 = stt(c, four(ps), vec("gnorm", 0), c, MUL, MUL, [h])
                    PB.put(i, [h2])

            later = None
            for m in range(2):
                tok = slice(m * 128, m * 128 + 128)
                rs = sm(2, 4)
                hsq = []
                for b in range(2):
                    q = 2 * m + b
                    o0, r0, vn = D[q], LT[q], BT[q]
                    h2 = None
                    if m == 1:
                        i, ps, busy = PB.get()
                        i2, ps2, busy2 = PA.get()
                        for j in range(4):
                            hd = 4 * b + j
                            S = ST[:, hd * 128:hd * 128 + 128]
                            h = mm(ps[:, j * 128:j * 128 + 128], QK[:, 8 + hd, tok], S, True, True, busy + [hst[b]])
                            h = mm(ps2[:, j * 128:j * 128 + 128], QK[:, hd, tok], S, True, True, busy2)
                        for j in range(4):
                            hd = 4 * b + j
                            h2 = ts(r0[:, j, :], ps[:, j * 128:j * 128 + 128], egc[:, 1, hd:hd + 1],
                                    beta[:, 1, hd:hd + 1], MUL, MUL, w=[h])
                        h2 = tt(r0, XN[:, 1, b * 512:b * 512 + 512].rearrange("p (a b) -> p a b", a=4), r0, SUB)
                        hr0 = h2
                        PB.put(i, [h2])
                        for j in range(4):
                            h2 = ts(o0[:, j, :], ps2[:, j * 128:j * 128 + 128], egc[:, 1, 4 * b + j:4 * b + j + 1],
                                    None, MUL)
                        PA.put(i2, [h2])
                        h2 = hr0
                    i, ps, busy = PB.get()
                    for j in range(4):
                        hd = 4 * b + j
                        rhs = r0[:, j, :] if m else XN[:, 0, hd * 128:hd * 128 + 128]
                        h = mm(ps[:, j * 128:j * 128 + 128], DT[q][:, j, :], rhs, True, True,
                               busy + [hDT[q], h2, hvb])
                    hv = act(vn, four(ps), ACT.Copy, [h])
                    PB.put(i, [hv])
                    if b == 0:
                        steps.pop(0)()
                    if m == 0:
                        i, ps, busy = PA.get()
                        for j in range(4):
                            hd = 4 * b + j
                            h = mm(ps[:, j * 128:j * 128 + 128], KD[:, hd * 128:hd * 128 + 128], vn[:, j, :],
                                   True, True, busy + [hv, hvb])
                        hst[b] = cp(ST[:, b * 512:b * 512 + 512], ps[:, :], [h])
                        PA.put(i, [hst[b]])
                    i, ps, busy = PB.get()
                    for j in range(4):
                        h = mm(ps[:, j * 128:j * 128 + 128], AT[q][:, j, :], vn[:, j, :], True, True,
                               busy + [hv, hAT[q]])
                    if m:
                        h2 = tt(o0, four(ps), o0, ADD, [h])
                    else:
                        h2 = cp(o0, four(ps), [h])
                    PB.put(i, [h2])
                    for j in range(4):
                        h3 = act(r0[:, j, :], o0[:, j, :], ACT.Square, [h2], scale=rq[:, m, 4 * b + j:4 * b + j + 1],
                                 accum_out=rs[:, b, j:j + 1])
                    if later:
                        hs0 = gated(*later)
                        later = None
                later = (m, rs, h3)
            hs1 = gated(*later)
            into_cat(0, hs0)
            into_cat(1, hs1)
            return memory

        def first_block_end(m):
            last_part(MF[:, 0:1024], m, [ada["fn"]])
            mod_part(AR[:, 0:6144], 0, m)

        def conv_glu(layer):
            ar.n = ARENA - 22 * 256
            G = ar.take(22, 256)
            hT = norm_features(HT, lambda k: vec("ffn", 8 * layer + k))
            barrier()
            if layer:
                ada["mod"] = load_modulation(0, AR[:, 0:6144])
                ada["fn"] = load("fn", MF[:, 0:1024], t["final_norm_w"].broadcast_to([128, 1024]), edge())
                ada["g"] = load_gains(0, (MF[:, 1024:2048], XN[:, 1, :]))
            up = t["ffn_w_up"][layer]
            for val in range(2):
                for chunk in range(6):
                    n = 512 if chunk < 5 else 256

                    def ev(c, ps, h, chunk=chunk, val=val):
                        f = chunk * 4 + c
                        y = G[:, f, :]
                        if val:
                            return [tt(y, ps, y, MUL, [h] + hG)]
                        hv = taps(y, ps, "fconv", 66 * layer + f, 22, 3, 2, [h])
                        act(y, y, ACT.Silu, [hv], bias=vec("fconvb", 22 * layer + f))
                        return [hv]
                    hG = edge()
                    gemm_f(up[:, val * 2816 + chunk * 512:val * 2816 + chunk * 512 + n], 8, HT, ev, hT)
                    if chunk < 5:
                        if "sum" in ada:
                            ada_sum()
                        ada_chunk(12 * layer + 5 * val + chunk)
            if layer:
                modulation(AR[:, 0:6144], [ada["mod"]] + ada["g"], (MF[:, 1024:2048], XN[:, 1, :]))
            dn = t["ffn_w_down"][layer]

            def ada_next(n):
                def go():
                    ada_sum()
                    if n:
                        ada_chunk(n)
                return go
            down([(dn[2560:2816], 20, 2)] + [(dn[c * 512:c * 512 + 512], 4 * c, 4) for c in range(5)], G, add_x, edge(),
                 [ada_next(12 * layer + 10), ada_next(12 * layer + 11), ada_next(0)],
                 first_block_end if layer else norm_part)

        def project_out(src, layer, CAT, kt, evac=add_x):
            down([(src[c * 512:c * 512 + 512], 4 * c, 4) for c in range(kt // 4)], CAT, evac, edge(), (), norm_part)

        def nsa(CAT):
            ar.n = 12 * 256
            KC = ar.take(4, 256)
            KS = ar.take(4, 256)
            VS = ar.take(2, 512)
            GT = ar.take(2, 24)
            BI = ar.take(8, 512)
            n0 = ar.n
            hT = norm_features(HT, lambda k: vec("mix", 8 + k))
            barrier()
            tab, hot, row = ar.take(8), ar.take(512), ar.take(512)
            load("tab", tab[0:33, :], t["tab"], edge())
            load("tab", hot[0:33, :], t["hot"], edge())
            htab = loaded("tab")
            win = t["nsa_w_in"][0]
            hr = []

            def keep(dst):
                def ev(c, ps, h):
                    r = act(dst(c), ps, ACT.Copy, [h])
                    hr.append(r)
                    return [r]
                return ev
            for ch in range(2):
                gemm_f(win[:, ch * 512:ch * 512 + 512], 8, HT, keep(lambda c: CAT[:, 4 * ch + c, :]), hT)
                if ch == 0:
                    i, ps, busy = PB.get()
                    h = mm(ps[0:8, :], tab[0:33, :], hot[0:33, :], True, True, busy + [htab])
                    h = cp(row[0:8, :], ps[0:8, :], [h])
                    PB.put(i, [h])
                    h = load("row", scratch, row[0:8, :].unsqueeze(1).broadcast_to([8, 128, 512]), [h])
                    for hd in range(8):
                        for m in range(2):
                            ap = bass.AP(scratch.tensor, scratch[hd].offset + 255 - 128 * m, [[511, 128], [1, 256]])
                            load("bias", BI[:, hd, m * 256:m * 256 + 256], ap, [h])
                    hb = loaded("bias")
            gemm_f(win[:, 1024:1536], 8, HT, keep(lambda c: KC[:, c, :]), hT)
            for ch in range(2):
                slot, wt, landed = weights(win[:, 1536 + 512 * ch:2048 + 512 * ch], 8, 512)
                gemm_f(None, 8, HT, keep(lambda c: KS[:, 2 * ch + c, :]), hT, n=512, cols=[0, 128],
                       keep=(slot, wt, landed))

                def ev(m, ps, h):
                    r = cp(VS[:, m, ch * 256:ch * 256 + 256], ps, [h])
                    hr.append(r)
                    return [r]
                gemm_t(wt, landed, 8, HT, 256, 256, ev, hT)
                done_with(slot)

            def ev(m, ps, h):
                r = act(GT[:, m, :], ps, ACT.Sigmoid, [h])
                hr.append(r)
                return [r]
            gemm_t(SW[:, :, 16:40], None, 8, HT, 24, 0, ev, hT)
            ar.n = n0
            barrier()
            for k in ("pe", "dve", "act"):
                Q.pending[k].append(hb)
            BL = ar.take(32, 32)
            HID = ar.take(32)
            KCT, VC = ar.take(32), ar.take(2, 128)
            BL2, HD = ar.take(32, 32), ar.take(128)
            halves, slots = [], []
            i, ps, busy = PB.get()
            for kv, bl in enumerate((BL, BL2)):
                for gr in range(2):
                    src = KC[:, 2 * kv + gr, :]
                    s = bass.AP(src.tensor, src.offset, [list(src.ap[0]), [1, 32], [16, 15]])
                    p = PV[:, vat["posk"] + 32 * kv:vat["posk"] + 32 * kv + 32].unsqueeze(2).broadcast_to([128, 32, 15])
                    h = tt(bl[:, :, gr * 16:gr * 16 + 15], s, p, ADD)
                hbl = v(lambda e, bl=bl: e.memset(bl[:, :, 15:32:16], 0.0))
                w1 = t["nsa_cmp_w1_v" if kv else "nsa_cmp_w1_k"][0]
                halves.append((bl, hbl, weights(w1, 32, 128)))
            for l in range(32):
                for kv, (bl, hbl, (slot, wt, landed)) in enumerate(halves):
                    h = mm(ps[64 * kv:64 * kv + 32, 0:128], bl[:, l, :], wt[:, l, :], l == 0, l == 31,
                           busy + [landed, hbl])
            for x in halves:
                done_with(x[2][0])
            for kv in range(2):
                h = act(HD[64 * kv:64 * kv + 32, :], ps[64 * kv:64 * kv + 32, 0:128], ACT.Silu, [h])
            PB.put(i, [h])
            for kv in range(2):
                slot, wt, landed = weights(t["nsa_cmp_w2_v" if kv else "nsa_cmp_w2_k"][0], 1, 128)
                r = slice(64 * kv, 64 * kv + 32)
                i, ps, busy = PB.get()
                h2 = pe(lambda e, ps=ps, r=r: e.transpose(ps[:, 0:32], HD[r, :], IDENT[r, r]), busy + [h])
                hh = cp(HID, ps[:, 0:32], [h2] + ([e] if kv else []))
                PB.put(i, [hh])
                i, ps, busy = PB.get()
                if kv == 0:
                    hm = mm(ps[:, 0:32], wt[:, 0, :], HID, True, True, busy + [landed, hh])
                    e = cp(KCT, ps[:, 0:32], [hm])
                else:
                    for gr in range(2):
                        hm = mm(ps[0:15, gr * 128:gr * 128 + 128], HID[:, gr * 16:gr * 16 + 15], wt[:, 0, :], True,
                                True, busy + [landed, hh])
                    e = cp(VC[0:15, :, :], ps[0:15, 0:256].rearrange("p (a b) -> p a b", a=2), [hm])
                PB.put(i, [e])
                done_with(slot)
            probe("kct", KCT, [e])
            hcmp = e
            ar.n = n0
            ar.n += 1024 + 32 + 32 + 256
            PR = Ring([[ar.take(2, 256), ar.take(2, 256)] for _ in range(3)])
            for k in range(3):
                PR.put(k, [hcmp, h])
            TR = Ring([[ar.take(2, 256), ar.take(2, 256)] for _ in range(1)])
            SC = Ring([BL.rearrange("p a b -> p (a b)")[:, 32 * j:32 * j + 32].rearrange("p (a b) -> p a b", a=2)
                       for j in range(3)])
            PT = Ring([BL.rearrange("p a b -> p (a b)")[:, 256 * (j + 1):256 * (j + 1) + 256] for j in range(2)])
            scale = 128.0 ** -0.5
            st = [{} for _ in range(8)]
            steps, memory = memory_steps(1)
            held = []

            def queries(n):
                if n == 0:
                    held.append(weights(win[:, 2584:3096], 8, 512))
                gemm_f(None, 8, HT, keep(lambda c: CAT[:, 8 + c, :]), hT, n=512, cols=[256 * n, 256 * n + 128],
                       keep=held[0])
                if n:
                    done_with(held[0][0])

            def scores(hd):
                gr, o = hd // 4, st[hd]
                o["r"], bf, rb = PR.get()
                bias = BI[:, hd, :].rearrange("p (a b) -> p a b", a=2)
                o["o"] = []
                for br in range(2):
                    i, ps, busy = PB.get()
                    for m in range(2):
                        h = mm(ps[:, m * 256:m * 256 + 256], CAT[:, hd, m * 128:m * 128 + 128], KS[:, 2 * br + gr, :],
                               True, True, busy + hr)
                    o["o"].append(softmax_top(ps, [h, hb] + rb, scale, bias, bf[br]))
                    PB.put(i, o["o"][-1][5])
                o["r2"], sc, rb2 = SC.get()
                i, ps, busy = PB.get()
                for m in range(2):
                    h = mm(ps[:, m * 16:m * 16 + 15], CAT[:, hd, m * 128:m * 128 + 128],
                           KCT[:, gr * 16:gr * 16 + 15], True, True, busy + [hcmp])
                mx, s = sm(2), sm(2)
                sc15 = sc[:, :, 0:15]
                h = stt(sc15, ps[:, 0:32].rearrange("p (a b) -> p a b", a=2)[:, :, 0:15], scale, bias[:, :, 31:256:16],
                        MUL, ADD, [h] + rb2)
                PB.put(i, [h])
                red(mx, sc15, MAX)
                h = ts(mx, mx, FLOOR, -1.0, MAX, MUL)
                o["o"].append((sc15, 1.0, mx, s, h, [], sc15))

            def exps(hd):
                st[hd]["e"] = [softmax_exp(x) for x in st[hd]["o"]]

            def norm(hd):
                o = st[hd]
                o["h"] = [softmax_end(o["o"][br], o["e"][br], GT[:, :, 3 * hd + (1, 2, 0)[br]]) for br in range(3)]

            def turned(hd):
                o = st[hd]
                o["r4"], o["tr"], rb = TR.get()
                o["t"] = []
                for br in range(2):
                    h, e = turn(o["o"][br][6], o["tr"][br], [o["h"][br]] + rb)
                    o["t"].append(e)
                PR.put(o["r"], [h])
                o["r5"], pt, rb5 = PT.get()
                i, ps, busy = PA.get()
                for m in range(2):
                    h = tp(ps[0:15, m * 128:m * 128 + 128], o["o"][2][6][:, m, :], busy + [o["h"][2]])
                SC.put(o["r2"], [h])
                e = act(pt[0:15, :], ps[0:15, 0:256], ACT.Copy, [h] + rb5)
                PA.put(i, [e])
                o["pt"] = pt, e

            def out_(hd):
                gr, o = hd // 4, st[hd]
                pt, e = o["pt"]
                i, ps, busy = PA.get()
                mm(ps[:, 0:256], VC[0:15, gr, :], pt[0:15, :], True, False, busy + [e])
                for br in range(2):
                    for k in range(2):
                        h = mm(ps[:, 0:256], VS[:, k, br * 256 + gr * 128:br * 256 + gr * 128 + 128],
                               o["tr"][br][:, k, :], False, br == 1 and k == 1, o["t"])
                TR.put(o["r4"], [h])
                PT.put(o["r5"], [h])
                PA.put(i, [cp(CAT[:, hd, :], ps[:, 0:256], [h])])

            pipeline(8, [(2, turned), (0, scores), None, (0, exps), (1, norm), (2, out_)],
                     [lambda: queries(0), steps[0], lambda: queries(1)] + steps[1:])
            return memory

        def ada_chunk(n):
            layer, ch = n // 12, n % 12
            cs = slice(ch * 512, ch * 512 + 512)
            if n == 0:
                ada["cc"] = act(CC[:, :], PV[:, vat["c"]:vat["c"] + 8], ACT.Silu)
            if n == 0:
                ada["b", 0] = load("adb0", ADR[32:33, :], t["b_ada_2"][0:1, 0:512])
            if n < 23:
                l2, c2 = (n + 1) // 12, (n + 1) % 12
                r2 = 64 - 32 * (n % 2)
                ada["b", n + 1] = load(f"adb{(n + 1) % 2}", ADR[r2:r2 + 1, :], t["b_ada_2"][l2:l2 + 1, c2 * 512:c2 * 512 + 512],
                                       [ada["mm"]] if n else [])
            slot, wt, landed = weights(t["w_ada_2"][layer, :, cs], 8, 512)
            acc = wt[:, 0, :]
            h = ts(acc, acc, CC[:, 0:1], None, MUL, w=[landed, ada["cc"]])
            for k in range(1, 8):
                h = stt(acc, wt[:, k, :], CC[:, k:k + 1], acc, MUL, ADD)
            r = 32 + 32 * (n % 2)
            ada["sum"] = (layer, cs, slot, acc, h, ada.pop(("b", n)), r)

        def ada_sum():
            layer, cs, slot, acc, h, hb, r = ada.pop("sum")
            i, ps, busy = PB.get()
            mm(ps[0:1, :], ONES[:, 0:1], acc, True, False, busy + [h])
            ada["mm"] = h = mm(ps[0:1, :], ONES[r:r + 1, 0:1], ADR[r:r + 1, :], False, True, [hb])
            done_with(slot)
            e = act(ADR[0:1, :], ps[0:1, :], ACT.Copy, [h] + ([ada["out"]] if "out" in ada else []))
            PB.put(i, [e])
            ada["out"] = load(f"ado{layer}", mods[layer:layer + 1, cs], ADR[0:1, :], [e])

        ada = {}

        def load_modulation(layer, MOD, cut=(0, 6144)):
            c0, c1 = cut
            return load("mod", MOD[:, c0:c1], mods[layer:layer + 1, c0:c1].broadcast_to([128, c1 - c0]),
                        edge() + [loaded(f"ado{layer}")])

        def load_gains(layer, places):
            for name, j in zip(("norm1_g_2", "norm2_g_2"), places):
                load("ng", j, t[name][layer:layer + 1, :].broadcast_to([128, 1024]), edge())
            return [loaded("ng")]

        def modulation(MOD, w, places):
            for i, j in zip((1, 4), places):
                m = MOD[:, i * 1024:i * 1024 + 1024]
                stt(m, m, 1.0, j, ADD, MUL, w)

        def mod_part(MOD, which, m):
            r = sm(1)
            h = act(XN[:, m, :], X[:, m, :], ACT.Square, edge() if m == 0 else [Q.last["dve"]], accum_out=r)
            h = ts(r, r, 1.0 / 1024, 1e-6, MUL, ADD, [h])
            power(r, [h])
            h = stt(XN[:, m, :], X[:, m, :], r, MOD[:, (3 * which + 1) * 1024:(3 * which + 2) * 1024], MUL, MUL)
            normed[m] = tt(XN[:, m, :], XN[:, m, :], MOD[:, 3 * which * 1024:(3 * which + 1) * 1024], ADD)

        def last_part(weight, m, w):
            r = sm(1)
            h = act(XN[:, m, :], X[:, m, :], ACT.Square, edge() if m == 0 else [Q.last["dve"]], accum_out=r)
            h = ts(r, r, 1.0 / 1024, 1e-6, MUL, ADD, [h])
            power(r, [h])
            return stt(X[:, m, :], X[:, m, :], r, weight, MUL, MUL, w)

        def gated_add(MOD, which):
            def ev(m, c, ps, h):
                gt = MOD[:, (3 * which + 2) * 1024 + c * 512:(3 * which + 2) * 1024 + c * 512 + 512]
                j = XN[:, m, c * 512:c * 512 + 512]
                o = X[:, m, c * 512:c * 512 + 512]
                h1 = tt(j, ps[:, :], gt, MUL, [h])
                tt(o, o, j, ADD)
                return [h1]
            return ev

        def mixers(layer, MOD):
            n0 = ar.n
            hT = norm_features(HT, None)
            barrier()
            YM, YA = ar.take(4, 256), ar.take(4, 256)
            n1 = ar.n
            MQK = ar.take(8, 256)
            MV = ar.take(2, 512)
            LG = ar.take(2, 16)
            AQ = ar.take(2, 768)
            BV = AR[:, ar.n:ar.n + 1280]
            win = t["w_in_2"][layer]
            hb = load("bv", BV[:, 0:512], t["b_in_2"][layer:layer + 1, 1024:1536].broadcast_to([128, 512]), edge())
            load("bv", BV[:, 512:1280], t["b_in_2"][layer:layer + 1, 2064:2832].broadcast_to([128, 768]), edge())
            hb = loaded("bv")

            RAW = [XN[:, 0, j * 256:j * 256 + 256] for j in range(4)]
            rr = Ring(RAW)
            hx = list(hT)
            for ch in range(2):
                def ev(c, ps, h):
                    f = 4 * ch + c
                    i, raw, rb = rr.get()
                    h1 = act(raw, ps, ACT.Identity, [h] + rb + hx, bias=vec("bqk", 8 * layer + f))
                    hv = taps(MQK[:, f, :], raw, "mconv", 40 * layer + f, 8, 5, 2, [h1])
                    rr.put(i, [hv])
                    act(MQK[:, f, :], MQK[:, f, :], ACT.Silu, [hv], bias=vec("mconvb", 8 * layer + f))
                    return [h1]
                gemm_f(win[:, ch * 512:ch * 512 + 512], 8, HT, ev, hT)
                if ch == 0:
                    def ev_lg(m, ps, h):
                        return [tt(LG[:, m, :], ps, RB[:, rat["bgate"] + 16 * layer:rat["bgate"] + 16 * layer + 16], ADD, [h])]
                    o = 40 + 52 * layer
                    gemm_t(SW[:, :, o:o + 16], None, 8, HT, 16, 0, ev_lg, hT)
                    e1 = sm(2, 8)
                    LG2 = LG.rearrange("p a (b c) -> p a b c", b=4)
                    neg = sm(2, 8)
                    neg4 = neg.rearrange("p a (b c) -> p a b c", b=2)
                    h = ts(neg4, LG2[:, :, 1:4:2, :], -1.0, None, MUL)
                    heads_softplus(neg, neg, e1)
            i, ps, busy = PB.get()
            hn = Q.last["dve"]
            for m in range(2):
                for d in range(2):
                    U = C("down" if d else "up", 512)
                    for k in range(2):
                        h = mm(ps[:, m * 8 + d * 4:m * 8 + d * 4 + 4], U[:, k * 256 + m * 128:k * 256 + m * 128 + 128],
                               neg[:, k, 4 * d:4 * d + 4], k == 0, k == 1, busy + [hn])
            nb = sm(2, 8)
            h = cp(nb.rearrange("p a b -> p (a b)"), ps[:, 0:16], [h])
            PB.put(i, [h])
            cb = sm(2, 8)
            h = tt(cb.rearrange("p a (b c) -> p a b c", b=2), LG2[:, :, 0:3:2, :], nb.rearrange("p a (b c) -> p a b c", b=2),
                   ADD)
            hcb = h
            for c0, dst, n, b0 in ((1024, MV, 512, 0), (2064, AQ, 512, 512), (2576, AQ, 256, 1024)):
                slot, wt, landed = weights(win[:, c0:c0 + n], 8, n)

                def ev(m, ps, h):
                    d = dst[:, m, 512:768] if n == 256 else dst[:, m, 0:512]
                    return [tt(d, ps, BV[:, b0:b0 + n], ADD, [h, hb])]
                gemm_t(wt, landed, 8, HT, n, 0, ev, hT)
                done_with(slot)

            def ev(c, ps, h):
                return [act(YM[:, c, :], ps, ACT.Sigmoid, [h], bias=vec("bo", 4 * layer + c))]
            gemm_f(win[:, 1536:2048], 8, HT, ev, hT)
            rs = sm(2, 10)
            XF = XN.rearrange("p a b -> p (a b)")
            T2 = XF[:, 1280:1920]
            for m in range(2):
                h = tt(T2, AQ[:, m, 0:640], AQ[:, m, 0:640], MUL)
                h = red(rs[:, m, :], T2.rearrange("p (h d) -> p h d", d=64), ADD)
            h = ts(rs, rs, 1.0 / 64, 1e-6, MUL, ADD)
            h = power(rs, [h])
            before = edge()
            QR = XF[:, 0:1280].rearrange("p (a b) -> p a b", a=2)
            for m in range(2):
                x3 = AQ[:, m, 0:640].rearrange("p (h d) -> p h d", d=64)
                h = tt(x3, x3, rs[:, m, :].unsqueeze(2).broadcast_to([128, 10, 64]), MUL, w=before, q=g)
                for nme, h0, h1 in (("qg", 0, 8), ("kg", 8, 10)):
                    gn = RB[:, rat[nme] + 64 * layer:rat[nme] + 64 * layer + 64].unsqueeze(1)\
                        .broadcast_to([128, h1 - h0, 64])
                    h = tt(x3[:, h0:h1, :], x3[:, h0:h1, :], gn, MUL, q=g)
                cos = CS[:, cat_["ropec"] + 64 * m:cat_["ropec"] + 64 * m + 64]
                sin = CS[:, cat_["ropes"] + 64 * m:cat_["ropes"] + 64 * m + 64]
                x4 = AQ[:, m, 0:640].rearrange("p (h u d) -> p h u d", u=4, d=16)
                t4 = T2.rearrange("p (h u d) -> p h u d", u=4, d=16)
                s4 = sin.rearrange("p (u d) -> p u d", u=4)
                for u in range(4):
                    h = tt(t4[:, :, u, :], x4[:, :, u ^ 1, :], s4[:, u, :].unsqueeze(1).broadcast_to([128, 10, 16]),
                           MUL, q=g)
                h = tt(x3, x3, cos.unsqueeze(1).broadcast_to([128, 10, 64]), MUL, q=g)
                q4 = lambda ap: ap.rearrange("p (u h d) -> p u h d", u=2, d=64)
                for u in range(2):
                    h = tt(QR[:, m, 0:512].rearrange("p (h u d) -> p u h d", u=2, d=64)[:, u, :, :],
                           q4(AQ[:, m, 0:512])[:, u, :, :], q4(T2[:, 0:512])[:, u, :, :], ADD, q=g)
                hqr = tt(QR[:, m, 512:640], AQ[:, m, 512:640], T2[:, 512:640], ADD, q=g)
            GA = MOD[:, 0:2048].rearrange("p (a b) -> p a b", a=8)
            GM = MN[:, :, :]
            held = {}

            def gate_step(which, half, pair):
                def go():
                    dst, c0, bias = ((GM, 2832, "bgm"), (GA, 3856, "bga"))[which]
                    if pair == 0:
                        held["w"] = weights(win[:, c0 + half * 512:c0 + half * 512 + 512], 8, 512)

                    def ev(c, ps, h):
                        f = 4 * half + c
                        held[which] = act(dst[:, f, :], ps, ACT.Identity, [h], bias=vec(bias, 8 * layer + f))
                        return [held[which]]
                    gemm_f(None, 8, HT, ev, n=512, cols=[256 * pair, 256 * pair + 128], keep=held["w"])
                    if pair == 1:
                        done_with(held["w"][0])
                return go

            def branch_step(which, half, pair):
                def go():
                    cs = slice(half * 512, half * 512 + 512)
                    if which == 0 and pair == 0:
                        srcm = t["w_branch_m_2"][layer, :, cs].rearrange("(k p) n -> p k n", p=128)
                        srca = t["w_branch_a_2"][layer, :, cs].rearrange("(u k p) n -> u p k n", u=2, p=64)
                        part = lambda place, j: place[:, 2048 * j:2048 * j + 2048].rearrange("p (k n) -> p k n", k=4)
                        i3, place, landed = fill(lambda place: [(part(place, 0), srcm), (part(place, 1)[0:64], srca[0]),
                                                                (part(place, 1)[64:128], srca[1])])
                        held["b", half] = i3, (part(place, 0), part(place, 1)), landed
                    i3, wts, landed = held["b", half]
                    y = (YM, YA)[which]
                    i, ps, busy = PB.get()
                    for j in range(2):
                        c = 2 * pair + j
                        for k in range(4):
                            h = mm(ps[:, j * 256:j * 256 + 256], wts[which][:, k, c * 128:c * 128 + 128], y[:, k, :],
                                   k == 0, k == 3, busy + [landed, held["y", which]])
                    f = 4 * half + 2 * pair
                    p3 = ps[:, :].rearrange("p (a b) -> p a b", a=2)
                    d = (GM, GA)[which][:, f:f + 2, :]
                    e = tt(d, p3, d, MUL, [h, held["sig", which]])
                    PB.put(i, [e])
                    if which == 1:
                        d = GM[:, f:f + 2, :]
                        e = tt(d, d, GA[:, f:f + 2, :], ADD)
                        if pair == 1:
                            done_with(i3)
                    held["e"] = e
                return go
            probe(f"mqk{layer}", MQK, edge())
            probe(f"aq{layer}", AQ, edge())
            n2 = ar.n
            E = Ring([[ar.take(2, 256), ar.take(2, 256)] for _ in range(3)])
            S3 = Ring([ar.take(2, 128)])
            st = [{} for _ in range(4)]

            def weigh(hd):
                o = st[hd]
                o["r"], dws, rb = E.get()
                o["nm"], o["dens"], o["em"] = nm, dens, em = sm(2, 2), sm(2, 2), sm(2, 2)
                o["dw"] = dws
                o["top"] = []
                for d in range(2):
                    dw = dws[d]
                    i2, ps, busy2 = PB.get()
                    for k in range(2):
                        h = mm(ps[:, k * 128:k * 128 + 128], bc(cb[:, k, 4 * d + hd:4 * d + hd + 1], 128), IDENT,
                               True, True, busy2 + [hcb])
                    mask = C("mbwd" if d else "mfwd", 512).rearrange("p (a b) -> p a b", a=2)
                    h = tt(dw, mask, ps[:, 0:256].unsqueeze(1).broadcast_to([128, 2, 256]), ADD, [h] + rb)
                    PB.put(i2, [h])
                    red(nm[:, d, :], dw, MAX)
                    o["top"].append(ts(nm[:, d, :], nm[:, d, :], 0.0, -1.0, MAX, MUL))
                o["hem"] = tt(em, nm, nb.rearrange("p a (b c) -> p b c a", b=2)[:, :, hd, :], ADD)

            def exps(hd):
                o = st[hd]
                for d in range(2):
                    for m in range(2):
                        act(o["dw"][d][:, m, :], o["dw"][d][:, m, :], ACT.Exp, [o["top"][d]],
                            bias=o["nm"][:, d, m:m + 1])
                o["e"] = act(o["em"], o["em"], ACT.Exp, [o["hem"]])

            def scores(hd):
                o = st[hd]
                o["i"], o["pq"], busy = PB.get()
                for m in range(2):
                    o["hq"] = mm(o["pq"][:, m * 256:m * 256 + 256], MQK[:, hd, m * 128:m * 128 + 128],
                                 MQK[:, 4 + hd, :], True, True, busy)

            def norm(hd):
                o = st[hd]
                pq, dens, em = o["pq"], o["dens"], o["em"]
                for d in range(2):
                    for m in range(2):
                        h = v(lambda e, dw=o["dw"][d], m=m, d=d, pq=pq, dens=dens: e.tensor_tensor_reduce(
                            dw[:, m, :], pq[:, m * 256:m * 256 + 256], dw[:, m, :], 128.0 ** -0.5, 0.0, MUL, ADD,
                            dens[:, d, m:m + 1]), [o["e"], o["hq"]])
                PB.put(o["i"], [h])
                stt(em, dens, -1.0, em, MUL, MAX)
                tt(dens, dens, em, MAX)
                v(lambda e, dens=dens: e.reciprocal(dens, dens))
                dwf, dwb = o["dw"]
                for m in range(2):
                    ts(dwf[:, m, :], dwf[:, m, :], dens[:, 0, m:m + 1], None, MUL)
                    o["h"] = stt(dwf[:, m, :], dwb[:, m, :], dens[:, 1, m:m + 1], dwf[:, m, :], MUL, ADD)

            def turned(hd):
                o = st[hd]
                dwf, dwb = o["dw"]
                _, o["t"] = turn(dwf, dwb, [o["h"]])

            def out_(hd):
                o = st[hd]
                dwf, dwb = o["dw"]
                o["i"], ps, busy = PA.get()
                for m in range(2):
                    for k in range(2):
                        h = mm(ps[:, m * 128:m * 128 + 128], dwb[:, k, m * 128:m * 128 + 128],
                               MV[:, k, hd * 128:hd * 128 + 128], k == 0, k == 1, busy + [o["t"]])
                o["ps"] = p3 = ps[:, 0:256].rearrange("p (a b) -> p a b", a=2)
                o["rs"] = sm(2)
                for m in range(2):
                    o["sq"] = act(dwf[:, m, 0:128], p3[:, m, :], ACT.Square, [h], accum_out=o["rs"][:, m:m + 1])

            def scaled(hd):
                o = st[hd]
                rs = o["rs"]
                h = ts(rs, rs, 1.0 / 128, 1e-6, MUL, ADD, w=[o["sq"]])
                power(rs, [h])
                o["r3"], o["s3"], rb = S3.get()
                for m in range(2):
                    h = ts(o["s3"][:, m, :], o["ps"][:, m, :], rs[:, m:m + 1], None, MUL, w=rb)
                PA.put(o["i"], [h])
                E.put(o["r"], [h])
                o["h"] = h

            def gated(hd):
                o = st[hd]
                i, ps, busy = PA.get()
                for m in range(2):
                    h = tp(ps[:, m * 128:m * 128 + 128], o["s3"][:, m, :], busy + [o["h"]])
                S3.put(o["r3"], [h])
                h = stt(YM[:, hd, :], ps[:, 0:256], vec("mnorm", 4 * layer + hd), YM[:, hd, :], MUL, MUL, [h])
                held["y", 0] = h
                PA.put(i, [h])

            pipeline(4, [(3, scaled), (2, turned), (0, weigh), (1, scores), None, (0, exps), (1, norm), (3, gated), (2, out_)],
                     [gate_step(0, 0, 0), gate_step(0, 0, 1), gate_step(0, 1, 0), gate_step(0, 1, 1),
                      gate_step(1, 0, 0), gate_step(1, 0, 1)])
            probe(f"ym{layer}", YM, edge())
            held["sig", 0] = act(GM, GM, ACT.Sigmoid, [held[0]])
            barrier()
            ar.n = n2
            QT = AR[:, n1:n1 + 1280].rearrange("p (a b) -> p a b", a=5)
            hq = []
            for pr in (4, 0, 1, 2, 3):
                i, ps, busy = PB.get()
                for m in range(2):
                    h = tp(ps[:, m * 128:m * 128 + 128], QR[:, m, pr * 128:pr * 128 + 128], busy + [hqr])
                e = act(QT[:, pr, :], ps[:, 0:256], ACT.Copy, [h])
                PB.put(i, [e])
                hq.append(e)
            SR, TR = Ring([ar.take(2, 256) for _ in range(3)]), Ring([ar.take(2, 256) for _ in range(2)])
            st = [{} for _ in range(8)]

            def scores(hd):
                pr, o = hd % 4, st[hd]
                p0 = slice(64 * (hd // 4), 64 * (hd // 4) + 64)
                o["r"], s, rb = SR.get()
                o["i"], ps, busy = PB.get()
                for m in range(2):
                    h = mm(ps[:, m * 256:m * 256 + 256], QT[p0, pr, m * 128:m * 128 + 128], QT[p0, 4, :], True, True,
                           busy + hq)
                o["o"] = softmax_top(ps, [h] + rb, 64.0 ** -0.5, None, s)

            def exps(hd):
                o = st[hd]
                o["e"] = softmax_exp(o["o"])
                PB.put(o["i"], [o["e"]])

            def norm(hd):
                o = st[hd]
                o["h"] = softmax_end(o["o"], o["e"], None)

            def turned(hd):
                o = st[hd]
                o["r2"], o["tr"], rb = TR.get()
                h, o["t"] = turn(o["o"][6], o["tr"], [o["h"]] + rb)
                SR.put(o["r"], [h])

            def out_(hd):
                pr, u, o = hd % 4, hd // 4, st[hd]
                p0 = slice(64 * u, 64 * u + 64)
                i, ps, busy = PA.get()
                for k in range(2):
                    h = mm(ps[p0, 0:256], AQ[:, k, 640 + 64 * u:704 + 64 * u], o["tr"][:, k, :], k == 0, k == 1,
                           busy + [o["t"]])
                TR.put(o["r2"], [h])
                held["y", 1] = cp(YA[p0, pr, :], ps[p0, 0:256], [h])
                PA.put(i, [held["y", 1]])

            pipeline(8, [(2, turned), (0, scores), None, (0, exps), (1, norm), (2, out_)],
                     [gate_step(1, 1, 0), gate_step(1, 1, 1)]
                     + [branch_step(0, half, pair) for half in range(2) for pair in range(2)])
            probe(f"ya{layer}", YA, edge())
            held["sig", 1] = act(GA, GA, ACT.Sigmoid, [held[1]])
            for half in range(2):
                for pair in range(2):
                    branch_step(1, half, pair)()
            down([(t["w_out_2"][layer][512 * c:512 * c + 512, :], 4 * c, 4) for c in range(2)], GM, gated_add(MOD, 0),
                 [held["e"]], (), lambda m: mod_part(MOD, 1, m))

        def moe(layer, MOD):
            hT = norm_features(HT, None)
            barrier()
            if layer == 0:
                hmod = [load_modulation(1, MOD, (0, 5120))] + load_gains(1, (MF[:, 0:1024], MF[:, 1024:2048]))
            else:
                hmod = [load("fn", MF[:, 0:1024], t["final_norm_g_2"].broadcast_to([128, 1024]), edge())]
            o = 56 + 52 * layer
            LGT = ar.take(2, 40)
            CB = ar.take(2, 32)

            def ev(m, ps, h):
                h1 = tt(LGT[:, m, 0:4], ps[:, 0:4], RB[:, rat["brg"] + 4 * layer:rat["brg"] + 4 * layer + 4], ADD, [h])
                h1 = tt(LGT[:, m, 8:40], ps[:, 4:36], RB[:, rat["bre"] + 32 * layer:rat["bre"] + 32 * layer + 32], ADD)
                return [h1]
            gemm_t(SW[:, :, o:o + 36], None, 8, HT, 36, 0, ev, hT)
            probe(f"lgt{layer}", LGT, edge())
            v(lambda e: e.memset(LGT[:, :, 4:8], NEG))
            IO = C("iota", 8)
            mx, s, pg, top, ix, ixf, gm = sm(2), sm(2), sm(2, 8), sm(2, 8), sm(2, 8), sm(2, 8), sm(2, 8)
            el, w1, one, sel = sm(2, 8), sm(2, 2), sm(2, 8), sm(2, 32)
            ixu = ix.bitcast(U32)
            over = lambda x, n: x.unsqueeze(2).broadcast_to([128, 2, n])
            two = lambda x: x.unsqueeze(1).broadcast_to([128, 2, 8])

            def softmax8(dst, src):
                red(mx, src, MAX)
                h = ts(mx, mx, -1.0, None, MUL)
                for m in range(2):
                    h2 = act(dst[:, m, :], src[:, m, :], ACT.Exp, [h], bias=mx[:, m:m + 1], accum_out=s[:, m:m + 1])
                v(lambda e: e.reciprocal(s, s), [h2])
                return tt(dst, dst, over(s, 8), MUL)

            def best(src):
                for m in range(2):
                    v(lambda e, m=m: e.max(top[:, m, :], src[:, m, :]))
                    v(lambda e, m=m: e.max_index(ixu[:, m, :], top[:, m, :], src[:, m, :]))
                return cp(ixf, ixu)

            softmax8(pg, LGT[:, :, 0:8])
            v(lambda e: e.memset(pg[:, :, 4:8], -1.0))
            best(pg)
            ptop = sm(2)
            cp(ptop, top[:, :, 0])
            tt(gm, two(IO), ixf[:, :, 0:1].broadcast_to([128, 2, 8]), ALU.is_equal)
            s4 = sel.rearrange("p m (a b) -> p m a b", a=4)
            for m in range(2):
                tt(s4[:, m], LGT[:, m, 8:40].rearrange("p (a b) -> p a b", a=4),
                   gm[:, m, 0:4].unsqueeze(2).broadcast_to([128, 4, 8]), MUL)
            tt(sel[:, :, 0:16], sel[:, :, 0:16], sel[:, :, 16:32], ADD)
            tt(el, sel[:, :, 0:8], sel[:, :, 8:16], ADD)
            softmax8(el, el)
            best(el)
            tt(s, top[:, :, 0], top[:, :, 1], ADD)
            v(lambda e: e.reciprocal(s, s))
            tt(s, s, ptop, MUL)
            tt(w1, top[:, :, 0:2], over(s, 2), MUL)
            for j, dst in ((0, one), (1, el)):
                tt(dst, two(IO), ixf[:, :, j:j + 1].broadcast_to([128, 2, 8]), ALU.is_equal)
                tt(dst, dst, w1[:, :, j:j + 1].broadcast_to([128, 2, 8]), MUL)
            tt(one, one, el, ADD)
            for m in range(2):
                hcb = tt(CB[:, m, :].rearrange("p (a b) -> p a b", a=4), one[:, m, :].unsqueeze(1)
                         .broadcast_to([128, 4, 8]), gm[:, m, 0:4].unsqueeze(2).broadcast_to([128, 4, 8]), MUL)
            probe(f"cb{layer}", CB, [hcb])
            MK, RK = ar.take(2, 32), ar.take(2, 32)
            FL = ar.take(2)
            flag = FL[0:1, 1:2].bitcast(I32)
            h = ts(MK, CB, 0.0, None, ALU.is_gt, w=[hcb])
            i, ps, busy = PB.get()
            for m in range(2):
                for k in range(2):
                    hh = mm(ps[:, m * 32:m * 32 + 32], C("up", 512)[:, k * 256 + m * 128:k * 256 + m * 128 + 128],
                            MK[:, k, :], k == 0, k == 1, busy + [h])
            for k in range(2):
                hh = mm(ps[:, 64:96], ONES, MK[:, k, :], k == 0, k == 1)
            tt(RK, ps[:, 0:64].rearrange("p (a b) -> p a b", a=2), MK, MUL, [hh])
            h = red(FL[:, 0:1], ps[:, 64:96], MAX)
            PB.put(i, [h])
            hrk = cp(flag, FL[0:1, 0:1])
            barrier()
            n0 = ar.n
            got = [PA.get() for _ in range(4)]
            busyA = [b for _, _, bs in got for b in bs]
            acc = [bank for _, bank, _ in got]
            SL = C("slots", CAP)
            Q.part(flag, LIMIT, [hrk])
            stream["said"] = []

            SEL = Ring([(ar.take(2, 128), ar.take(2, 128)) for _ in range(2)])
            HG = Ring([ar.take(8, 128) for _ in range(2)])
            SWT = Ring([ar.take(256) for _ in range(2)])
            AC = Ring([ar.take(512)])
            AT = Ring([ar.take(4, 128) for _ in range(2)])
            YS = Ring([ar.take(1024) for _ in range(2)])

            def gather(pair):
                r, (sel, sw), rb = SEL.get()
                pick = lambda x: x[:, :, 2 * pair:2 * pair + 2].unsqueeze(3).broadcast_to([128, 2, 2, CAP])
                s4, w4 = (x.rearrange("p m (e s) -> p m e s", e=2) for x in (sel, sw))
                h = None
                for m in range(2):
                    pm = lambda x: x[:, m, 2 * pair:2 * pair + 2].unsqueeze(2).broadcast_to([128, 2, CAP])
                    h = tt(s4[:, m], SL.unsqueeze(1).broadcast_to([128, 2, CAP]), pm(RK), ALU.is_equal, rb)
                hsel = h
                for m in range(2):
                    pm = lambda x: x[:, m, 2 * pair:2 * pair + 2].unsqueeze(2).broadcast_to([128, 2, CAP])
                    hw = tt(w4[:, m], s4[:, m], pm(CB), MUL)
                r2, hg, rb2 = HG.get()
                he = []
                for half in range(2):
                    i, ps, busy = PB.get()
                    for j in range(4):
                        for m in range(2):
                            k = half * 4 + j
                            h = mm(ps[:, j * 128:j * 128 + 128], XN[:, m, k * 128:k * 128 + 128], sel[:, m, :],
                                   m == 0, m == 1, busy + [hsel])
                    o = hg[:, half * 4:half * 4 + 4, :]
                    src = ps[:, :].rearrange("p (a b) -> p a b", a=4)
                    e = cp(o, src, [h] + rb2) if half else act(o, src, ACT.Copy, [h] + rb2)
                    PB.put(i, [e])
                    he.append(e)
                r3, swt, rb3 = SWT.get()
                i, ps, busy = PB.get()
                for m in range(2):
                    h = tp(ps[:, m * 128:m * 128 + 128], sw[:, m, :], busy + [hw])
                e = act(swt, ps[:, 0:256], ACT.Copy, [h] + rb3)
                PB.put(i, [e])
                SEL.put(r, [h])
                return (r2, hg, he), (r3, swt, e)

            def up(pair, g_):
                r2, hg, he = g_
                wg = [weights(t["w_gate_2"][layer, 2 * pair + e], 8, 512) for e in range(2)]
                wu = [weights(t["w_up_2"][layer, 2 * pair + e], 8, 512) for e in range(2)]
                wd = [weights(t["w_down_2"][layer, 2 * pair + e], 4, 1024) for e in range(2)]
                r, ac, rb = AC.get()
                banks_ = []
                for wx in (wg, wu):
                    i, ps, busy = PB.get()
                    for k in range(8):
                        for e in range(2):
                            h = mm(ps[64 * e:64 * e + 64, :], hg[:, k, 64 * e:64 * e + 64], wx[e][1][:, k, :],
                                   k == 0, k == 7, busy + he + [wx[e][2]])
                    done_with(wx[0][0])
                    done_with(wx[1][0])
                    banks_.append((i, ps, h))
                HG.put(r2, [h])
                i, ps, h = banks_[0]
                e1 = act(ac, ps[:, :], ACT.Silu, [h] + rb)
                PB.put(i, [e1])
                i, ps, h = banks_[1]
                e2 = tt(ac, ps[:, :], ac, MUL, [h, e1])
                PB.put(i, [e2])
                return wd, r, ac, e2

            def lower(u_):
                wd, r, ac, e2 = u_
                i, ps, busy = PB.get()
                for f in range(4):
                    h = tp(ps[:, f * 128:f * 128 + 128], ac[:, f * 128:f * 128 + 128], busy + [e2])
                AC.put(r, [h])
                r, at, rb = AT.get()
                hat = act(at, ps[:, :].rearrange("p (a b) -> p a b", a=4), ACT.Copy, [h] + rb)
                PB.put(i, [hat])
                y = [PB.get() for _ in range(2)]
                for f in range(4):
                    for c in range(2):
                        for e in range(2):
                            h = mm(y[c][1][64 * e:64 * e + 64, :], at[:, f, 64 * e:64 * e + 64],
                                   wd[e][1][:, f, c * 512:c * 512 + 512], f == 0, f == 3,
                                   y[0][2] + y[1][2] + [hat, wd[e][2]])
                done_with(wd[0][0])
                done_with(wd[1][0])
                AT.put(r, [h])
                r, ys, rb = YS.get()
                e1 = act(ys[:, 0:512], y[0][1][:, :], ACT.Copy, [h] + rb)
                e2 = cp(ys[:, 512:1024], y[1][1][:, :], [h] + rb)
                PB.put(y[0][0], [e1])
                PB.put(y[1][0], [e2])
                return r, ys, [e1, e2]

            def scatter(pair, s_, y_):
                r3, swt, e = s_
                r, ys, he = y_
                for m in range(2):
                    for c in range(2):
                        h = mm(acc[2 * m + c][:, :], swt[:, m * 128:m * 128 + 128], ys[:, c * 512:c * 512 + 512],
                               pair == 0, pair == 15, busyA + he + [e])
                SWT.put(r3, [h])
                YS.put(r, [h])

            g_, s_ = gather(0)
            y_ = None
            for pair in range(16):
                u_ = up(pair, g_)
                if y_ is not None:
                    scatter(pair - 1, s_old, y_)
                s_old = s_
                if pair < 15:
                    g_, s_ = gather(pair + 1)
                y_ = lower(u_)
            scatter(15, s_old, y_)

            stream["replay"], stream["said"] = stream["said"], None
            Q.way()
            ar.n = n0
            for ring in (PA, PB):
                ring.busy = [[] for _ in ring.busy]
            GA = Ring([ar.take(4, 256) for _ in range(2)])
            CR = Ring([ar.take(256) for _ in range(2)])
            for pair in range(16):
                wg = [weights(t["w_gate_2"][layer, 2 * pair + e], 8, 512) for e in range(2)]
                wu = [weights(t["w_up_2"][layer, 2 * pair + e], 8, 512) for e in range(2)]
                wd = [weights(t["w_down_2"][layer, 2 * pair + e], 4, 1024) for e in range(2)]
                outs = []
                for e_ in range(2):
                    ex = 2 * pair + e_
                    r, ga, rb = GA.get()
                    r2, cr, rb2 = CR.get()
                    i, ps, busy = PB.get()
                    for k in range(2):
                        h = mm(ps[:, 0:256], bc(CB[:, k, ex:ex + 1], 128), C("id2", 512)[:, k * 256:k * 256 + 256],
                               k == 0, k == 1, busy)
                    hc_ = act(cr, ps[:, 0:256], ACT.Copy, [h] + rb2)
                    PB.put(i, [hc_])
                    for f in range(4):
                        i, ps, busy = PB.get()
                        for j, (sl, wt, landed) in enumerate((wg[e_], wu[e_])):
                            for k in range(8):
                                h = mm(ps[:, j * 256:j * 256 + 256], wt[:, k, f * 128:f * 128 + 128], HT[:, k, :],
                                       k == 0, k == 7, busy + [landed])
                        e = act(ga[:, f, :], ps[:, 0:256], ACT.Silu, [h] + rb)
                        e = tt(ga[:, f, :], ps[:, 256:512], ga[:, f, :], MUL, [h, e])
                        PB.put(i, [e])
                        e = tt(ga[:, f, :], ga[:, f, :], cr, MUL, [hc_])
                    CR.put(r2, [e])
                    outs.append((r, ga, e))
                for x in (wg, wu):
                    done_with(x[0][0])
                    done_with(x[1][0])
                for e_ in range(2):
                    r, ga, e = outs[e_]
                    for f in range(4):
                        for m in range(2):
                            for c in range(2):
                                h = mm(acc[2 * m + c][:, :], ga[:, f, m * 128:m * 128 + 128],
                                       wd[e_][1][:, f, c * 512:c * 512 + 512], pair == 0 and e_ == 0 and f == 0,
                                       pair == 15 and e_ == 1 and f == 3, [e, wd[e_][2]])
                    GA.put(r, [h])
                done_with(wd[0][0])
                done_with(wd[1][0])
            stream["replay"] = None
            joined = Q.meet()
            for ring in (PA, PB):
                ring.busy = [list(joined) for _ in ring.busy]
            for k in ("pe", "dve", "act", "pool"):
                Q.pending[k] = list(joined)
            ev = gated_add(MOD, 1)
            if layer == 0:
                modulation(MOD, hmod, (MF[:, 0:1024], MF[:, 1024:2048]))
            for m in range(2):
                for c in range(2):
                    PA.put(got[2 * m + c][0], ev(m, c, acc[2 * m + c], joined[0]))
                if layer == 0:
                    mod_part(MOD, 0, m)
                else:
                    h = last_part(MF[:, 0:1024], m, hmod)
                    load("out", out[0, 128 * m:128 * m + 128, :], X[:, m, :], [h], k="sp")
            if layer == 0:
                load_modulation(1, MOD, (5120, 6144))
                for k in ("dve",):
                    Q.pending.setdefault(k, []).append(loaded("mod"))

        ar.n = 0
        CAT = ar.take(12, 256)
        memory = gdn(CAT)
        probe("mix0", CAT, edge())
        ar.n = 12 * 256
        barrier()
        memory_attention(CAT, memory)
        probe("cat0", CAT, edge())
        project_out(t["w_out"][0], 0, CAT, 12)
        probe("xa0", X[:, :, :], edge())
        conv_glu(0)
        probe("xb0", X[:, :, :], edge())
        memory = nsa(CAT)
        ar.n = 12 * 256
        barrier()
        memory_attention(CAT, memory)
        probe("cat1", CAT, edge())
        project_out(t["w_out"][1], 1, CAT, 12)
        conv_glu(1)
        for layer in range(2):
            ar.n = 0
            MOD = ar.take(6144)
            mixers(layer, MOD)
            probe(f"xm{layer}", X[:, :, :], edge())
            ar.n = 6144
            moe(layer, MOD)
            probe(f"xe{layer}", X[:, :, :], edge())
        finals = [loaded("out")] + ([loaded("dbg")] if dbg is not None else [])

        Q.count()
        block = ctx.enter_context(nc.Block())

        @block.sync
        def _(eng):
            Q.write("sp", eng)
            for x in finals:
                eng.wait_ge(x.sem, x.value)

        @block.tensor
        def _(eng):
            Q.write("pe", eng)

        @block.vector
        def _(eng):
            Q.write("dve", eng)

        @block.scalar
        def _(eng):
            Q.write("act", eng)

        @block.gpsimd
        def _(eng):
            Q.write("pool", eng)


_BIG = ["x", "mem", "mem_w_kv", "w_out", "gdn_w_in", "nsa_w_in", "nsa_cmp_w1_k", "nsa_cmp_w2_k", "nsa_cmp_w1_v",
        "nsa_cmp_w2_v", "ffn_w_up", "ffn_w_down", "w_ada_2", "b_ada_2", "norm1_g_2", "norm2_g_2", "w_in_2", "b_in_2",
        "w_branch_m_2", "w_branch_a_2", "w_out_2", "w_router_group_2", "w_router_expert_2", "w_gate_2", "w_up_2",
        "w_down_2"]


def lay_out(inputs):
    a = {k: np.ascontiguousarray(inputs[k]) for k in _BIG}
    i = {k: np.asarray(v) for k, v in inputs.items()}
    cols = lambda z: np.asarray(z).reshape(-1, 128)
    b = i["b_in_2"]
    parts = [i["norm_mix_w"], i["norm_ffn_w"], i["mem_norm_w"], i["gdn_conv_w"], i["gdn_norm_w"], i["ffn_conv_w"],
             i["ffn_conv_b"], i["nsa_cmp_pos_k"], i["nsa_cmp_pos_v"], b[:, 0:1024], b[:, 1536:2048], b[:, 2832:3856],
             b[:, 3856:4880], i["conv_w_2"], i["conv_b_2"], i["mlstm_norm_g_2"], i["c_2"]]
    a["vecs"] = np.ascontiguousarray(np.concatenate([cols(z) for z in parts], 0).T)
    rows = [i["gdn_a_log"], i["gdn_dt_bias"], i["b_router_group_2"], i["b_router_expert_2"], i["q_norm_g_2"],
            i["k_norm_g_2"], b[:, 2048:2064]]
    a["rows"] = np.ascontiguousarray(np.concatenate([np.asarray(z).reshape(-1) for z in rows])[None])
    table, _, _, hot = constants()
    a["cst"] = table
    a["hot"] = hot
    a["tab"] = np.ascontiguousarray(np.concatenate([i["rel_bias"], np.full((1, 8), NEG, np.float32)], 0))
    a["final_norm_w"] = i["final_norm_w"].reshape(1, 1024)
    a["final_norm_g_2"] = i["final_norm_g_2"].reshape(1, 1024)
    return a


def kernel(**inputs):
    import concourse.bacc as _bacc
    from concourse.bass_utils import run_bass_kernel_spmd as _run

    nc = _bacc.Bacc("TRN2", target_bir_lowering=False, num_devices=1)
    arrays, t = {}, {}
    for name, a in lay_out(inputs).items():
        arrays[f"in_{name}"] = a
        t[name] = nc.dram_tensor(f"in_{name}", a.shape, F32, kind="ExternalInput").ap()
    out = nc.dram_tensor("out_x", (1, 256, 1024), F32, kind="ExternalOutput").ap()
    build(nc, t, out)
    r = _run(nc, [arrays], core_ids=[0])
    return r.results[0]["out_x"]
```
